# Optimizing a Trainium2 kernel written in Bass

```python
import jax, jax.numpy as jnp
from jax import lax
import numpy as np

D_MODEL = 1024
BATCH = 1
SEQ = 512
DEPTH = 2

CHUNK = 64
LN_EPS = 1e-5
GMLP_HEADS = 4
GMLP_WIDTH = D_MODEL
GMLP_HEAD_DIM = GMLP_WIDTH // GMLP_HEADS
GMLP_BLOCK = 128
POOL_WINDOWS = (2, 4, 8, 16)
POOL_GROUPS = len(POOL_WINDOWS)
POOL_WIDTH = D_MODEL
POOL_GROUP_DIM = POOL_WIDTH // POOL_GROUPS
EVEN_IN = 3 * GMLP_WIDTH + 2 * POOL_WIDTH
EVEN_MIX = GMLP_WIDTH + POOL_WIDTH
MLA_HEADS = 16
MLA_NOPE = 128
MLA_ROPE = 64
MLA_V = 128
MLA_Q_RANK = 256
MLA_KV_RANK = 128
MLA_WIDTH = MLA_HEADS * MLA_V
ODD_IN = MLA_Q_RANK + MLA_KV_RANK + MLA_ROPE + MLA_WIDTH
ROPE_THETA = 10000.0
Q_BLOCK = 128
ATTN_SCALE = (MLA_NOPE + MLA_ROPE) ** -0.5
DEEPNORM_ALPHA = (2.0 * DEPTH) ** 0.25
DEEPNORM_BETA = (8.0 * DEPTH) ** -0.25
N_EVEN = (DEPTH + 1) // 2
N_ODD = DEPTH // 2


def layer_norm(x, g, b):
    xf = x.astype(jnp.float32)
    mu = jnp.mean(xf, axis=-1, keepdims=True)
    var = jnp.mean(jnp.square(xf - mu), axis=-1, keepdims=True)
    return ((xf - mu) * lax.rsqrt(var + LN_EPS) * g + b).astype(x.dtype)

def rms_norm(x, g):
    xf = x.astype(jnp.float32)
    ms = jnp.mean(jnp.square(xf), axis=-1, keepdims=True)
    return (xf * lax.rsqrt(ms + LN_EPS) * g).astype(x.dtype)

def rope_cos_sin(positions):
    inv = 1.0 / (ROPE_THETA ** (jnp.arange(0, MLA_ROPE, 2, dtype=jnp.float32) / MLA_ROPE))
    ang = positions.astype(jnp.float32)[..., None] * inv
    return jnp.cos(ang), jnp.sin(ang)

def apply_rope(x, cos, sin):
    half = x.shape[-1] // 2
    x1 = x[..., :half].astype(jnp.float32)
    x2 = x[..., half:].astype(jnp.float32)
    return jnp.concatenate([x1 * cos - x2 * sin, x2 * cos + x1 * sin], axis=-1).astype(x.dtype)

def gmlp_spatial_unit(u, v, norm_g, norm_b, ws, bs):
    B, S, _ = u.shape
    nb = S // GMLP_BLOCK
    v = layer_norm(v.reshape(B, S, GMLP_HEADS, GMLP_HEAD_DIM), norm_g, norm_b)
    v = v.reshape(B, nb, GMLP_BLOCK, GMLP_HEADS, GMLP_HEAD_DIM)
    pos_chunk = jnp.arange(GMLP_BLOCK) // CHUNK
    mask = pos_chunk[None, :] <= pos_chunk[:, None]
    w = jnp.where(mask[None], ws, jnp.zeros_like(ws))
    sv = jnp.einsum('hts,bnshd->bnthd', w, v) + bs.T[:, :, None]
    return u * sv.reshape(B, S, GMLP_WIDTH)

def multiscale_pool(xb, pool_w, pool_b, pool_scale):
    B, S, _ = xb.shape
    xg = xb.reshape(B, S, POOL_GROUPS, POOL_GROUP_DIM).astype(jnp.float32)
    cs = jnp.cumsum(xg, axis=1)
    t = jnp.arange(S)
    means = []
    for g, win in enumerate(POOL_WINDOWS):
        csg = cs[:, :, g]
        lagged = jnp.concatenate([jnp.zeros((B, win, POOL_GROUP_DIM), csg.dtype), csg[:, :S - win]], axis=1)
        cnt = jnp.minimum(t + 1, win).astype(jnp.float32)
        means.append((csg - lagged) / cnt[None, :, None])
    pooled = jnp.stack(means, axis=2) - xg
    y = jnp.einsum('bsgd,gde->bsge', pooled.astype(xb.dtype), pool_w).reshape(B, S, POOL_WIDTH)
    return (y + pool_b) * pool_scale

def even_mixer(h, w_in, gmlp_norm_g, gmlp_norm_b, gmlp_ws, gmlp_bs, pool_w, pool_b, pool_scale, w_out):
    proj = h @ w_in
    u, v, z_a, x_b, z_b = jnp.split(proj, [GMLP_WIDTH, 2 * GMLP_WIDTH, 3 * GMLP_WIDTH,
                                           3 * GMLP_WIDTH + POOL_WIDTH], axis=-1)
    a = gmlp_spatial_unit(u, v, gmlp_norm_g, gmlp_norm_b, gmlp_ws, gmlp_bs) * jax.nn.silu(z_a)
    b = multiscale_pool(x_b, pool_w, pool_b, pool_scale) * jax.nn.silu(z_b)
    return jnp.concatenate([a, b], axis=-1) @ w_out

def mla_mixer(h, positions, w_in, q_norm_g, kv_norm_g, w_uq, w_uk, w_uv, w_out):
    B, S, _ = h.shape
    proj = h @ w_in
    q_c, kv_c, k_r, z = jnp.split(proj, [MLA_Q_RANK, MLA_Q_RANK + MLA_KV_RANK,
                                         MLA_Q_RANK + MLA_KV_RANK + MLA_ROPE], axis=-1)
    q_c = rms_norm(q_c, q_norm_g)
    kv_c = rms_norm(kv_c, kv_norm_g)
    q = jnp.einsum('bsr,rhd->bshd', q_c, w_uq)
    q_nope, q_rope = q[..., :MLA_NOPE], q[..., MLA_NOPE:]
    cos, sin = rope_cos_sin(positions)
    q_rope = apply_rope(q_rope, cos[:, :, None, :], sin[:, :, None, :])
    k_rope = apply_rope(k_r, cos, sin)
    q_lat = jnp.einsum('bshd,rhd->bshr', q_nope, w_uk)
    nb = S // Q_BLOCK
    q_lat_b = q_lat.reshape(B, nb, Q_BLOCK, MLA_HEADS, MLA_KV_RANK).transpose(1, 0, 2, 3, 4)
    q_rope_b = q_rope.reshape(B, nb, Q_BLOCK, MLA_HEADS, MLA_ROPE).transpose(1, 0, 2, 3, 4)
    key_chunk = jnp.arange(S) // CHUNK

    def attend_block(args):
        ql, qr, i = args
        s = jnp.einsum('bqhr,bkr->bhqk', ql, kv_c) + jnp.einsum('bqhd,bkd->bhqk', qr, k_rope)
        s = s.astype(jnp.float32) * ATTN_SCALE
        q_chunk = (i * Q_BLOCK + jnp.arange(Q_BLOCK)) // CHUNK
        mask = key_chunk[None, :] <= q_chunk[:, None]
        p = jax.nn.softmax(jnp.where(mask, s, -jnp.inf), axis=-1).astype(kv_c.dtype)
        return jnp.einsum('bhqk,bkr->bqhr', p, kv_c)

    o_lat = lax.map(attend_block, (q_lat_b, q_rope_b, jnp.arange(nb)))
    o_lat = o_lat.transpose(1, 0, 2, 3, 4).reshape(B, S, MLA_HEADS, MLA_KV_RANK)
    o = jnp.einsum('bshr,rhd->bshd', o_lat, w_uv).reshape(B, S, MLA_WIDTH)
    return (o * jax.nn.silu(z)) @ w_out

def first_inputs(seed: int = 0) -> dict:
    key = jax.random.key(seed)
    ks = jax.random.split(key, 24)
    f32 = jnp.float32

    def nrm(k, shape, s):
        return s * jax.random.normal(k, shape, f32)

    x = nrm(ks[0], (BATCH, SEQ, D_MODEL), 1.0)
    c = nrm(ks[1], (BATCH, D_MODEL), 1.0)
    offs = jax.random.randint(ks[2], (BATCH, 1), 0, 4096, dtype=jnp.int32)
    positions = offs + jnp.arange(SEQ, dtype=jnp.int32)[None, :]
    ada_w = nrm(ks[3], (DEPTH, D_MODEL, 3 * D_MODEL), 0.1 * D_MODEL ** -0.5)
    ada_b = nrm(ks[4], (DEPTH, 3 * D_MODEL), 0.01)
    ln_g = 1.0 + nrm(ks[5], (DEPTH, D_MODEL), 0.02)
    ln_b = nrm(ks[6], (DEPTH, D_MODEL), 0.02)
    e_w_in = nrm(ks[7], (N_EVEN, D_MODEL, EVEN_IN), D_MODEL ** -0.5)
    gmlp_norm_g = 1.0 + nrm(ks[8], (N_EVEN, GMLP_HEAD_DIM), 0.02)
    gmlp_norm_b = nrm(ks[9], (N_EVEN, GMLP_HEAD_DIM), 0.02)
    gmlp_ws = nrm(ks[10], (N_EVEN, GMLP_HEADS, GMLP_BLOCK, GMLP_BLOCK), 0.5 * GMLP_BLOCK ** -0.5)
    gmlp_bs = 1.0 + nrm(ks[11], (N_EVEN, GMLP_HEADS, GMLP_BLOCK), 0.02)
    pool_w = nrm(ks[12], (N_EVEN, POOL_GROUPS, POOL_GROUP_DIM, POOL_GROUP_DIM), POOL_GROUP_DIM ** -0.5)
    pool_b = nrm(ks[13], (N_EVEN, POOL_WIDTH), 0.01)
    pool_scale = 1.0 + nrm(ks[14], (N_EVEN, POOL_WIDTH), 0.1)
    e_w_out = nrm(ks[15], (N_EVEN, EVEN_MIX, D_MODEL), DEEPNORM_BETA * EVEN_MIX ** -0.5)
    o_w_in = nrm(ks[16], (N_ODD, D_MODEL, ODD_IN), D_MODEL ** -0.5)
    mla_q_norm_g = 1.0 + nrm(ks[17], (N_ODD, MLA_Q_RANK), 0.02)
    mla_kv_norm_g = 1.0 + nrm(ks[18], (N_ODD, MLA_KV_RANK), 0.02)
    mla_w_uq = nrm(ks[19], (N_ODD, MLA_Q_RANK, MLA_HEADS, MLA_NOPE + MLA_ROPE), MLA_Q_RANK ** -0.5)
    mla_w_uk = nrm(ks[20], (N_ODD, MLA_KV_RANK, MLA_HEADS, MLA_NOPE), MLA_KV_RANK ** -0.5)
    mla_w_uv = nrm(ks[21], (N_ODD, MLA_KV_RANK, MLA_HEADS, MLA_V), MLA_KV_RANK ** -0.5)
    o_w_out = nrm(ks[22], (N_ODD, MLA_WIDTH, D_MODEL), DEEPNORM_BETA * MLA_WIDTH ** -0.5)
    return {"x": x, "c": c, "positions": positions, "ada_w": ada_w, "ada_b": ada_b,
            "ln_g": ln_g, "ln_b": ln_b, "e_w_in": e_w_in, "gmlp_norm_g": gmlp_norm_g,
            "gmlp_norm_b": gmlp_norm_b, "gmlp_ws": gmlp_ws, "gmlp_bs": gmlp_bs,
            "pool_w": pool_w, "pool_b": pool_b, "pool_scale": pool_scale, "e_w_out": e_w_out,
            "o_w_in": o_w_in, "mla_q_norm_g": mla_q_norm_g, "mla_kv_norm_g": mla_kv_norm_g,
            "mla_w_uq": mla_w_uq, "mla_w_uk": mla_w_uk, "mla_w_uv": mla_w_uv, "o_w_out": o_w_out}

def first_block(x, c, positions, ada_w, ada_b, ln_g, ln_b, e_w_in, gmlp_norm_g, gmlp_norm_b,
              gmlp_ws, gmlp_bs, pool_w, pool_b, pool_scale, e_w_out, o_w_in, mla_q_norm_g,
              mla_kv_norm_g, mla_w_uq, mla_w_uk, mla_w_uv, o_w_out):
    cond = jax.nn.silu(c)
    for l in range(DEPTH):
        mod = cond @ ada_w[l] + ada_b[l]
        shift, scale, gate = jnp.split(mod, 3, axis=-1)
        h = x * (1.0 + scale[:, None, :]) + shift[:, None, :]
        if l % 2 == 0:
            e = l // 2
            y = even_mixer(h, e_w_in[e], gmlp_norm_g[e], gmlp_norm_b[e], gmlp_ws[e], gmlp_bs[e],
                           pool_w[e], pool_b[e], pool_scale[e], e_w_out[e])
        else:
            o = l // 2
            y = mla_mixer(h, positions, o_w_in[o], mla_q_norm_g[o], mla_kv_norm_g[o],
                          mla_w_uq[o], mla_w_uk[o], mla_w_uv[o], o_w_out[o])
        x = layer_norm(DEEPNORM_ALPHA * x + (1.0 + gate[:, None, :]) * y, ln_g[l], ln_b[l])
    return x


D_MIX = D_MODEL
D_RET = D_MIX // 2
D_SB = D_MIX - D_RET
RET_HEADS = 4
RET_HEAD_DIM = D_RET // RET_HEADS
SB_HEADS = 8
SB_HEAD_DIM = D_SB // SB_HEADS
ROPE_BASE = 10000.0
EPS = 1e-6
ADA_SCALE = 0.2
SPLIT_SIZES = [D_RET] * 4 + [D_SB] * 4
D_IN = sum(SPLIT_SIZES)


def rms_norm_2(x, g):
    xf = x.astype(jnp.float32)
    return xf * lax.rsqrt(jnp.mean(xf * xf, axis=-1, keepdims=True) + EPS) * g.astype(jnp.float32)

def split_heads(x, n_heads):
    b, s, _ = x.shape
    return x.reshape(b, s, n_heads, -1).transpose(0, 2, 1, 3)

def merge_heads(x):
    b, h, s, d = x.shape
    return x.transpose(0, 2, 1, 3).reshape(b, s, h * d)

def rotary(x, pos):
    half = x.shape[-1] // 2
    inv = ROPE_BASE ** (-jnp.arange(half, dtype=jnp.float32) / half)
    ang = pos[:, None] * inv[None, :]
    cos, sin = jnp.cos(ang), jnp.sin(ang)
    x1, x2 = x[..., :half], x[..., half:]
    return jnp.concatenate([x1 * cos - x2 * sin, x1 * sin + x2 * cos], axis=-1)

def retention(q, k, v):
    b, h, s, d = q.shape
    n = s // CHUNK
    log_gamma = jnp.log1p(-(2.0 ** (-5.0 - jnp.arange(h, dtype=jnp.float32))))
    idx = jnp.arange(CHUNK, dtype=jnp.float32)
    dmask = jnp.exp(jnp.abs(idx[:, None] - idx[None, :])[None] * log_gamma[:, None, None])
    q_dec = jnp.exp((idx + 1.0)[None, :] * log_gamma[:, None])
    k_dec = jnp.exp((CHUNK - 1.0 - idx)[None, :] * log_gamma[:, None])
    chunk_dec = jnp.exp(CHUNK * log_gamma)

    k = k * (d ** -0.5)
    qc = q.reshape(b, h, n, CHUNK, d)
    kc = k.reshape(b, h, n, CHUNK, d)
    vc = v.reshape(b, h, n, CHUNK, v.shape[-1])

    scores = jnp.einsum('bhncd,bhnmd->bhncm', qc, kc) * dmask[None, :, None]
    o_inner = jnp.einsum('bhncm,bhnme->bhnce', scores, vc)

    kv = jnp.einsum('bhnmd,bhnme->nbhde', kc * k_dec[None, :, None, :, None], vc)

    def step(state, kv_i):
        return state * chunk_dec[None, :, None, None] + kv_i, state

    init = jnp.zeros((b, h, d, v.shape[-1]), dtype=kv.dtype)
    _, prev = lax.scan(step, init, kv)
    o_cross = jnp.einsum('bhncd,nbhde->bhnce', qc, prev) * q_dec[None, :, None, :, None]

    o = (o_inner + o_cross).reshape(b, h, s, v.shape[-1])
    mu = jnp.mean(o, axis=-1, keepdims=True)
    var = jnp.mean(jnp.square(o - mu), axis=-1, keepdims=True)
    return (o - mu) * lax.rsqrt(var + EPS)

def stick_breaking(q, k, v):
    b, h, s, d = q.shape
    nb = s // Q_BLOCK
    scale = d ** -0.5
    q_blocks = q.reshape(b, h, nb, Q_BLOCK, d).transpose(2, 0, 1, 3, 4)
    key_pos = jnp.arange(s)

    def block(args):
        qi, bi = args
        t = bi * Q_BLOCK + jnp.arange(Q_BLOCK)
        mask = key_pos[None, :] < t[:, None]
        z = jnp.einsum('bhqd,bhsd->bhqs', qi, k) * scale
        log_beta = jax.nn.log_sigmoid(z)
        log_keep = jnp.where(mask, jax.nn.log_sigmoid(-z), 0.0)
        suffix = lax.cumsum(log_keep, axis=3, reverse=True) - log_keep
        a = jnp.where(mask, jnp.exp(log_beta + suffix), 0.0)
        return jnp.einsum('bhqs,bhse->bhqe', a, v)

    out = lax.map(block, (q_blocks, jnp.arange(nb)))
    return out.transpose(1, 2, 0, 3, 4).reshape(b, h, s, v.shape[-1])

def hybrid_layer(x, c_act, norm_g, w_ada, b_ada, w_in, w_out, pos):
    mod = c_act @ w_ada + b_ada
    shift, scale, gate = jnp.split(mod, 3, axis=-1)
    h = rms_norm_2(x, norm_g) * (1.0 + scale[:, None, :]) + shift[:, None, :]
    proj = h @ w_in
    split_at = [int(i) for i in np.cumsum(SPLIT_SIZES)[:-1]]
    rq, rk, rv, rg, sq, sk, sv, sg = jnp.split(proj, split_at, axis=-1)

    y_ret = retention(rotary(split_heads(rq, RET_HEADS), pos),
                      rotary(split_heads(rk, RET_HEADS), pos),
                      split_heads(rv, RET_HEADS))
    y_ret = merge_heads(y_ret) * jax.nn.silu(rg)

    y_sb = stick_breaking(split_heads(sq, SB_HEADS), split_heads(sk, SB_HEADS),
                          split_heads(sv, SB_HEADS))
    y_sb = merge_heads(y_sb) * jax.nn.silu(sg)

    y = jnp.concatenate([y_ret, y_sb], axis=-1) @ w_out
    return x + gate[:, None, :] * y

def second_inputs(seed: int = 0) -> dict:
    key = jax.random.key(seed)
    ks = jax.random.split(key, 8)
    f32 = jnp.float32
    x = jax.random.normal(ks[0], (BATCH, SEQ, D_MODEL), f32)
    c = jax.random.normal(ks[1], (BATCH, D_MODEL), f32)
    norm_g = 1.0 + 0.02 * jax.random.normal(ks[2], (DEPTH, D_MODEL), f32)
    w_ada = jax.random.normal(ks[3], (DEPTH, D_MODEL, 3 * D_MODEL), f32) * (ADA_SCALE * D_MODEL ** -0.5)
    b_ada = 0.02 * jax.random.normal(ks[4], (DEPTH, 3 * D_MODEL), f32)
    w_in = jax.random.normal(ks[5], (DEPTH, D_MODEL, D_IN), f32) * (D_MODEL ** -0.5)
    w_out = jax.random.normal(ks[6], (DEPTH, D_MIX, D_MODEL), f32) * (D_MIX ** -0.5)
    final_g = 1.0 + 0.02 * jax.random.normal(ks[7], (D_MODEL,), f32)
    return {"x": x, "c": c, "norm_g": norm_g, "w_ada": w_ada, "b_ada": b_ada,
            "w_in": w_in, "w_out": w_out, "final_g": final_g}

def second_block(x, c, norm_g, w_ada, b_ada, w_in, w_out, final_g):
    pos = jnp.arange(x.shape[1], dtype=jnp.float32)
    c_act = jax.nn.silu(c.astype(jnp.float32))
    h = x.astype(jnp.float32)
    for layer in range(DEPTH):
        h = hybrid_layer(h, c_act, norm_g[layer], w_ada[layer], b_ada[layer],
                         w_in[layer], w_out[layer], pos)
    return rms_norm_2(h, final_g).astype(x.dtype)


def setup_inputs(seed=0):
    out = dict(first_inputs(seed))
    for name, value in second_inputs(seed + 1).items():
        if name != "x":
            out[name + "_2"] = value
    return out


def reference(
    x, c, positions, ada_w, ada_b, ln_g, ln_b, e_w_in, gmlp_norm_g, gmlp_norm_b, gmlp_ws,
    gmlp_bs, pool_w, pool_b, pool_scale, e_w_out, o_w_in, mla_q_norm_g, mla_kv_norm_g, mla_w_uq,
    mla_w_uk, mla_w_uv, o_w_out, c_2, norm_g_2, w_ada_2, b_ada_2, w_in_2, w_out_2, final_g_2,
):
    x = first_block(
        x, c, positions, ada_w, ada_b, ln_g, ln_b, e_w_in, gmlp_norm_g, gmlp_norm_b, gmlp_ws,
        gmlp_bs, pool_w, pool_b, pool_scale, e_w_out, o_w_in, mla_q_norm_g, mla_kv_norm_g,
        mla_w_uq, mla_w_uk, mla_w_uv, o_w_out,
    )
    return second_block(
        x, c_2, norm_g_2, w_ada_2, b_ada_2, w_in_2, w_out_2, final_g_2,
    )


_drawn_inputs = setup_inputs


def setup_inputs(seed=0):
    import zlib

    import numpy as np

    out = dict(_drawn_inputs(seed))
    spreads = {}
    factors = {'ada_b': 8.0,
     'gmlp_norm_g': 8.0,
     'gmlp_norm_b': 8.0,
     'gmlp_bs': 8.0,
     'pool_b': 8.0,
     'pool_scale': 4.383,
     'mla_q_norm_g': 8.0,
     'mla_kv_norm_g': 8.0,
     'norm_g_2': 8.0,
     'b_ada_2': 3.576,
     'final_g_2': 2.809}
    for name, (base, spread) in spreads.items():
        noise = np.random.default_rng([zlib.crc32(name.encode()), seed]).standard_normal(out[name].shape)
        drawn = base * np.exp(spread * noise) if base else spread * noise
        out[name] = __import__('jax').numpy.asarray(drawn.astype(out[name].dtype))
    for name, factor in factors.items():
        out[name] = (out[name] * factor).astype(out[name].dtype)
    return out
```

```python
from contextlib import ExitStack

import numpy as np

import concourse.bass as bass
from concourse import mybir

F32 = mybir.dt.float32
F32R = mybir.dt.float32r
I32 = mybir.dt.int32
ALU = mybir.AluOpType
ACT = mybir.ActivationFunctionType
AX = mybir.AxisListType

P = 128
D = 1024
S = 512
NB = S // P
DC = D // P
DEPTH = 4
HD = 256
GH = 4
WINDOWS = (2, 4, 8, 16)
PAD = 16
MH = 16
MLA_ROPE = 64
MLA_SCALE = (128 + 64) ** -0.5
ALPHA = (2.0 * 2) ** 0.25
RH = 4
SP_PAIRS = 4
TILE = 2048
HEAD_COLS = 1280
SEC = 8
UNITS = 3 * DEPTH
MASKED = -1.0e30
INV_2PI = float(1.0 / (2.0 * np.pi))
HALF_PI = float(np.pi / 2)
PI_DOWN = 3.1415925
ROUND = 1.5 * 2.0 ** 23
TWO_PI_PARTS = (6.28125, 0.0019350051879882812, 3.0199159795e-07)

COL = {}
_n = 0
for _name, _k in (("ada_b", 8 * UNITS), ("c", 16), ("ln_g", 16), ("ln_b", 16), ("gmlp_g", 2), ("gmlp_b", 2),
                  ("pool_b", 8), ("pool_scale", 8), ("q_g", 2), ("kv_g", 1), ("norm_g", 16), ("final_g", 8),
                  ("inv", 2), ("eps", 2), ("half", 2)):
    COL[_name] = _n
    _n += _k
NCOL = _n

MAT = {}
_m = 0
for _name, _k in (("ident", P), ("ones", P), ("center", P), ("strict", P), ("edge", 4 * PAD)):
    MAT[_name] = _m
    _m += _k
NMAT = _m


def plan_steps():
    steps = []
    first_out1 = 20 + DC + 2 + 8 + MH // 2
    st = {"T": 0, "C": 0, "post": 0, "cast": 0, "val": 0, "m": 0, "stat": 0}
    tile_done = {}
    tmp_owner = {}
    redux_chunk = {}
    pending = [None]

    def begin(cols=TILE):
        T = st["T"]
        st["T"] += 1
        steps.append(dict(op="tile", T=T, cols=cols))
        return T

    def chunk(kind, T, tmp=True, post=True, cast=False, val=False, **kw):
        C = st["C"]
        st["C"] += 1
        d = dict(op="chunk", kind=kind, T=T, C=C, **kw)
        if tmp:
            d["m"] = st["m"]
            st["m"] += 1
        if val:
            d["val"] = st["val"]
            st["val"] += 1
        if cast:
            d["cast"] = st["cast"]
            st["cast"] += 1
        if post:
            st["post"] += 1
        d["post"] = st["post"] if post else None
        if tmp:
            tmp_owner[d["m"]] = st["post"]
        steps.append(d)
        if T is not None:
            tile_done[T] = ("chunk", C + 1)
        return d

    def stat(width, eps, mean, lhs, count_bank, banks):
        d = dict(stat=st["stat"], width=width, eps=eps, mean=mean, lhs=lhs, count_bank=count_bank, banks=banks)
        st["stat"] += 1
        steps.append(dict(op="stat_cols", **d))
        return d

    def redux(u):
        d = chunk("redux", None, tmp=False, post=True, u=u)
        redux_chunk[u] = d["C"]

    def after_tile(T):
        if T % 8 == 0 and T >= 8 and T // 8 + 1 < UNITS:
            redux(T // 8 + 1)
        if T == first_out1:
            redux(6)

    redux(0)
    redux(1)
    steps.append(dict(op="h", l=0))
    for h in range(GH):
        T = begin()
        chunk("V", T, h=h, c=0)
        chunk("V", T, h=h, c=1)
        if h >= 1:
            steps.append(dict(op="spatial", h=h - 1))
        after_tile(T)
    for kind in ("U", "Z", "ZB"):
        for i in range(4):
            T = begin()
            for sub in range(2):
                d = chunk(kind, T, n=2 * i + sub, sub=sub, tmp=kind != "ZB", post=kind != "ZB",
                          cast=kind == "Z", val=kind == "Z")
            if kind == "U" and i == 0:
                steps.insert(len(steps) - 2, dict(op="spatial", h=GH - 1))
            after_tile(T)

    def pool_mm(g):
        for e in range(2):
            chunk("Y", None, g=g, e=e, n=2 * g + e)

    for g in range(4):
        T = begin()
        for sub in range(2):
            chunk("XB", T, n=2 * g + sub, g=g, sub=sub, tmp=False)
        if g >= 1:
            pool_mm(g - 1)
        after_tile(T)
    pool_mm(3)
    steps.append(dict(op="mixb_split"))
    for n in range(DC):
        T = begin()
        chunk("OUT0", T, n=n, l=0)
        after_tile(T)
    s = stat(D, 0, True, "sums", 7, (6, 5))
    steps.append(dict(op="stat_bcast", **s))
    steps.append(dict(op="ln", l=1, s=s["stat"]))
    T = begin()
    chunk("QC", T, n=0, sub=0, tmp=False, post=False)
    chunk("QC", T, n=1, sub=1, tmp=False, post=False)
    T = begin()
    chunk("QC", T, n=2, sub=0, tmp=False, post=False)
    chunk("QC", T, n=3, sub=1, tmp=False, post=False)
    steps.append(dict(op="qkv_squares"))
    after_tile(T)
    for i in range(8):
        T = begin()
        for sub in range(2):
            chunk("SZ", T, n=2 * i + sub, sub=sub, tmp=False, post=False)
        if i == 0:
            steps.append(dict(op="trig"))
            sq = stat(256, 0, False, "q2", 7, (6,))
        if i == 1:
            steps.append(dict(op="stat_bcast", **sq))
            steps.append(dict(op="q_norm", s=sq["stat"]))
        if i == 2:
            skv = stat(128, 0, False, "kv2", 7, (6,))
        if i == 3:
            steps.append(dict(op="stat_bcast", **skv))
            steps.append(dict(op="kv_norm", s=skv["stat"]))
        if i == 4:
            steps.append(dict(op="kv_transpose"))
        if i == 5:
            steps.append(dict(op="k_rope"))
        after_tile(T)
    first = st["T"]
    for h in range(-1, MH + 2):
        steps.append(dict(op="head", h=h))
    for j in range(MH // 2):
        tile_done[first + j] = ("head", 2 * j + 2)
    st["T"] += MH // 2
    for n in range(DC):
        T = begin()
        chunk("OUT1", T, n=n, l=1)
        after_tile(T)
    s = stat(D, 0, True, "sums", 7, (6, 5))
    steps.append(dict(op="stat_bcast", **s))
    steps.append(dict(op="ln", l=2, s=s["stat"]))
    for l in (2, 3):
        s = stat(D, 1, False, "squares", 7, (6,))
        steps.append(dict(op="stat_bcast", **s))
        steps.append(dict(op="h", l=l, s=s["stat"]))
        base = 8 * (l - 2)
        norm = None
        for u in range(9):
            a = u - 1
            if a >= 0:
                steps.append(dict(op="att_scores", l=l, u=a, g=base + a))
            if u < 8:
                T = begin()
                for sub, kind in enumerate(("AQ", "AK")):
                    chunk(kind, T, l=l, u=u, g=base + u, sub=sub, cast=True, val=u >= SP_PAIRS)
                    if sub == 0 and norm:
                        steps.append(dict(op="stat_bcast", **norm))
                        steps.append(dict(op="ret_norm", l=l, u=a - 1, s=norm["stat"]))
                        norm = None
                after_tile(T)
                T = begin()
                chunk("AV", T, l=l, u=u, g=base + u, sub=0, tmp=False, post=False)
            elif norm:
                steps.append(dict(op="stat_bcast", **norm))
                steps.append(dict(op="ret_norm", l=l, u=a - 1, s=norm["stat"]))
            if a >= 0:
                steps.append(dict(op="att_mid", l=l, u=a, g=base + a))
            if u < 8:
                chunk("AG", T, l=l, u=u, g=base + u, sub=1, tmp=False, post=False)
            if a >= 0:
                steps.append(dict(op="att_out", l=l, u=a, g=base + a))
            if u < 8:
                chunk("VT", None, l=l, u=u, g=base + u, cast=True)
                after_tile(T)
            if a >= SP_PAIRS:
                norm = stat(P, 1, False, "ret2", 7, (7,))
        steps.append(dict(op="stat_bcast", **norm))
        steps.append(dict(op="ret_norm", l=l, u=7, s=norm["stat"]))
        steps.append(dict(op="mix_split", l=l))
        for i in range(4):
            T = begin()
            for sub in range(2):
                chunk("OUT%d" % l, T, n=2 * i + sub, l=l, sub=sub)
            after_tile(T)
    s = stat(D, 1, False, "squares", 7, (6,))
    steps.append(dict(op="stat_bcast", **s))
    steps.append(dict(op="final", s=s["stat"]))
    return steps, st, tile_done, tmp_owner, redux_chunk, first


def build(nc, wt, adat, colst, matst, rmatst, xt, pos, wst, bst, poolt, decayt, rot, out):
    steps, totals, tile_done, tmp_owner, redux_chunk, head_tile = plan_steps()
    NT = totals["T"]
    cols_of = {T: HEAD_COLS if head_tile <= T < head_tile + MH // 2 else TILE for T in range(NT)}

    with ExitStack() as ctx:
        def sem(name):
            return ctx.enter_context(nc.semaphore(name))

        at = [(nc.sbuf_base + 31) // 32 * 32]

        def place(name, shape, dt, offset=None):
            n = 4 * int(np.prod(shape[1:]))
            n = (n + 31) // 32 * 32
            if offset is None:
                offset = at[0]
                at[0] += n
            return nc.alloc_sbuf_tensor_at(name, shape, dt, offset=offset)

        cols = place("cols", [P, NCOL], F32)
        mats = place("mats", [P, NMAT], F32)
        rmats = place("rmats", [P, 4, P], F32R)
        neg_tri, neg_ones, unseen, ident_r = (rmats[:, i, :] for i in range(4))
        mod = place("mod", [P, 8 * UNITS], F32)
        red = place("red", [P, 2, 8], F32)
        cond = place("cond", [P, 16], F32)
        h_scale = place("h_scale", [P, DEPTH, DC], F32)
        h_shift = place("h_shift", [P, DEPTH, DC], F32)
        gate = place("gate", [P, 2, DC], F32)
        q_gain = place("q_gain", [P, 2], F32)
        st_mean = place("st_mean", [P, NB], F32)
        st_sq = place("st_sq", [P, NB], F32)
        st_var = place("st_var", [P, NB], F32)
        st_sd = place("st_sd", [P, NB], F32)
        st_r = place("st_r", [P, NB], F32)
        st_mr = place("st_mr", [P, NB], F32)
        v_stats = place("v_stats", [P, 2, 6], F32)
        v_mv = place("v_mv", [P, 2, 2], F32)
        v_sd = place("v_sd", [P, 2], F32)
        v_rs = place("v_rs", [P, 2], F32)
        neg_max = place("neg_max", [P, NB], F32)
        esum = place("esum", [P, NB], F32)
        rsum = place("rsum", [P, NB], F32)
        w_raw = [place(f"w_raw{i}", [P, TILE], F32) for i in range(2)]
        w_hi = [place(f"w_hi{i}", [P, TILE], F32R) for i in range(2)]
        w_lo = [place(f"w_lo{i}", [P, TILE], F32R) for i in range(2)]
        ada_raw = place("ada_raw", [P, 2, D], F32)
        acc = place("acc", [P, 2, D], F32)
        x = place("x", [P, DC, S], F32)
        h_at = at[0]
        h_hi = place("h_hi", [P, DC, S], F32R)
        h_lo = place("h_lo", [P, DC, S], F32R)
        tmp = place("tmp", [P, 4, S], F32)
        rmats_raw = place("rmats_raw", [P, 4 * P], F32, at[0] - 4 * 4 * S)
        s_at = at[0]
        sum1 = place("sum1", [P, S], F32)
        sum2 = place("sum2", [P, S], F32)
        sqr = place("sqr", [P, S], F32)
        area = at[0]
        KB = 1024

        ada_first = place("ada_first", [P, 16, D], F32, area)
        vn = place("vn", [P, 2, NB, HD], F32, area)
        pooled = place("pooled", [P, 2, 2, S], F32, area)
        park = place("park", [P, DC, S], F32, area + 8 * KB)
        mixa_hi = place("mixa_hi", [P, DC, S], F32R, area + 24 * KB)
        mixa_lo = place("mixa_lo", [P, DC, S], F32R, area + 40 * KB)
        poolw = place("poolw", [P, 4, 2, HD], F32, area + 56 * KB)
        ws = place("ws", [P, GH, P], F32, area + 64 * KB)
        bs = place("bs", [P, GH, P], F32, area + 66 * KB)
        rb = place("rb", [P, DC, P], F32, area + 68 * KB)
        padded = place("padded", [P, 4, PAD + S], F32, area + 64 * KB)
        mixb_hi = place("mixb_hi", [P, DC, S], F32R, h_at)
        mixb_lo = place("mixb_lo", [P, DC, S], F32R, h_at + 16 * KB)
        sz = place("sz", [P, MH, S], F32, area)
        mixc_lo = place("mixc_lo", [P, MH, S], F32R, area)
        mixc_hi = place("mixc_hi", [P, MH, S], F32R, h_at)
        b = area + 32 * KB
        qc_hi = place("qc_hi", [P, 2, S], F32R, b)
        qc_lo = place("qc_lo", [P, 2, S], F32R, b + 4 * KB)
        kv_hi = place("kv_hi", [P, S], F32R, b + 8 * KB)
        kv_lo = place("kv_lo", [P, S], F32R, b + 10 * KB)
        kv_tok = place("kv_tok", [P, NB, P], F32, b + 12 * KB)
        kr_hi = place("kr_hi", [P, S], F32R, b + 14 * KB)
        kr_lo = place("kr_lo", [P, S], F32R, b + 16 * KB)
        cos1 = place("cos1", [P, S], F32, b + 18 * KB)
        sin1 = place("sin1", [P, S], F32, b + 20 * KB)
        qn_hi = place("qn_hi", [P, S], F32R, b + 22 * KB)
        qn_lo = place("qn_lo", [P, S], F32R, b + 24 * KB)
        ql_hi = place("ql_hi", [P, S], F32R, b + 26 * KB)
        ql_lo = place("ql_lo", [P, S], F32R, b + 28 * KB)
        qr_hi = place("qr_hi", [P, S], F32R, b + 30 * KB)
        qr_lo = place("qr_lo", [P, S], F32R, b + 32 * KB)
        pT = place("pT", [P, NB, S], F32, b + 34 * KB)
        qkv = place("qkv", [P, 4, S], F32, b + 34 * KB)
        kv_f = place("kv_f", [P, S], F32, b + 26 * KB)
        kv_sq = place("kv_sq", [P, 2, S], F32, b + 28 * KB)
        ang = place("ang", [P, 3, S], F32, b + 22 * KB)
        posi = place("posi", [P, S], I32, b + 32 * KB)
        rope_t = place("rope_t", [P, S], F32, s_at)
        rope_y = place("rope_y", [P, S], F32, s_at + 2 * KB)
        qr_f = place("qr_f", [P, S], F32, s_at + 4 * KB)
        decay = place("decay", [P, RH, S], F32, area)
        rot_c = place("rot_c", [P, S], F32, area + 8 * KB)
        rot_s = place("rot_s", [P, S], F32, area + 10 * KB)
        b = area + 12 * KB
        aq_hi = place("aq_hi", [P, 2, S], F32R, b)
        aq_lo = place("aq_lo", [P, 2, S], F32R, b + 4 * KB)
        ak_hi = place("ak_hi", [P, S], F32R, b + 8 * KB)
        ak_lo = place("ak_lo", [P, S], F32R, b + 10 * KB)
        av_hi = place("av_hi", [P, NB, P], F32R, b + 12 * KB)
        av_lo = place("av_lo", [P, NB, P], F32R, b + 14 * KB)
        v_raw = place("v_raw", [P, S], F32, b + 16 * KB)
        ag = place("ag", [P, 2, S], F32, b + 18 * KB)
        mixf = place("mixf", [P, DC, S], F32, b + 22 * KB)
        sp_hi = place("sp_hi", [P, 5, S], F32R, b + 38 * KB)
        sp_lo = place("sp_lo", [P, 5, S], F32R, b + 48 * KB)
        rot_t = place("rot_t", [P, S], F32, b + 58 * KB)
        rot_y = place("rot_y", [P, S], F32, b + 60 * KB)
        stage = place("stage", [P, 3, S], F32, s_at)
        outf = place("outf", [P, DC, S], F32, h_at)

        bank = ctx.enter_context(nc.psum_tensor("bank", [P, 8, S], F32))

        ident = mats[:, MAT["ident"]:MAT["ident"] + P]
        ones = mats[:, MAT["ones"]:MAT["ones"] + P]
        center = mats[:, MAT["center"]:MAT["center"] + P]
        strict = mats[:, MAT["strict"]:MAT["strict"] + P]

        def col(name, i=0, n=1):
            return cols[:, COL[name] + i:COL[name] + i + n]

        def f(t):
            return t.bitcast(F32)

        cols_in = sem("cols_in")
        const_in = sem("const_in")
        layer0_in = sem("layer0_in")
        pool_in = sem("pool_in")
        decay_in = sem("decay_in")
        w_landed = [sem(f"w_landed{i}") for i in range(2)]
        w_hi_done = sem("w_hi_done")
        w_lo_done = sem("w_lo_done")
        ada_landed = [sem(f"ada_landed{i}") for i in range(2)]
        ada_first_landed = [sem(f"ada_first_landed{i}") for i in range(16)]
        ada_done = sem("ada_done")
        cond_done = sem("cond_done")
        masks_done = sem("masks_done")
        chunk_full = sem("chunk_full")
        chunk_taken = sem("chunk_taken")
        post_done = sem("post_done")
        val_done = sem("val_done")
        cast_done = sem("cast_done")
        cols_done = sem("cols_done")
        h_t = sem("h_t")
        h_hi_done = sem("h_hi_done")
        h_v_done = sem("h_v_done")
        h_lo_done = sem("h_lo_done")
        x_new = sem("x_new")
        sums_done = sem("sums_done")
        stc_done = sem("stc_done")
        stv_done = sem("stv_done")
        sts_done = sem("sts_done")
        str_done = sem("str_done")
        stb_done = sem("stb_done")
        v_var_done = sem("v_var_done")
        v_sd_done = sem("v_sd_done")
        rows_full = sem("rows_full")
        rb_done = sem("rb_done")
        ws_done = sem("ws_done")
        sv_full = sem("sv_full")
        sv_taken = sem("sv_taken")
        pad_done = sem("pad_done")
        zb_done = sem("zb_done")
        mixb_hi_done = sem("mixb_hi_done")
        mixb_lo_done = sem("mixb_lo_done")
        ang_done = sem("ang_done")
        trig_done = sem("trig_done")
        sq_done = sem("sq_done")
        qk_val = sem("qk_val")
        qk_hi = sem("qk_hi")
        qk_lo = sem("qk_lo")
        kvt_full = sem("kvt_full")
        kvt_taken = sem("kvt_taken")
        fin_done = sem("fin_done")
        out_done = sem("out_done")
        sc_full = sem("sc_full")
        max_done = sem("max_done")
        exp_done = sem("exp_done")
        rsum_done = sem("rsum_done")
        p_done = sem("p_done")
        t_full = sem("t_full")
        t_taken = sem("t_taken")
        pv_full = sem("pv_full")
        ol_hi_done = sem("ol_hi_done")
        ol_lo_done = sem("ol_lo_done")
        o_full = sem("o_full")
        o_taken = sem("o_taken")
        mc_hi_done = sem("mc_hi_done")
        mc_lo_done = sem("mc_lo_done")
        qn_full = sem("qn_full")
        qn_hi_done = sem("qn_hi_done")
        qn_lo_done = sem("qn_lo_done")
        ql_full = sem("ql_full")
        ql_hi_done = sem("ql_hi_done")
        ql_lo_done = sem("ql_lo_done")
        qr_full = sem("qr_full")
        qr_taken = sem("qr_taken")
        qr_val = sem("qr_val")
        qr_hi_done = sem("qr_hi_done")
        qr_lo_done = sem("qr_lo_done")
        z_full = sem("z_full")
        z_log = sem("z_log")
        sp_val = sem("sp_val")
        sp_hi_done = sem("sp_hi_done")
        sp_lo_done = sem("sp_lo_done")
        cum_full = sem("cum_full")
        a_exp = sem("a_exp")
        a_hi_done = sem("a_hi_done")
        a_lo_done = sem("a_lo_done")
        ao_full = sem("ao_full")
        mixf_done = sem("mixf_done")
        rs_full = sem("rs_full")
        rs_val = sem("rs_val")
        rs_hi_done = sem("rs_hi_done")
        rs_lo_done = sem("rs_lo_done")
        ro_full = sem("ro_full")
        ro_taken = sem("ro_taken")
        rc_full = sem("rc_full")
        rsq_done = sem("rsq_done")
        m_hi_done = sem("m_hi_done")
        m_lo_done = sem("m_lo_done")
        in_order = {e: sem(f"{e}_in_order") for e in ("act", "dve", "pool")}

        block = ctx.enter_context(nc.Block())

        def tri(J):
            a = [(0, 0), (1, 0), (2, 0), (3, 0)]
            b = [(4, 0), (3, 128), (2, 256), (1, 384)]
            return a[J], b[J]

        RET_PLACE = [(0, 0), (1, 0), (2, 0), (1, 384)]

        def chain(eng, name):
            count = [0]

            def link(ins):
                count[0] += 1
                ins.then_inc(in_order[name], 1)
                eng.wait_ge(in_order[name], count[0])
            return link

        def wait_unit_scores(eng, g):
            if g >= 0:
                l, u = g // 8, g % 8
                if u < SP_PAIRS:
                    eng.wait_ge(z_full, SP_PAIRS * l + u + 1)
                else:
                    eng.wait_ge(rs_full, RH * l + u - SP_PAIRS + 1)

        def wait_unit_out(eng, g):
            if g >= 0:
                l, u = g // 8, g % 8
                if u < SP_PAIRS:
                    eng.wait_ge(ao_full, SP_PAIRS * l + u + 1)
                else:
                    eng.wait_ge(ro_full, RH * l + u - SP_PAIRS + 1)

        def wait_stage(eng, g):
            l, u = (g - 1) // 8, (g - 1) % 8
            if u < SP_PAIRS:
                eng.wait_ge(a_lo_done, 5 * (SP_PAIRS * l + u + 1))
            else:
                eng.wait_ge(h_lo_done, 4 * DC)

        def wait_tile_done(eng, T):
            if T < 0:
                return
            kind, n = tile_done[T]
            eng.wait_ge(chunk_full if kind == "chunk" else o_full, n)

        MIX_ORDER = [4, 5, 6, 7, 0, 1, 2, 3]
        T_BASE = {("ln", 1): 0, ("ln", 2): DC, ("h", 2): 2 * DC, ("h", 3): 3 * DC}
        RET_UNIT = [8 * (r // RH) + SP_PAIRS + r % RH for r in range(2 * RH)]
        HEAD_CHUNK = tile_done[head_tile - 1][1]
        stats = [d for d in steps if d["op"] == "stat_cols"]
        RET_INDEX = {d["stat"]: i for i, d in enumerate(d for d in stats if d["lhs"] == "ret2")}
        RET_STAT = {i: s for s, i in RET_INDEX.items()}
        STAT_SUMS = {d["stat"]: i + 1 for i, d in enumerate(d for d in stats if d["lhs"] in ("sums", "squares"))}
        H_BASE = {0: 0, 1: DC, 2: 2 * DC, 3: 3 * DC}
        kinds = [d for d in steps if d["op"] == "chunk"]
        Y_CHUNK = {d["g"]: d["C"] for d in kinds if d["kind"] == "Y" and d["e"] == 1}
        AG_CHUNK = {d["g"]: d["C"] for d in kinds if d["kind"] == "AG"}
        QC_CHUNK = min(d["C"] for d in kinds if d["kind"] == "QC")
        XB_LAST = max(d["C"] for d in kinds if d["kind"] == "XB")
        POST_VT_BEFORE = {}
        before = None
        post_of = {}
        for d in steps:
            if d["op"] == "chunk" and d["kind"] == "AV":
                POST_VT_BEFORE[d["C"]] = before
            if d["op"] == "chunk" and d["kind"] == "VT":
                before = d["post"]
            if d["op"] == "chunk":
                key = (d["kind"], d.get("l", 0), d.get("n", d.get("u", d.get("h"))), d.get("c", 0))
                post_of[key] = d["post"]

        @block.sync
        def _(sp):
            sp.dma_start(cols[:], colst).then_inc(cols_in, 16)
            for i in range(2 * SEC):
                sp.dma_start(ada_first[:, i, :], adat[i]).then_inc(ada_first_landed[i], 16)
                if i == 0:
                    sp.dma_start(mats[:], matst).then_inc(const_in, 16)
                    sp.dma_start(rmats_raw[:], rmatst).then_inc(const_in, 16)
            sp.dma_start(x[:], xt).then_inc(const_in, 16)
            sp.dma_start(ws[:], wst).then_inc(layer0_in, 16)
            sp.dma_start(bs[:], bst).then_inc(layer0_in, 16)
            for T in range(NT):
                if T >= 2:
                    sp.wait_ge(w_lo_done, T - 1)
                n = cols_of[T]
                sp.dma_start(w_raw[T % 2][:, 0:n], wt[T, :, 0:n]).then_inc(w_landed[T % 2], 16)
                q = T + 2 * SEC
                if q < SEC * UNITS:
                    if T >= 2:
                        sp.wait_ge(ada_done, q - 1)
                    sp.dma_start(ada_raw[:, T % 2, :], adat[q]).then_inc(ada_landed[T % 2], 16)
                if T == 4:
                    sp.wait_ge(ada_done, 2 * SEC)
                    sp.dma_start(poolw[:], poolt).then_inc(pool_in, 16)
                if T == 29:
                    sp.wait_ge(h_lo_done, 2 * DC)
                    sp.dma_start(posi[:], pos.partition_broadcast(P)).then_inc(layer0_in, 16)
                if T == head_tile + MH // 2 + DC + 1:
                    wait_tile_done(sp, T - 2)
                    sp.dma_start(decay[:], decayt).then_inc(decay_in, 16)
                    sp.dma_start(rot_c[:], rot[0]).then_inc(decay_in, 16)
                    sp.dma_start(rot_s[:], rot[1]).then_inc(decay_in, 16)
            for n in range(DC):
                sp.wait_ge(fin_done, n + 1)
                sp.dma_start(out[:, n, :], outf[:, n, :]).then_inc(out_done, 16)
            sp.wait_ge(out_done, 16 * DC)

        @block.tensor
        def _(pe):
            def mm3(dst, ah, al, bh, bl, start, stop):
                pe.matmul(dst, ah, bl, start=start, stop=False, skip_group_check=True)
                pe.matmul(dst, al, bh, start=False, stop=False, skip_group_check=True)
                return pe.matmul(dst, ah, bh, start=False, stop=stop, skip_group_check=True)

            h_seen = [0]

            def wait_h(l, k):
                if 8 * l + k + 1 > h_seen[0]:
                    h_seen[0] = 8 * l + k + 1
                    pe.wait_ge(h_lo_done, h_seen[0])

            layer = [0]

            def chunk(d):
                kind, T, C = d["kind"], d["T"], d["C"]
                if C >= 2:
                    pe.wait_ge(chunk_taken, C - 1)
                dst = bank[:, C % 2, :]
                if kind == "redux":
                    u = d["u"]
                    pe.wait_ge(ada_done, SEC * (u + 1))
                    if u == 0:
                        pe.wait_ge(const_in, 48)
                    for j in range(DC):
                        ins = pe.matmul(dst[:, j:j + 1], acc[:, u % 2, j * P:(j + 1) * P], ones[:, 0:1],
                                        start=True, stop=True)
                elif kind == "V":
                    for i in range(2):
                        blk = 2 * d["c"] + i
                        for k in range(DC):
                            wait_h(0, k)
                            w = slice(k * HD, (k + 1) * HD)
                            ins = mm3(dst[:, i * HD:(i + 1) * HD],
                                      h_hi[:, k, blk * P:(blk + 1) * P], h_lo[:, k, blk * P:(blk + 1) * P],
                                      w_hi[T % 2][:, w], w_lo[T % 2][:, w], i == 0 and k == 0, k == DC - 1)
                elif kind == "Y":
                    g, e = d["g"], d["e"]
                    if g == 0 and e == 0:
                        pe.wait_ge(pool_in, 16)
                    pe.wait_ge(post_done, post_of["XB", 0, 2 * g + 1, 0])
                    for k in range(2):
                        ins = pe.matmul(dst, poolw[:, g, k, e * P:(e + 1) * P], pooled[:, g % 2, k, :],
                                        start=k == 0, stop=k == 1)
                elif kind in ("OUT0", "OUT1"):
                    for k in range(2 * DC):
                        w = slice(k * P, (k + 1) * P)
                        if kind == "OUT0":
                            if d["n"] == 0 and k == 0:
                                pe.wait_ge(post_done, post_of["Z", 0, DC - 1, 0])
                            if d["n"] == 0 and k >= DC:
                                pe.wait_ge(mixb_lo_done, k - DC + 1)
                            rh, rl = (mixa_hi, mixa_lo) if k < DC else (mixb_hi, mixb_lo)
                            rh, rl = rh[:, k % DC, :], rl[:, k % DC, :]
                        else:
                            if d["n"] == 0:
                                pe.wait_ge(mc_lo_done, k + 1)
                            rh, rl = mixc_hi[:, k, :], mixc_lo[:, k, :]
                        ins = mm3(dst, w_hi[T % 2][:, w], w_lo[T % 2][:, w], rh, rl, k == 0, k == 2 * DC - 1)
                elif kind == "VT":
                    pe.wait_ge(chunk_taken, C - 1)
                    for b in range(NB):
                        ins = pe.transpose(dst[:, b * P:(b + 1) * P], v_raw[:, b * P:(b + 1) * P], ident)
                else:
                    order = MIX_ORDER if kind in ("OUT2", "OUT3") else range(DC)
                    for i, k in enumerate(order):
                        if kind in ("OUT2", "OUT3"):
                            if d["n"] == 0:
                                pe.wait_ge(m_lo_done, DC * (d["l"] - 2) + i + 1)
                        else:
                            wait_h(layer[0], k)
                        a = k * HD + d["sub"] * P
                        ins = mm3(dst, w_hi[T % 2][:, a:a + P], w_lo[T % 2][:, a:a + P],
                                  h_hi[:, k, :], h_lo[:, k, :], i == 0, i == DC - 1)
                ins.then_inc(chunk_full, 1)

            def head_q(t):
                j, e = t // 2, t % 2
                T = head_tile + j
                pe.wait_ge(w_lo_done, T + 1)
                if e == 0:
                    if t == 0:
                        pe.wait_ge(qk_lo, 4)
                    else:
                        pe.wait_ge(ql_lo_done, t)
                    for k in range(2):
                        w = slice(k * 384 + 2 * P, k * 384 + 3 * P)
                        ins = mm3(bank[:, 7, :], w_hi[T % 2][:, w], w_lo[T % 2][:, w],
                                  qc_hi[:, k, :], qc_lo[:, k, :], k == 0, k == 1)
                    ins.then_inc(qr_full, 1)
                    pe.wait_ge(qr_taken, j + 1)
                else:
                    pe.wait_ge(ql_lo_done, t)
                for k in range(2):
                    w = slice(k * 384 + e * P, k * 384 + (e + 1) * P)
                    ins = mm3(bank[:, 7, :], w_hi[T % 2][:, w], w_lo[T % 2][:, w],
                              qc_hi[:, k, :], qc_lo[:, k, :], k == 0, k == 1)
                ins.then_inc(qn_full, 1)

            def head_ql(t):
                T, e = head_tile + t // 2, t % 2
                pe.wait_ge(qn_lo_done, t + 1)
                w = slice(768 + e * P, 768 + (e + 1) * P)
                mm3(bank[:, 7, :], w_hi[T % 2][:, w], w_lo[T % 2][:, w], qn_hi[:], qn_lo[:],
                    True, True).then_inc(ql_full, 1)

            def head_scores(t):
                e = t % 2
                r = slice(64 * e, 64 * e + 64)
                pe.wait_ge(ql_lo_done, t + 1)
                pe.wait_ge(qr_lo_done, t // 2 + 1)
                for i in range(NB):
                    if t >= 1:
                        pe.wait_ge(exp_done, NB * (t - 1) + i + 1)
                    n = (i + 1) * P
                    q = slice(i * P, (i + 1) * P)
                    mm3(bank[:, i, 0:n], ql_hi[:, q], ql_lo[:, q], kv_hi[:, 0:n], kv_lo[:, 0:n], True, False)
                    mm3(bank[:, i, 0:n], qr_hi[r, q], qr_lo[r, q], kr_hi[r, 0:n], kr_lo[r, 0:n],
                        False, True).then_inc(sc_full, 1)

            def head_turn(t):
                for i in range(NB):
                    g = NB * t + i
                    pe.wait_ge(p_done, g + 1)
                    if g >= 2:
                        pe.wait_ge(t_taken, g - 1)
                    for kb in range(i + 1):
                        ins = pe.transpose(bank[:, 4 + g % 2, kb * P:(kb + 1) * P],
                                           tmp[:, i, kb * P:(kb + 1) * P], ident)
                    ins.then_inc(t_full, 1)

            def head_pv(t, kbs):
                if 0 in kbs:
                    pe.wait_ge(t_taken, NB * (t + 1))
                    if t >= 1:
                        pe.wait_ge(o_taken, t)
                for kb in kbs:
                    ins = pe.matmul(bank[:, 6, kb * P:S], kv_tok[:, kb, :], pT[:, kb, kb * P:S],
                                    start=kb == 0, stop=kb == NB - 1, skip_group_check=True)
                if NB - 1 in kbs:
                    ins.then_inc(pv_full, 1)

            def head_o(t):
                T, e = head_tile + t // 2, t % 2
                pe.wait_ge(ol_lo_done, t + 1)
                w = slice(1024 + e * P, 1024 + (e + 1) * P)
                mm3(bank[:, 6, :], w_hi[T % 2][:, w], w_lo[T % 2][:, w], qn_hi[:], qn_lo[:],
                    True, True).then_inc(o_full, 1)

            for d in steps:
                op = d["op"]
                if op == "tile":
                    pe.wait_ge(w_lo_done, d["T"] + 1)
                elif op == "chunk":
                    chunk(d)
                elif op == "h":
                    layer[0] = d["l"]
                elif op == "ln":
                    layer[0] = 1
                elif op == "spatial":
                    h = d["h"]
                    if h == 0:
                        pe.wait_ge(ws_done, 1)
                        pe.matmul(bank[:, 4, :], ones, ws[:].rearrange("p h t -> p (h t)"), start=True,
                                  stop=True).then_inc(rows_full, 1)
                        pe.wait_ge(rb_done, 1)
                    pe.wait_ge(post_done, post_of["V", 0, h, 1])
                    for j in range(2):
                        if h >= 1:
                            pe.wait_ge(sv_taken, 2 * (h - 1) + j + 1)
                        for b in range(NB):
                            ins = pe.matmul(bank[:, 4 + j, b * P:(b + 1) * P], vn[:, h % 2, b, j * P:(j + 1) * P],
                                            ws[:, h, :], start=True, stop=True)
                        ins.then_inc(sv_full, 1)
                elif op == "stat_cols":
                    lhs, si = d["lhs"], d["stat"]
                    if lhs in ("sums", "squares"):
                        pe.wait_ge(sums_done, STAT_SUMS[si])
                    elif lhs in ("q2", "kv2"):
                        pe.wait_ge(sq_done, 1 if lhs == "q2" else 2)
                    else:
                        pe.wait_ge(rsq_done, RET_INDEX[si] + 1)
                    src = {"sums": sum2[:], "squares": sum2[:], "q2": kv_sq[:, 0, :], "kv2": kv_sq[:, 1, :],
                           "ret2": stage[:, 1, :]}[lhs]
                    for b in range(NB):
                        ins = pe.matmul(bank[:, 7, b:b + 1], src[:, b * P:(b + 1) * P], ones[:, 0:1],
                                        start=True, stop=True)
                        if d["mean"]:
                            ins = pe.matmul(bank[:, 7, NB + b:NB + b + 1], sum1[:, b * P:(b + 1) * P],
                                            ones[:, 0:1], start=True, stop=True)
                    ins.then_inc(stc_done, 1)
                elif op == "stat_bcast":
                    pe.wait_ge(str_done, d["stat"] + 1)
                    for src, bk in zip((st_r, st_mr), d["banks"]):
                        for b in range(NB):
                            ins = pe.matmul(bank[:, bk, b * P:(b + 1) * P],
                                            src[:, b:b + 1].broadcast_to([P, P]), ident, start=True, stop=True)
                    ins.then_inc(stb_done, 1)
                elif op == "kv_transpose":
                    pe.wait_ge(qk_val, 3)
                    for b in range(NB):
                        ins = pe.transpose(bank[:, 4, b * P:(b + 1) * P], kv_f[:, b * P:(b + 1) * P], ident)
                    ins.then_inc(kvt_full, 1)
                elif op == "head":
                    t = d["h"]
                    if t == 0:
                        pe.wait_ge(kvt_taken, 1)
                        pe.wait_ge(chunk_taken, HEAD_CHUNK)
                    if 0 <= t < MH:
                        head_scores(t)
                    if 0 <= t - 2 < MH:
                        head_o(t - 2)
                    if 0 <= t - 1 < MH:
                        head_turn(t - 1)
                    if t + 1 < MH:
                        head_q(t + 1)
                    if 0 <= t - 1 < MH:
                        head_pv(t - 1, (0, 1))
                    if t + 1 < MH:
                        head_ql(t + 1)
                    if 0 <= t - 1 < MH:
                        head_pv(t - 1, (2, 3))
                elif op == "att_scores":
                    g, u, l = d["g"], d["u"], d["l"]
                    if 1 <= u <= SP_PAIRS:
                        pe.wait_ge(mixf_done, g)
                    if u < SP_PAIRS:
                        s = SP_PAIRS * (l - 2) + u
                        pe.wait_ge(post_done, post_of["AK", l, u, 0])
                        started = set()
                        for e in range(2):
                            for J in range(NB):
                                bk, c0 = tri(J)[e]
                                ins = mm3(bank[:, 2 + bk, c0:c0 + (NB - J) * P], ak_hi[:, J * P:(J + 1) * P],
                                          ak_lo[:, J * P:(J + 1) * P], aq_hi[:, e, J * P:S],
                                          aq_lo[:, e, J * P:S], bk not in started, False)
                                started.add(bk)
                        ins.then_inc(z_full, 1)
                    else:
                        r = RH * (l - 2) + u - SP_PAIRS
                        pe.wait_ge(post_done, post_of["AK", l, u, 0])
                        for J in range(NB):
                            bk, c0 = RET_PLACE[J]
                            ins = mm3(bank[:, 2 + bk, c0:c0 + (NB - J) * P], ak_hi[:, J * P:(J + 1) * P],
                                      ak_lo[:, J * P:(J + 1) * P], aq_hi[:, 0, J * P:S], aq_lo[:, 0, J * P:S],
                                      J < 3, True)
                        ins.then_inc(rs_full, 1)
                elif op == "att_mid":
                    u, l = d["u"], d["l"]
                    if u < SP_PAIRS:
                        s = SP_PAIRS * (l - 2) + u
                        pe.wait_ge(sp_lo_done, 5 * (s + 1))
                        for e in range(2):
                            for J in range(NB):
                                bk, c0 = tri(J)[e]
                                for j in range(J, NB):
                                    bj, cj = tri(j)[e]
                                    lhs = neg_tri if j == J else neg_ones
                                    o = bank[:, 2 + bk, c0 + (j - J) * P:c0 + (NB - J) * P]
                                    for part in (sp_lo, sp_hi):
                                        pe.matmul(o, lhs, part[:, bj, cj:cj + (NB - j) * P],
                                                  start=False, stop=False, skip_group_check=True)
                                ins = pe.matmul(bank[:, 2 + bk, c0:c0 + P], ident_r, unseen,
                                                start=False, stop=False, skip_group_check=True)
                        ins.then_inc(cum_full, 1)
                    else:
                        r = RH * (l - 2) + u - SP_PAIRS
                        pe.wait_ge(rs_lo_done, 3 * (r + 1))
                        pe.wait_ge(post_done, post_of["VT", l, u, 0])
                        if r >= 1:
                            pe.wait_ge(ro_taken, r)
                        for J in range(NB):
                            bk, c0 = RET_PLACE[J]
                            w = slice(c0, c0 + (NB - J) * P)
                            ins = mm3(bank[:, 5, J * P:S], av_hi[:, J, :], av_lo[:, J, :], sp_hi[:, bk, w],
                                      sp_lo[:, bk, w], J == 0, J == NB - 1)
                        ins.then_inc(ro_full, 1)
                elif op == "att_out":
                    u, l = d["u"], d["l"]
                    if u < SP_PAIRS:
                        s = SP_PAIRS * (l - 2) + u
                        pe.wait_ge(a_lo_done, 5 * (s + 1))
                        pe.wait_ge(post_done, post_of["VT", l, u, 0])
                        for e in range(2):
                            for J in range(NB):
                                bk, c0 = tri(J)[e]
                                w = slice(c0, c0 + (NB - J) * P)
                                ins = mm3(bank[:, 2 + e, J * P:S], av_hi[:, J, :], av_lo[:, J, :],
                                          sp_hi[:, bk, w], sp_lo[:, bk, w], J == 0, J == NB - 1)
                        ins.then_inc(ao_full, 1)
                    else:
                        r = RH * (l - 2) + u - SP_PAIRS
                        pe.wait_ge(ro_taken, r + 1)
                        if r >= 1:
                            pe.wait_ge(mixf_done, RET_UNIT[r - 1] + 1)
                        pe.matmul(bank[:, 6, :], center, stage[:, 0, :], start=True, stop=True).then_inc(rc_full, 1)

        @block.scalar
        def _(act):
            link = chain(act, "act")

            def split_tile(T):
                n = cols_of[T]
                act.wait_ge(w_landed[T % 2], 16 * (T // 2 + 1))
                wait_tile_done(act, T - 2)
                act.activation(w_hi[T % 2][:, 0:n], w_raw[T % 2][:, 0:n], ACT.Copy).then_inc(w_hi_done, 1)

            def chunk(d):
                kind, C, l = d["kind"], d["C"], d.get("l", 0)
                act.wait_ge(chunk_full, C + 1)
                if "m" in d:
                    if d["m"] >= 4:
                        act.wait_ge(post_done, tmp_owner[d["m"] - 4])
                    dst = tmp[:, d["m"] % 4, :]
                src = bank[:, C % 2, :]
                func, scale, bias = ACT.Copy, 1.0, 0.0
                if kind == "redux":
                    u = d["u"]
                    if u >= 2:
                        act.wait_ge(post_done, post_of["redux", 0, u - 2, 0])
                    dst, src = red[:, u % 2, :], src[:, 0:8]
                elif kind == "Z":
                    func = ACT.Silu
                elif kind == "ZB":
                    act.wait_ge(post_done, post_of["Z", 0, d["n"], 0])
                    func, dst = ACT.Silu, park[:, d["n"], :]
                elif kind == "XB":
                    if d["n"] >= 2:
                        act.wait_ge(post_done, post_of["XB", 0, d["n"] - 2, 0])
                    else:
                        act.wait_ge(pad_done, 4)
                    dst = padded[:, d["n"] % 2, PAD:PAD + S]
                elif kind == "Y":
                    func, bias = ACT.Identity, col("pool_b", d["n"])
                elif kind in ("OUT0", "OUT1"):
                    scale = gate[:, l, d["n"]:d["n"] + 1]
                elif kind in ("OUT2", "OUT3"):
                    scale = mod[:, 8 * (3 * l + 2) + d["n"]:8 * (3 * l + 2) + d["n"] + 1]
                elif kind == "QC":
                    dst = qkv[:, d["n"], :]
                elif kind == "SZ":
                    func, dst = ACT.Silu, sz[:, d["n"], :]
                elif kind == "AQ" and d["u"] < SP_PAIRS:
                    scale = 0.125
                elif kind == "AV":
                    if d["g"] >= 1:
                        act.wait_ge(post_done, POST_VT_BEFORE[d["C"]])
                    dst = v_raw[:]
                elif kind == "AG":
                    g = d["g"]
                    if g >= 2:
                        act.wait_ge(mixf_done, g - 1)
                    func, dst = ACT.Silu, ag[:, g % 2, :]
                if kind[:3] == "OUT" and d["n"] == 0:
                    act.wait_ge(post_done, post_of["redux", 0, 3 * l + 2, 0])
                act.activation(dst, src, func, scale=scale, bias=bias).then_inc(chunk_taken, 1)

            act.wait_ge(cols_in, 16)
            act.activation(cond[:], col("c", 0, 16), ACT.Silu).then_inc(cond_done, 1)
            act.wait_ge(const_in, 48)
            act.activation(rmats[:].rearrange("p a b -> p (a b)"), rmats_raw[:], ACT.Copy).then_inc(masks_done, 1)
            act.wait_ge(masks_done, 1)
            split_tile(0)
            v_count = 0
            for d in steps:
                op = d["op"]
                if op == "tile":
                    T = d["T"] + 1
                    if T < NT:
                        split_tile(T)
                elif op == "chunk":
                    chunk(d)
                    if d["kind"] == "V":
                        v_count += 1
                        act.wait_ge(v_var_done, v_count)
                        act.activation(v_sd[:], v_mv[:, :, 1], ACT.Sqrt, bias=col("eps", 0)).then_inc(v_sd_done, 1)
                elif op == "stat_cols":
                    act.wait_ge(stv_done, d["stat"] + 1)
                    act.activation(st_sd[:], st_var[:], ACT.Sqrt,
                                   bias=col("eps", d["eps"])).then_inc(sts_done, 1)
                elif op == "h" and d["l"] == 0:
                    act.wait_ge(cols_done, 1)
                    for k in range(DC):
                        act.activation(h_hi[:, k, :], x[:, k, :], ACT.Identity, scale=h_scale[:, 0, k:k + 1],
                                       bias=h_shift[:, 0, k:k + 1]).then_inc(h_hi_done, 1)
                elif op == "ln" or op == "h":
                    l = d["l"]
                    first = T_BASE[op, l]
                    if op == "h" or l == 1:
                        act.wait_ge(cols_done, l + 1)
                    for k in range(DC):
                        act.wait_ge(h_t, first + k + 1)
                        t = x[:, k, :] if op == "ln" else tmp[:, k % 2, :]
                        if op == "h" or l == 1:
                            act.activation(h_hi[:, k, :], t, ACT.Identity, scale=h_scale[:, l, k:k + 1],
                                           bias=h_shift[:, l, k:k + 1]).then_inc(h_hi_done, 1)
                        if op == "ln":
                            g = DC * (l - 1) + k
                            if l == 1:
                                act.wait_ge(h_v_done, DC + k + 1)
                                act.wait_ge(h_hi_done, DC + k + 1)
                            act.activation(x[:, k, :], x[:, k, :], ACT.Identity, scale=col("ln_g", g),
                                           bias=col("ln_b", g)).then_inc(x_new, 1)
                elif op == "trig":
                    act.wait_ge(ang_done, 1)
                    act.activation(sin1[:], ang[:, 1, :], ACT.Sin, scale=col("inv", 1)).then_inc(trig_done, 1)
                    act.wait_ge(ang_done, 2)
                    act.activation(cos1[:], ang[:, 2, :], ACT.Sin).then_inc(trig_done, 1)
                elif op == "kv_transpose":
                    act.wait_ge(kvt_full, 1)
                    act.activation(kv_tok[:].rearrange("p b r -> p (b r)"), bank[:, 4, :],
                                   ACT.Copy).then_inc(kvt_taken, 1)
                elif op == "head":
                    t = d["h"]
                    for i in range(NB):
                        if 0 <= t - 1 < MH:
                            g = NB * (t - 1) + i
                            act.wait_ge(t_full, g + 1)
                            if i == 0 and t >= 2:
                                act.wait_ge(pv_full, t - 1)
                            n = (i + 1) * P
                            act.activation(pT[:, 0:i + 1, i * P:(i + 1) * P],
                                           bank[:, 4 + g % 2, 0:n].rearrange("p (a b) -> p a b", b=P),
                                           ACT.Copy).then_inc(t_taken, 1)
                        if 0 <= t < MH:
                            g = NB * t + i
                            n = (i + 1) * P
                            act.wait_ge(max_done, g + 1)
                            if t >= 1:
                                act.wait_ge(p_done, g - 3)
                                act.wait_ge(rsum_done, g - 3)
                            act.activation(tmp[:, i, 0:n], bank[:, i, 0:n], ACT.Exp, bias=neg_max[:, i:i + 1],
                                           accum_out=esum[:, i:i + 1]).then_inc(exp_done, 1)
                    if t % 2 == 1 and 1 <= t <= MH - 1:
                        split_tile(head_tile + (t + 1) // 2)
                    if t + 1 < MH and (t + 1) % 2 == 0:
                        j = (t + 1) // 2
                        act.wait_ge(qr_full, j + 1)
                        if j >= 1:
                            act.wait_ge(qr_val, j)
                        act.activation(qr_f[:], bank[:, 7, :], ACT.Copy).then_inc(qr_taken, 1)
                    if t + 1 < MH:
                        act.wait_ge(qn_full, t + 2)
                        if t - 1 >= 1:
                            act.wait_ge(o_full, t - 1)
                        act.activation(qn_hi[:], bank[:, 7, :], ACT.Copy).then_inc(qn_hi_done, 1)
                        act.wait_ge(ql_full, t + 2)
                        if t >= 0:
                            act.wait_ge(sc_full, NB * (t + 1))
                        act.activation(ql_hi[:], bank[:, 7, :], ACT.Copy).then_inc(ql_hi_done, 1)
                    if 0 <= t - 1 < MH:
                        act.wait_ge(pv_full, t)
                        act.activation(qn_hi[:], bank[:, 6, :], ACT.Copy).then_inc(ol_hi_done, 1)
                elif op == "att_scores" and d["u"] < SP_PAIRS:
                    s = SP_PAIRS * (d["l"] - 2) + d["u"]
                    nc.scalar.preload_act_table_set("natural_log_exp_and_others")
                    act.wait_ge(z_full, s + 1)
                    for i in range(5):
                        if i < 3:
                            if s >= 1:
                                wait_stage(act, d["g"])
                        else:
                            act.wait_ge(sp_lo_done, 5 * s + i - 2)
                        link(act.activation(stage[:, i % 3, :], bank[:, 2 + i, :], ACT.Abs))
                        link(act.activation(stage[:, i % 3, :], stage[:, i % 3, :], ACT.Exp, scale=-1.0))
                        act.activation(stage[:, i % 3, :], stage[:, i % 3, :], ACT.Ln, bias=1.0).then_inc(z_log, 1)
                elif op == "att_mid":
                    u, l = d["u"], d["l"]
                    if u < SP_PAIRS:
                        s = SP_PAIRS * (l - 2) + u
                        act.wait_ge(cum_full, s + 1)
                        for i in range(5):
                            if i >= 3:
                                act.wait_ge(a_lo_done, 5 * s + i - 2)
                            act.activation(stage[:, i % 3, :], bank[:, 2 + i, :], ACT.Exp).then_inc(a_exp, 1)
                    else:
                        r = RH * (l - 2) + u - SP_PAIRS
                        act.wait_ge(ro_full, r + 1)
                        act.activation(stage[:, 0, :], bank[:, 5, :], ACT.Copy).then_inc(ro_taken, 1)
                elif op == "att_out" and d["u"] >= SP_PAIRS:
                    r = RH * (d["l"] - 2) + d["u"] - SP_PAIRS
                    act.wait_ge(rc_full, r + 1)
                    act.activation(stage[:, 1, :], bank[:, 6, :], ACT.Square).then_inc(rsq_done, 1)

        @block.vector
        def _(dve):
            link = chain(dve, "dve")

            def split_tile(T):
                n = cols_of[T]
                dve.wait_ge(w_hi_done, T + 1)
                dve.tensor_tensor(w_lo[T % 2][:, 0:n], w_raw[T % 2][:, 0:n], f(w_hi[T % 2][:, 0:n]),
                                  ALU.subtract).then_inc(w_lo_done, 1)

            def ada_piece(q):
                u, k = q // SEC, q % SEC
                if q >= SEC * UNITS:
                    return
                if q < 2 * SEC:
                    dve.wait_ge(ada_first_landed[q], 16)
                    src = ada_first[:, q, :]
                else:
                    i = q - 2 * SEC
                    dve.wait_ge(ada_landed[i % 2], 16 * (i // 2 + 1))
                    src = ada_raw[:, i % 2, :]
                c = cond[:, 8 * (u // 6) + k:8 * (u // 6) + k + 1]
                if k == 0:
                    if u >= 2:
                        dve.wait_ge(chunk_full, redux_chunk[u - 2] + 1)
                    dve.tensor_scalar(acc[:, u % 2, :], src, c, None, ALU.mult).then_inc(ada_done, 1)
                else:
                    dve.wait_ge(ada_done, q)
                    dve.scalar_tensor_tensor(acc[:, u % 2, :], src, c, acc[:, u % 2, :], ALU.mult,
                                             ALU.add).then_inc(ada_done, 1)

            def rope(src, ct, sn, turned, res, half, signal, wait_before):
                for a in range(0, P, 2 * half):
                    x1, x2 = slice(a, a + half), slice(a + half, a + 2 * half)
                    dve.tensor_tensor(turned[x1, :], src[x2, :], sn[x2, :], ALU.mult)
                    ins = dve.tensor_tensor(turned[x2, :], src[x1, :], sn[x1, :], ALU.mult)
                link(ins)
                link(dve.tensor_tensor(res, src, ct, ALU.mult))
                dve.tensor_tensor(res, res, turned, ALU.add).then_inc(signal, 1)

            def chunk(d):
                kind, C, l, n = d["kind"], d["C"], d.get("l", 0), d.get("n")
                if d["post"] is None:
                    return
                dve.wait_ge(chunk_taken, C + 1)
                if d["post"] >= 2:
                    dve.wait_ge(post_done, d["post"] - 1)
                t = tmp[:, d["m"] % 4, :] if "m" in d else None
                if kind == "redux":
                    u = d["u"]
                    m = mod[:, 8 * u:8 * u + 8]
                    ins = dve.tensor_tensor(m, red[:, u % 2, :], col("ada_b", 8 * u, 8), ALU.add)
                    if u % 3 == 2 and u < 6:
                        link(ins)
                        ins = dve.tensor_scalar(gate[:, u // 3, :], m, 1.0, None, ALU.add)
                elif kind == "V":
                    h, c = d["h"], d["c"]
                    for i in range(2):
                        ins = dve.bn_stats(v_stats[:, i, :], t[:, i * HD:(i + 1) * HD])
                    link(ins)
                    for i in range(2):
                        ins = dve.bn_aggr(v_mv[:, i, :], v_stats[:, i, :])
                    ins.then_inc(v_var_done, 1)
                    count = 2 * h + c + 1
                    dve.wait_ge(v_sd_done, count)
                    link(dve.reciprocal(v_rs[:], v_sd[:]))
                    if h >= 2:
                        dve.wait_ge(sv_full, 2 * (h - 1))
                    for i in range(2):
                        ins = dve.tensor_scalar(vn[:, h % 2, 2 * c + i, :], t[:, i * HD:(i + 1) * HD],
                                                v_mv[:, i, 0:1], v_rs[:, i:i + 1], ALU.subtract, ALU.mult)
                elif kind == "U":
                    dve.wait_ge(sv_taken, n + 1)
                    ins = dve.tensor_tensor(park[:, n, :], park[:, n, :], t, ALU.mult)
                elif kind == "Z":
                    dve.wait_ge(post_done, post_of["U", 0, n, 0])
                    dve.tensor_tensor(park[:, n, :], park[:, n, :], t, ALU.mult).then_inc(val_done, 1)
                    dve.wait_ge(cast_done, d["cast"] + 1)
                    ins = dve.tensor_tensor(mixa_lo[:, n, :], park[:, n, :], f(mixa_hi[:, n, :]), ALU.subtract)
                elif kind == "XB":
                    g = d["g"]
                    win = WINDOWS[g]
                    src = padded[:, n % 2, :]
                    cur, step = src, 1
                    for i in range(g + 1):
                        nxt = padded[:, 2 + i % 2, :]
                        link(dve.tensor_tensor(nxt[:, PAD:], cur[:, PAD:], cur[:, PAD - step:PAD + S - step],
                                               ALU.add))
                        cur, step = nxt, 2 * step
                    edge = mats[:, MAT["edge"] + g * PAD:MAT["edge"] + g * PAD + win]
                    link(dve.tensor_tensor(cur[:, PAD:PAD + win], cur[:, PAD:PAD + win], edge, ALU.mult))
                    if g == 0:
                        dve.wait_ge(sv_full, 2 * GH)
                    if g >= 2:
                        dve.wait_ge(chunk_full, Y_CHUNK[g - 2] + 1)
                    ins = dve.scalar_tensor_tensor(pooled[:, g % 2, n % 2, :], cur[:, PAD:], 1.0 / win,
                                                   src[:, PAD:], ALU.mult, ALU.subtract)
                elif kind == "Y":
                    ins = dve.scalar_tensor_tensor(park[:, n, :], t, col("pool_scale", n), park[:, n, :],
                                                   ALU.mult, ALU.mult)
                elif kind in ("OUT0", "OUT1"):
                    if n == 0 and l == 1:
                        dve.wait_ge(x_new, DC)
                    ins = dve.scalar_tensor_tensor(x[:, n, :], x[:, n, :], ALPHA, t, ALU.mult, ALU.add)
                elif kind in ("OUT2", "OUT3"):
                    if n == 0:
                        dve.wait_ge(x_new, 2 * DC)
                    ins = dve.tensor_tensor(x[:, n, :], x[:, n, :], t, ALU.add)
                elif kind in ("AQ", "AK"):
                    u, g = d["u"], d["g"]
                    if u >= SP_PAIRS:
                        if u == SP_PAIRS:
                            dve.wait_ge(decay_in, 48)
                        rope(t, rot_c[:], rot_s[:], rot_t[:], rot_y[:], 64, val_done, None)
                        src = rot_y[:]
                    else:
                        src = t
                    dve.wait_ge(cast_done, d["cast"] + 1)
                    if kind == "AK":
                        ins = dve.tensor_tensor(ak_lo[:], src, f(ak_hi[:]), ALU.subtract)
                    elif u >= SP_PAIRS:
                        ins = dve.tensor_tensor(aq_lo[:, 0, :], src, f(aq_hi[:, 0, :]), ALU.subtract)
                    else:
                        for e in range(2):
                            ins = dve.scalar_tensor_tensor(aq_lo[:, e, :], src, col("half", e), f(aq_hi[:, e, :]),
                                                           ALU.mult, ALU.subtract)
                elif kind == "VT":
                    dve.wait_ge(cast_done, d["cast"] + 1)
                    ins = dve.tensor_tensor(av_lo[:].rearrange("p b r -> p (b r)"), t,
                                            f(av_hi[:].rearrange("p b r -> p (b r)")), ALU.subtract)
                ins.then_inc(post_done, 1)

            def h_low(l, k):
                dve.wait_ge(h_hi_done, H_BASE[l] + k + 1)
                dve.wait_ge(h_v_done, H_BASE[l] + k + 1)
                dve.tensor_tensor(h_lo[:, k, :], tmp[:, 2 + k % 2, :], f(h_hi[:, k, :]),
                                  ALU.subtract).then_inc(h_lo_done, 1)

            def h_columns(l):
                shift, scale = mod[:, 24 * l:24 * l + 8], mod[:, 24 * l + 8:24 * l + 16]
                if l == 0:
                    dve.wait_ge(post_done, post_of["redux", 0, 1, 0])
                    dve.tensor_scalar(h_scale[:, 0, :], scale, 1.0, None, ALU.add)
                    dve.tensor_copy(h_shift[:, 0, :], shift).then_inc(cols_done, 1)
                    return
                dve.wait_ge(post_done, post_of["redux", 0, 3 * l + 1, 0])
                gain = col("ln_g", 0, 8) if l == 1 else col("norm_g", 8 * (l - 2), 8)
                link(dve.tensor_scalar(h_scale[:, l, :], scale, 1.0, None, ALU.add))
                if l == 1:
                    link(dve.tensor_tensor(h_shift[:, 1, :], h_scale[:, 1, :], col("ln_b", 0, 8), ALU.mult))
                    link(dve.tensor_tensor(h_shift[:, 1, :], h_shift[:, 1, :], shift, ALU.add))
                else:
                    link(dve.tensor_copy(h_shift[:, l, :], shift))
                dve.tensor_tensor(h_scale[:, l, :], h_scale[:, l, :], gain, ALU.mult).then_inc(cols_done, 1)

            def statistics(d):
                si, w = d["stat"], 1.0 / d["width"]
                dve.wait_ge(stc_done, si + 1)
                if d["mean"]:
                    dve.tensor_scalar(st_sq[:], bank[:, 7, 0:NB], w, None, ALU.mult)
                    link(dve.tensor_scalar(st_mean[:], bank[:, 7, NB:2 * NB], w, None, ALU.mult))
                    link(dve.tensor_tensor(st_var[:], st_mean[:], st_mean[:], ALU.mult))
                    link(dve.tensor_tensor(st_var[:], st_sq[:], st_var[:], ALU.subtract))
                    dve.tensor_scalar(st_var[:], st_var[:], 0.0, None, ALU.max).then_inc(stv_done, 1)
                else:
                    dve.tensor_scalar(st_var[:], bank[:, 7, 0:NB], w, None, ALU.mult).then_inc(stv_done, 1)
                dve.wait_ge(sts_done, si + 1)
                ins = dve.reciprocal(st_r[:], st_sd[:])
                if d["mean"]:
                    link(ins)
                    ins = dve.tensor_tensor(st_mr[:], st_mean[:], st_r[:], ALU.mult)
                ins.then_inc(str_done, 1)

            def angles():
                dve.wait_ge(layer0_in, 48)
                dve.wait_ge(x_new, DC)
                a0, a1, a2 = (ang[:, i, :] for i in range(3))
                link(dve.tensor_copy(a0, posi[:]))
                link(dve.tensor_scalar(a0, a0, col("inv", 0), None, ALU.mult))
                for dst, turn, more in ((a1, 0.0, 0.0), (a2, 0.25, HALF_PI)):
                    link(dve.tensor_scalar(rope_t[:], a0, INV_2PI, turn, ALU.mult, ALU.add))
                    link(dve.tensor_scalar(rope_t[:], rope_t[:], ROUND, None, ALU.add))
                    link(dve.tensor_scalar(rope_t[:], rope_t[:], ROUND, None, ALU.subtract))
                    link(dve.scalar_tensor_tensor(dst, rope_t[:], -TWO_PI_PARTS[0], a0, ALU.mult, ALU.add))
                    link(dve.scalar_tensor_tensor(dst, rope_t[:], -TWO_PI_PARTS[1], dst, ALU.mult, ALU.add))
                    link(dve.scalar_tensor_tensor(dst, rope_t[:], -TWO_PI_PARTS[2], dst, ALU.mult, ALU.add))
                    if more:
                        link(dve.tensor_scalar(dst, dst, more, None, ALU.add))
                    dve.tensor_scalar(dst, dst, PI_DOWN, -PI_DOWN, ALU.min, ALU.max).then_inc(ang_done, 1)

            def head(t):
                if 0 <= t < MH:
                    for i in range(NB):
                        g = NB * t + i
                        dve.wait_ge(sc_full, g + 1)
                        link(dve.memset(bank[0:64, i, i * P + 64:(i + 1) * P], MASKED))
                        if t >= 1:
                            dve.wait_ge(exp_done, g - 3)
                        dve.tensor_reduce(neg_max[:, i:i + 1], bank[:, i, 0:(i + 1) * P], AX.X, ALU.max,
                                          negate=True).then_inc(max_done, 1)
                if 0 <= t - 2 < MH:
                    dve.wait_ge(o_full, t - 1)
                    dve.wait_ge(chunk_taken, HEAD_CHUNK)
                    dve.tensor_tensor(sz[:, t - 2, :], bank[:, 6, :], sz[:, t - 2, :],
                                      ALU.mult).then_inc(o_taken, 1)
                if t % 2 == 1 and 1 <= t <= MH - 1:
                    T = head_tile + (t + 1) // 2
                    split_tile(T)
                    ada_piece(T - 1 + 2 * SEC)
                if 0 <= t - 2 < MH:
                    dve.wait_ge(mc_hi_done, t - 1)
                    dve.tensor_tensor(mixc_lo[:, t - 2, :], sz[:, t - 2, :], f(mixc_hi[:, t - 2, :]),
                                      ALU.subtract).then_inc(mc_lo_done, 1)
                if 0 <= t < MH:
                    for i in range(NB):
                        g = NB * t + i
                        dve.wait_ge(exp_done, g + 1)
                        if t >= 1:
                            dve.wait_ge(p_done, g - 3)
                        dve.reciprocal(rsum[:, i:i + 1], esum[:, i:i + 1]).then_inc(rsum_done, 1)
                if t + 1 < MH and (t + 1) % 2 == 0:
                    j = (t + 1) // 2
                    dve.wait_ge(qr_taken, j + 1)
                    rope(qr_f[:], cos1[:], sin1[:], rope_t[:], rope_y[:], 32, qr_val, None)
                    dve.wait_ge(qr_hi_done, j + 1)
                    dve.tensor_tensor(qr_lo[:], rope_y[:], f(qr_hi[:]), ALU.subtract).then_inc(qr_lo_done, 1)
                if t + 1 < MH:
                    dve.wait_ge(qn_hi_done, t + 2)
                    dve.tensor_tensor(qn_lo[:], bank[:, 7, :], f(qn_hi[:]), ALU.subtract).then_inc(qn_lo_done, 1)
                    dve.wait_ge(ql_hi_done, t + 2)
                    dve.tensor_tensor(ql_lo[:], bank[:, 7, :], f(ql_hi[:]), ALU.subtract).then_inc(ql_lo_done, 1)
                if 0 <= t - 1 < MH:
                    dve.wait_ge(ol_hi_done, t)
                    dve.tensor_tensor(qn_lo[:], bank[:, 6, :], f(qn_hi[:]), ALU.subtract).then_inc(ol_lo_done, 1)

            def wait_sp_free(g):
                wait_unit_out(dve, g - 1)

            dve.wait_ge(cond_done, 1)
            for q in range(2 * SEC):
                ada_piece(q)
            for d in steps:
                op = d["op"]
                if op == "tile":
                    T = d["T"]
                    if T == 0:
                        split_tile(0)
                    if T + 1 < NT:
                        split_tile(T + 1)
                    ada_piece(T + 2 * SEC)
                elif op == "chunk":
                    if d["kind"] == "XB" and d["n"] == 0:
                        dve.wait_ge(sv_full, 2 * GH)
                        dve.wait_ge(sv_taken, 2 * GH)
                        for i in range(4):
                            dve.memset(padded[:, i, 0:PAD], 0.0).then_inc(pad_done, 1)
                        dve.wait_ge(pad_done, 4)
                    chunk(d)
                elif op == "spatial":
                    h = d["h"]
                    if h == 0:
                        dve.wait_ge(layer0_in, 32)
                        dve.memset(ws[64:P, :, 0:64], 0.0).then_inc(ws_done, 1)
                        dve.wait_ge(rows_full, 1)
                        for i in range(DC):
                            hh, j = i // 2, i % 2
                            link(dve.scalar_tensor_tensor(rb[:, i, :], bank[:, 4, hh * P:(hh + 1) * P],
                                                          col("gmlp_b", j), bs[:, hh, :], ALU.mult, ALU.add))
                        dve.sem_inc(rb_done, 1)
                    for j in range(2):
                        n = 2 * h + j
                        dve.wait_ge(sv_full, n + 1)
                        dve.scalar_tensor_tensor(park[:, n, :].rearrange("p (b t) -> p b t", b=NB),
                                                 bank[:, 4 + j, :].rearrange("p (b t) -> p b t", b=NB),
                                                 col("gmlp_g", j),
                                                 rb[:, n:n + 1, :].broadcast_to([P, NB, P]),
                                                 ALU.mult, ALU.add).then_inc(sv_taken, 1)
                elif op == "mixb_split":
                    for n in range(DC):
                        dve.wait_ge(mixb_hi_done, n + 1)
                        dve.tensor_tensor(mixb_lo[:, n, :], park[:, n, :], f(mixb_hi[:, n, :]),
                                          ALU.subtract).then_inc(mixb_lo_done, 1)
                elif op == "h" and d["l"] == 0:
                    h_columns(0)
                    for k in range(DC):
                        h_low(0, k)
                elif op == "h":
                    l = d["l"]
                    h_columns(l)
                    dve.wait_ge(stb_done, d["s"] + 1)
                    for k in range(DC + 1):
                        if k < DC:
                            dve.tensor_tensor(tmp[:, k % 2, :], x[:, k, :], bank[:, 6, :],
                                              ALU.mult).then_inc(h_t, 1)
                        if k >= 1:
                            h_low(l, k - 1)
                elif op == "ln":
                    l = d["l"]
                    if l == 1:
                        h_columns(1)
                    dve.wait_ge(stb_done, d["s"] + 1)
                    for k in range(DC + 1):
                        if k < DC:
                            link(dve.tensor_tensor(x[:, k, :], x[:, k, :], bank[:, 6, :], ALU.mult))
                            dve.tensor_tensor(x[:, k, :], x[:, k, :], bank[:, 5, :], ALU.subtract).then_inc(h_t, 1)
                        if k >= 1 and l == 1:
                            h_low(1, k - 1)
                elif op == "stat_cols":
                    statistics(d)
                elif op == "trig":
                    angles()
                elif op == "qkv_squares":
                    dve.wait_ge(chunk_taken, QC_CHUNK + 4)
                    dve.tensor_tensor(kv_sq[:, 0, :], qkv[:, 0, :], qkv[:, 0, :], ALU.mult)
                    link(dve.tensor_tensor(kv_sq[:, 1, :], qkv[:, 1, :], qkv[:, 1, :], ALU.mult))
                    dve.tensor_tensor(kv_sq[:, 0, :], kv_sq[:, 0, :], kv_sq[:, 1, :], ALU.add).then_inc(sq_done, 1)
                    dve.wait_ge(sq_done, 1)
                    dve.tensor_tensor(kv_sq[:, 1, :], qkv[:, 2, :], qkv[:, 2, :], ALU.mult).then_inc(sq_done, 1)
                    link(dve.tensor_scalar(q_gain[:], col("q_g", 0, 2), MLA_SCALE, None, ALU.mult))
                elif op == "q_norm":
                    dve.wait_ge(stb_done, d["s"] + 1)
                    for c in range(2):
                        dve.scalar_tensor_tensor(qkv[:, c, :], qkv[:, c, :], q_gain[:, c:c + 1], bank[:, 6, :],
                                                 ALU.mult, ALU.mult).then_inc(qk_val, 1)
                    for c in range(2):
                        dve.wait_ge(qk_hi, c + 1)
                        dve.tensor_tensor(qc_lo[:, c, :], qkv[:, c, :], f(qc_hi[:, c, :]),
                                          ALU.subtract).then_inc(qk_lo, 1)
                elif op == "kv_norm":
                    dve.wait_ge(stb_done, d["s"] + 1)
                    dve.wait_ge(trig_done, 2)
                    dve.scalar_tensor_tensor(kv_f[:], qkv[:, 2, :], col("kv_g"), bank[:, 6, :], ALU.mult,
                                             ALU.mult).then_inc(qk_val, 1)
                    dve.wait_ge(qk_hi, 3)
                    dve.tensor_tensor(kv_lo[:], kv_f[:], f(kv_hi[:]), ALU.subtract).then_inc(qk_lo, 1)
                elif op == "k_rope":
                    rope(qkv[:, 3, :], cos1[:], sin1[:], rope_t[:], rope_y[:], 32, qk_val, None)
                    dve.wait_ge(qk_hi, 4)
                    dve.tensor_tensor(kr_lo[:], rope_y[:], f(kr_hi[:]), ALU.subtract).then_inc(qk_lo, 1)
                elif op == "head":
                    head(d["h"])
                elif op == "att_scores" and d["u"] < SP_PAIRS:
                    s = SP_PAIRS * (d["l"] - 2) + d["u"]
                    dve.wait_ge(z_full, s + 1)
                    for i in range(1, 7):
                        if i <= 5:
                            dve.wait_ge(z_log, 5 * s + i)
                            dve.scalar_tensor_tensor(stage[:, (i - 1) % 3, :], bank[:, 1 + i, :], 0.0,
                                                     stage[:, (i - 1) % 3, :], ALU.max,
                                                     ALU.add).then_inc(sp_val, 1)
                        if i >= 2:
                            dve.wait_ge(sp_hi_done, 5 * s + i - 1)
                            dve.tensor_tensor(sp_lo[:, i - 2, :], stage[:, (i - 2) % 3, :],
                                              f(sp_hi[:, i - 2, :]), ALU.subtract).then_inc(sp_lo_done, 1)
                elif op == "att_scores":
                    r = RH * (d["l"] - 2) + d["u"] - SP_PAIRS
                    h = d["u"] - SP_PAIRS
                    dve.wait_ge(rs_full, r + 1)
                    if h >= 1:
                        dve.wait_ge(rc_full, r)
                        dve.wait_ge(stc_done, RET_STAT[r - 1] + 1)
                    for i in range(3):
                        for J in range(NB):
                            bk, c0 = RET_PLACE[J]
                            if bk == i:
                                w = slice(c0, c0 + (NB - J) * P)
                                ins = dve.tensor_tensor(stage[:, i, w], bank[:, 2 + i, w],
                                                        decay[:, h, 0:(NB - J) * P], ALU.mult)
                        ins.then_inc(rs_val, 1)
                    for i in range(3):
                        n = (S, S, 2 * P)[i]
                        dve.wait_ge(rs_hi_done, 3 * r + i + 1)
                        dve.tensor_tensor(sp_lo[:, i, 0:n], stage[:, i, 0:n], f(sp_hi[:, i, 0:n]),
                                          ALU.subtract).then_inc(rs_lo_done, 1)
                elif op == "att_mid" and d["u"] < SP_PAIRS:
                    s = SP_PAIRS * (d["l"] - 2) + d["u"]
                    for i in range(5):
                        dve.wait_ge(a_hi_done, 5 * s + i + 1)
                        dve.tensor_tensor(sp_lo[:, i, :], stage[:, i % 3, :], f(sp_hi[:, i, :]),
                                          ALU.subtract).then_inc(a_lo_done, 1)
                elif op == "att_out" and d["u"] < SP_PAIRS:
                    s = SP_PAIRS * (d["l"] - 2) + d["u"]
                    k = RH + d["u"]
                    dve.wait_ge(ao_full, s + 1)
                    dve.wait_ge(chunk_taken, AG_CHUNK[d["g"]] + 1)
                    dve.tensor_tensor(mixf[0:64, k, :], bank[0:64, 2, :], ag[0:64, d["g"] % 2, :], ALU.mult)
                    dve.tensor_tensor(mixf[64:P, k, :], bank[64:P, 3, :], ag[64:P, d["g"] % 2, :],
                                      ALU.mult).then_inc(mixf_done, 1)
                elif op == "ret_norm":
                    k = d["u"] - SP_PAIRS
                    g = 8 * (d["l"] - 2) + d["u"]
                    dve.wait_ge(stb_done, d["s"] + 1)
                    dve.wait_ge(chunk_taken, AG_CHUNK[g] + 1)
                    link(dve.tensor_tensor(mixf[:, k, :], bank[:, 6, :], ag[:, g % 2, :], ALU.mult))
                    dve.tensor_tensor(mixf[:, k, :], mixf[:, k, :], bank[:, 7, :], ALU.mult).then_inc(mixf_done, 1)
                elif op == "mix_split":
                    l = d["l"]
                    for i, k in enumerate(MIX_ORDER):
                        dve.wait_ge(m_hi_done, DC * (l - 2) + i + 1)
                        dve.tensor_tensor(h_lo[:, k, :], mixf[:, k, :], f(h_hi[:, k, :]),
                                          ALU.subtract).then_inc(m_lo_done, 1)
                elif op == "final":
                    dve.wait_ge(stb_done, d["s"] + 1)
                    for n in range(DC):
                        dve.scalar_tensor_tensor(outf[:, n, :], x[:, n, :], col("final_g", n), bank[:, 6, :],
                                                 ALU.mult, ALU.mult).then_inc(fin_done, 1)

        @block.gpsimd
        def _(pool):
            link = chain(pool, "pool")

            def cast(dst, src):
                return pool.tensor_scalar(dst, src, 1.0, None, ALU.mult)

            def sums(n, mean, last):
                if mean:
                    if n == 0:
                        link(pool.tensor_scalar(sum1[:], x[:, 0, :], 1.0, None, ALU.mult))
                    else:
                        link(pool.tensor_tensor(sum1[:], sum1[:], x[:, n, :], ALU.add))
                if n == 0:
                    link(pool.tensor_tensor(sum2[:], x[:, 0, :], x[:, 0, :], ALU.mult))
                else:
                    link(pool.tensor_tensor(sqr[:], x[:, n, :], x[:, n, :], ALU.mult))
                    ins = pool.tensor_tensor(sum2[:], sum2[:], sqr[:], ALU.add)
                    if n == DC - 1:
                        ins.then_inc(sums_done, 1)
                    else:
                        link(ins)

            def mask(i):
                for J in range(NB):
                    for bk, c0 in tri(J):
                        if bk == i:
                            v = stage[:, i % 3, c0:c0 + P]
                            link(pool.tensor_tensor(v, v, strict, ALU.mult))

            for d in steps:
                op = d["op"]
                if op == "chunk":
                    kind, C, l = d["kind"], d["C"], d.get("l", 0)
                    if "cast" in d:
                        if "val" in d:
                            pool.wait_ge(val_done, d["val"] + 1)
                        else:
                            pool.wait_ge(chunk_taken, C + 1)
                        t = tmp[:, d["m"] % 4, :]
                        if kind == "Z":
                            ins = cast(mixa_hi[:, d["n"], :], park[:, d["n"], :])
                        elif kind in ("AQ", "AK"):
                            u = d["u"]
                            wait_unit_scores(pool, d["g"] - 1)
                            src = rot_y[:] if u >= SP_PAIRS else t
                            if kind == "AK":
                                ins = cast(ak_hi[:], src)
                            elif u >= SP_PAIRS:
                                ins = cast(aq_hi[:, 0, :], src)
                            else:
                                for e in range(2):
                                    ins = pool.tensor_scalar(aq_hi[:, e, :], src, col("half", e), None, ALU.mult)
                        elif kind == "VT":
                            wait_unit_out(pool, d["g"] - 1)
                            ins = cast(av_hi[:].rearrange("p b r -> p (b r)"), t)
                        ins.then_inc(cast_done, 1)
                    if kind[:3] == "OUT":
                        pool.wait_ge(post_done, d["post"])
                        sums(d["n"], l < 2, None)
                elif op == "mixb_split":
                    pool.wait_ge(chunk_full, XB_LAST + 1)
                    for n in range(DC):
                        pool.wait_ge(post_done, post_of["Y", 0, n, 0])
                        cast(mixb_hi[:, n, :], park[:, n, :]).then_inc(mixb_hi_done, 1)
                elif op == "h" and d["l"] == 0:
                    pool.wait_ge(cols_done, 1)
                    pool.wait_ge(const_in, 48)
                    for k in range(DC):
                        if k >= 2:
                            pool.wait_ge(h_lo_done, k - 1)
                        pool.tensor_scalar(tmp[:, 2 + k % 2, :], x[:, k, :], h_scale[:, 0, k:k + 1],
                                           h_shift[:, 0, k:k + 1], ALU.mult, ALU.add).then_inc(h_v_done, 1)
                elif op == "h" or op == "ln":
                    l = d["l"]
                    if op == "ln" and l == 2:
                        for k in range(DC):
                            pool.wait_ge(x_new, DC + k + 1)
                            sums(k, False, None)
                        continue
                    pool.wait_ge(cols_done, l + 1)
                    for k in range(DC):
                        pool.wait_ge(h_t, T_BASE[op, l] + k + 1)
                        if k >= 2:
                            pool.wait_ge(h_lo_done, H_BASE[l] + k - 1)
                        t = x[:, k, :] if op == "ln" else tmp[:, k % 2, :]
                        pool.tensor_scalar(tmp[:, 2 + k % 2, :], t, h_scale[:, l, k:k + 1],
                                           h_shift[:, l, k:k + 1], ALU.mult, ALU.add).then_inc(h_v_done, 1)
                elif op == "q_norm":
                    for c in range(2):
                        pool.wait_ge(qk_val, c + 1)
                        cast(qc_hi[:, c, :], qkv[:, c, :]).then_inc(qk_hi, 1)
                elif op == "kv_norm":
                    pool.wait_ge(qk_val, 3)
                    cast(kv_hi[:], kv_f[:]).then_inc(qk_hi, 1)
                elif op == "k_rope":
                    pool.wait_ge(qk_val, 4)
                    cast(kr_hi[:], rope_y[:]).then_inc(qk_hi, 1)
                elif op == "head":
                    t = d["h"]
                    if 0 <= t - 2 < MH:
                        pool.wait_ge(o_taken, t - 1)
                        cast(mixc_hi[:, t - 2, :], sz[:, t - 2, :]).then_inc(mc_hi_done, 1)
                    if 0 <= t < MH:
                        for i in range(NB):
                            g = NB * t + i
                            pool.wait_ge(rsum_done, g + 1)
                            n = (i + 1) * P
                            pool.tensor_scalar(tmp[:, i, 0:n], tmp[:, i, 0:n], rsum[:, i:i + 1], None,
                                               ALU.mult).then_inc(p_done, 1)
                    if t + 1 < MH and (t + 1) % 2 == 0:
                        j = (t + 1) // 2
                        pool.wait_ge(qr_val, j + 1)
                        if t >= 0:
                            pool.wait_ge(sc_full, NB * (t + 1))
                        cast(qr_hi[:], rope_y[:]).then_inc(qr_hi_done, 1)
                elif op == "att_scores" and d["u"] < SP_PAIRS:
                    s = SP_PAIRS * (d["l"] - 2) + d["u"]
                    wait_unit_out(pool, d["g"] - 1)
                    for i in range(5):
                        pool.wait_ge(sp_val, 5 * s + i + 1)
                        mask(i)
                        cast(sp_hi[:, i, :], stage[:, i % 3, :]).then_inc(sp_hi_done, 1)
                elif op == "att_scores":
                    r = RH * (d["l"] - 2) + d["u"] - SP_PAIRS
                    wait_unit_out(pool, d["g"] - 1)
                    for i in range(3):
                        n = (S, S, 2 * P)[i]
                        pool.wait_ge(rs_val, 3 * r + i + 1)
                        cast(sp_hi[:, i, 0:n], stage[:, i, 0:n]).then_inc(rs_hi_done, 1)
                elif op == "att_mid" and d["u"] < SP_PAIRS:
                    s = SP_PAIRS * (d["l"] - 2) + d["u"]
                    for i in range(5):
                        pool.wait_ge(a_exp, 5 * s + i + 1)
                        cast(sp_hi[:, i, :], stage[:, i % 3, :]).then_inc(a_hi_done, 1)
                elif op == "mix_split":
                    l = d["l"]
                    pool.wait_ge(chunk_full, AG_CHUNK[8 * (l - 2) + 7] + 1)
                    for i, k in enumerate(MIX_ORDER):
                        pool.wait_ge(mixf_done, 8 * (l - 2) + i + 1)
                        cast(h_hi[:, k, :], mixf[:, k, :]).then_inc(m_hi_done, 1)


def kernel(x, c, positions, ada_w, ada_b, ln_g, ln_b, e_w_in, gmlp_norm_g, gmlp_norm_b, gmlp_ws, gmlp_bs,
           pool_w, pool_b, pool_scale, e_w_out, o_w_in, mla_q_norm_g, mla_kv_norm_g, mla_w_uq, mla_w_uk,
           mla_w_uv, o_w_out, c_2, norm_g_2, w_ada_2, b_ada_2, w_in_2, w_out_2, final_g_2):
    import concourse.bacc as bacc
    from concourse.bass_utils import run_bass_kernel_spmd as run

    A = np.asarray
    f32 = np.float32

    def rows(w):
        return A(w).reshape(-1, P, w.shape[-1]).transpose(1, 0, 2)

    tiles = []

    def add(t):
        t = t.reshape(P, -1)
        if t.shape[1] < TILE:
            t = np.concatenate([t, np.zeros((P, TILE - t.shape[1]), f32)], axis=1)
        tiles.append(t)

    w = rows(A(e_w_in)[0])
    for base in (D, 0, 2 * D, 4 * D, 3 * D):
        for i in range(4):
            add(w[:, :, base + i * HD:base + (i + 1) * HD])
    w = rows(A(e_w_out)[0])
    for n in range(DC):
        add(w[:, :, n * P:(n + 1) * P])
    w = rows(A(o_w_in)[0])
    add(w[:, :, 0:256])
    kr = w[:, :, 384:448]
    add(np.concatenate([w[:, :, 256:384], kr, kr], axis=2))
    for i in range(8):
        add(w[:, :, 448 + i * 256:448 + (i + 1) * 256])
    uq = rows(A(mla_w_uq)[0].reshape(256, MH * 192)).reshape(P, 2, MH, 192)
    uk = A(mla_w_uk)[0].transpose(2, 1, 0)
    uv = A(mla_w_uv)[0]
    for j in range(MH // 2):
        a, b = 2 * j, 2 * j + 1
        q = np.concatenate([uq[:, :, a, 0:P], uq[:, :, b, 0:P], uq[:, :, a, P:], uq[:, :, b, P:]], axis=2)
        add(np.concatenate([q.reshape(P, 768), uk[:, a], uk[:, b], uv[:, a], uv[:, b]], axis=1))
    w = rows(A(o_w_out)[0])
    for n in range(DC):
        add(w[:, :, n * P:(n + 1) * P])
    for l in range(2):
        w = rows(A(w_in_2)[l])
        for u in range(8):
            first, i = (4 * 512, u) if u < SP_PAIRS else (0, u - SP_PAIRS)
            q, k, v, g = (w[:, :, first + 512 * s + i * P:first + 512 * s + (i + 1) * P] for s in range(4))
            add(np.concatenate([q, k], axis=2))
            add(np.concatenate([v, g], axis=2))
        w = rows(A(w_out_2)[l])
        for n in range(4):
            add(w[:, :, n * 256:(n + 1) * 256])
    wt = np.stack(tiles)

    ada = np.concatenate([A(ada_w), A(w_ada_2)]).reshape(DEPTH, DC, P, 3, D).transpose(0, 3, 1, 2, 4)
    ada = np.ascontiguousarray(ada.reshape(DEPTH * 3 * DC, P, D))

    def col(v):
        return A(v).reshape(-1, P).T

    inv1 = (1.0 / (f32(10000.0) ** (np.arange(0, MLA_ROPE, 2, dtype=f32) / f32(MLA_ROPE)))).astype(f32)
    sign = np.tile(np.repeat(np.array([1.0, -1.0], f32), 32), 2)
    colst = np.concatenate([
        col(ada_b), col(b_ada_2), col(c), col(c_2), col(ln_g), col(ln_b), col(gmlp_norm_g), col(gmlp_norm_b),
        col(pool_b), col(pool_scale), col(mla_q_norm_g), col(mla_kv_norm_g), col(norm_g_2), col(final_g_2),
        np.tile(inv1, 4)[:, None], sign[:, None], np.full((P, 1), 1e-5, f32), np.full((P, 1), 1e-6, f32),
        np.repeat(np.eye(2, dtype=f32), 64, axis=0),
    ], axis=1)

    i = np.arange(P)
    edge = np.ones((P, 4, PAD), f32)
    for g, win in enumerate(WINDOWS):
        edge[:, g, 0:win] = (win / np.arange(1, win + 1)).astype(f32)
    matst = np.concatenate([
        np.eye(P), np.ones((P, P)), np.eye(P) - 1.0 / P, i[:, None] < i[None, :],
        edge.reshape(P, 4 * PAD)], axis=1).astype(f32)
    rmatst = np.concatenate([-1.0 * (i[:, None] >= i[None, :]), -np.ones((P, P)),
                             MASKED * (i[:, None] >= i[None, :]), np.eye(P)], axis=1).astype(f32)

    m, n = np.arange(P)[:, None], np.arange(S)[None, :]
    same = (m // 64) == (n // 64)
    power = np.where(same, np.abs(n - m), n - m)
    seen = (m // 64) <= (n // 64)
    logs = np.log1p(-(2.0 ** (-5.0 - np.arange(RH))))
    decayt = np.stack([np.where(seen, np.exp(np.where(seen, power, 0) * g), 0.0) * P ** -0.5 for g in logs],
                      axis=1).astype(f32)
    inv2 = (f32(10000.0) ** (-np.arange(64, dtype=f32) / f32(64))).astype(f32)
    angle = (inv2[:, None] * np.arange(S, dtype=f32)[None, :]).astype(np.float64)
    sn = np.sin(angle)
    rot = np.stack([np.concatenate([np.cos(angle)] * 2), np.concatenate([sn, -sn])]).astype(f32)

    arrays = {
        "wt": wt, "adat": ada, "colst": colst, "matst": matst, "rmatst": rmatst,
        "xt": A(x)[0].T.reshape(DC, P, S).transpose(1, 0, 2),
        "pos": A(positions)[0],
        "wst": A(gmlp_ws)[0].transpose(2, 0, 1),
        "bst": np.broadcast_to(A(gmlp_bs)[0][None], (P, GH, P)),
        "poolt": A(pool_w)[0].reshape(4, 2, P, HD).transpose(2, 0, 1, 3),
        "decayt": decayt, "rot": rot,
    }
    arrays = {k: np.ascontiguousarray(v) for k, v in arrays.items()}
    nc = bacc.Bacc("TRN2", target_bir_lowering=False, num_devices=1)
    args = [nc.dram_tensor(k, v.shape, mybir.dt.from_np(v.dtype), kind="ExternalInput").ap()
            for k, v in arrays.items()]
    out = nc.dram_tensor("out", (P, DC, S), F32, kind="ExternalOutput").ap()
    build(nc, *args, out)
    r = run(nc, [arrays], core_ids=[0])
    return r.results[0]["out"].transpose(1, 0, 2).reshape(D, S).T[None]
```

```python
from contextlib import ExitStack

import numpy as np

import concourse.bass as bass
from concourse import mybir

F32 = mybir.dt.float32
F32R = mybir.dt.float32r
I32 = mybir.dt.int32
ALU = mybir.AluOpType
ACT = mybir.ActivationFunctionType
AX = mybir.AxisListType

P = 128
D = 1024
S = 512
NB = S // P
DC = D // P
DEPTH = 4
HD = 256
GH = 4
WINDOWS = (2, 4, 8, 16)
PAD = 16
MH = 16
MLA_ROPE = 64
MLA_SCALE = (128 + 64) ** -0.5
ALPHA = (2.0 * 2) ** 0.25
RH = 4
SP_PAIRS = 4
TILE = 2048
HEAD_COLS = 1280
QUARTER = 512
SEC = 8
UNITS = 3 * DEPTH
MASKED = -1.0e30
INV_2PI = float(1.0 / (2.0 * np.pi))
HALF_PI = float(np.pi / 2)
PI_DOWN = 3.1415925
ROUND = 1.5 * 2.0 ** 23
TWO_PI_PARTS = (6.28125, 0.0019350051879882812, 3.0199159795e-07)

COL = {}
_n = 0
for _name, _k in (("ada_b", 8 * UNITS), ("c", 16), ("ln_g", 16), ("ln_b", 16), ("gmlp_g", 2), ("gmlp_b", 2),
                  ("pool_b", 8), ("pool_scale", 8), ("q_g", 2), ("kv_g", 1), ("norm_g", 16), ("final_g", 8),
                  ("inv", 2), ("eps", 2), ("half", 2)):
    COL[_name] = _n
    _n += _k
NCOL = _n

MAT = {}
_m = 0
for _name, _k in (("ident", P), ("ones", P), ("center", P), ("strict", P), ("edge", 4 * PAD)):
    MAT[_name] = _m
    _m += _k
NMAT = _m


def plan_steps():
    steps = []
    first_out1 = 20 + DC + 2 + 8 + MH // 2
    st = {"T": 0, "C": 0, "post": 0, "cast": 0, "val": 0, "m": 0, "stat": 0}
    tile_done = {}
    tmp_owner = {}
    redux_chunk = {}

    def begin(late_ada=False):
        T = st["T"]
        st["T"] += 1
        steps.append(dict(op="tile", T=T, late_ada=late_ada))
        return T

    def chunk(kind, T, tmp=True, post=True, cast=False, val=False, **kw):
        C = st["C"]
        st["C"] += 1
        d = dict(op="chunk", kind=kind, T=T, C=C, **kw)
        if tmp:
            d["m"] = st["m"]
            st["m"] += 1
        if val:
            d["val"] = st["val"]
            st["val"] += 1
        if cast:
            d["cast"] = st["cast"]
            st["cast"] += 1
        if post:
            st["post"] += 1
        d["post"] = st["post"] if post else None
        if tmp:
            tmp_owner[d["m"]] = st["post"]
        steps.append(d)
        if T is not None:
            tile_done[T] = ("chunk", C + 1)
        return d

    def stat(width, eps, mean, lhs, count_bank, banks):
        d = dict(stat=st["stat"], width=width, eps=eps, mean=mean, lhs=lhs, count_bank=count_bank, banks=banks)
        st["stat"] += 1
        steps.append(dict(op="stat_cols", **d))
        return d

    def redux(u):
        d = chunk("redux", None, tmp=False, post=True, u=u)
        redux_chunk[u] = d["C"]

    def after_tile(T):
        if T % 8 == 0 and T >= 8 and T // 8 + 1 < UNITS:
            redux(T // 8 + 1)
        if T == first_out1:
            redux(6)

    redux(0)
    redux(1)
    steps.append(dict(op="h", l=0))
    for h in range(GH):
        T = begin()
        chunk("V", T, h=h, c=0)
        chunk("V", T, h=h, c=1)
        if h == 0:
            steps.append(dict(op="spatial_rows"))
        else:
            steps.append(dict(op="spatial", h=h - 1))
        after_tile(T)
    for kind in ("U", "Z", "ZB"):
        for i in range(4):
            T = begin()
            for sub in range(2):
                d = chunk(kind, T, n=2 * i + sub, sub=sub, tmp=kind != "ZB", post=kind != "ZB",
                          cast=kind == "Z", val=kind == "Z")
            if kind == "U" and i == 0:
                steps.insert(len(steps) - 2, dict(op="spatial", h=GH - 1))
            after_tile(T)

    def pool_mm(g):
        for e in range(2):
            chunk("Y", None, g=g, e=e, n=2 * g + e)

    for g in range(4):
        T = begin()
        for sub in range(2):
            chunk("XB", T, n=2 * g + sub, g=g, sub=sub, tmp=False)
        if g >= 1:
            pool_mm(g - 1)
        after_tile(T)
    pool_mm(3)
    steps.append(dict(op="mixb_split"))
    for n in range(DC):
        T = begin()
        chunk("OUT0", T, n=n, l=0)
        after_tile(T)
    s = stat(D, 0, True, "sums", 7, (6, 5))
    steps.append(dict(op="stat_bcast", **s))
    steps.append(dict(op="ln", l=1, s=s["stat"]))
    T = begin()
    chunk("QC", T, n=0, sub=0, tmp=False, post=False)
    chunk("QC", T, n=1, sub=1, tmp=False, post=False)
    T = begin()
    chunk("QC", T, n=2, sub=0, tmp=False, post=False)
    chunk("QC", T, n=3, sub=1, tmp=False, post=False)
    steps.append(dict(op="qkv_squares"))
    after_tile(T)
    for i in range(8):
        T = begin()
        for sub in range(2):
            chunk("SZ", T, n=2 * i + sub, sub=sub, tmp=False, post=False)
        if i == 0:
            steps.append(dict(op="trig"))
            sq = stat(256, 0, False, "q2", 7, (6,))
        if i == 1:
            steps.append(dict(op="stat_bcast", **sq))
            steps.append(dict(op="q_norm", s=sq["stat"]))
        if i == 2:
            skv = stat(128, 0, False, "kv2", 7, (6,))
        if i == 3:
            steps.append(dict(op="stat_bcast", **skv))
            steps.append(dict(op="kv_norm", s=skv["stat"]))
        if i == 4:
            steps.append(dict(op="kv_transpose"))
        if i == 5:
            steps.append(dict(op="k_rope"))
        after_tile(T)
    first = st["T"]
    for h in range(-1, MH + 2):
        steps.append(dict(op="head", h=h))
    for j in range(MH // 2):
        tile_done[first + j] = ("head", 2 * j + 2)
    st["T"] += MH // 2
    for n in range(DC):
        T = begin()
        chunk("OUT1", T, n=n, l=1)
        after_tile(T)
    s = stat(D, 0, True, "sums", 7, (6, 5))
    steps.append(dict(op="stat_bcast", **s))
    steps.append(dict(op="ln", l=2, s=s["stat"]))
    for l in (2, 3):
        s = stat(D, 1, False, "stream" if l == 2 else "squares", 7, (6,))
        steps.append(dict(op="stat_bcast", **s))
        steps.append(dict(op="h", l=l, s=s["stat"]))
        base = 8 * (l - 2)
        norm = None
        for u in range(8):
            a = u - 1
            T = begin()
            if a >= 0:
                steps.append(dict(op="att_scores", l=l, u=a, g=base + a))
            for sub, kind in enumerate(("AQ", "AK")):
                chunk(kind, T, l=l, u=u, g=base + u, sub=sub, cast=True, val=u >= SP_PAIRS)
                if sub == 0 and 0 <= a < SP_PAIRS:
                    steps.append(dict(op="att_scores2", l=l, u=a, g=base + a))
                if sub == 0 and norm:
                    steps.append(dict(op="stat_bcast", **norm))
                    steps.append(dict(op="ret_norm", l=l, u=a - 1, s=norm["stat"]))
                    norm = None
            after_tile(T)
            T = begin()
            chunk("AV", T, l=l, u=u, g=base + u, sub=0, tmp=False, post=False)
            if a >= 0:
                steps.append(dict(op="att_mid", l=l, u=a, g=base + a))
            chunk("AG", T, l=l, u=u, g=base + u, sub=1, tmp=False, post=False)
            if a >= 0:
                steps.append(dict(op="att_out", l=l, u=a, g=base + a))
            if u == 7:
                steps.append(dict(op="mix_split", l=l, part=range(6)))
            chunk("VT", None, l=l, u=u, g=base + u, cast=True)
            after_tile(T)
            if a >= SP_PAIRS:
                norm = stat(P, 1, False, "ret2", 7, (7,))
        out_tile = st["T"]
        C = st["C"]

        def out_part(*part):
            steps.append(dict(op="out_part", l=l, T=out_tile, C=C, part=part))

        steps.append(dict(op="att_scores", l=l, u=7, g=base + 7))
        out_part(0, 1, 2, 3)
        steps.append(dict(op="stat_bcast", **norm))
        steps.append(dict(op="ret_norm", l=l, u=6, s=norm["stat"]))
        steps.append(dict(op="mix_split", l=l, part=(6,)))
        T = begin(late_ada=True)
        steps.append(dict(op="att_mid", l=l, u=7, g=base + 7))
        out_part(4)
        norm = stat(P, 1, False, "ret2", 7, (7,))
        out_part(5)
        steps.append(dict(op="stat_bcast", **norm))
        steps.append(dict(op="ret_norm", l=l, u=7, s=norm["stat"]))
        out_part(6)
        steps.append(dict(op="mix_split", l=l, part=(7,)))
        out_part(7)
        for i in range(4):
            if i > 0:
                T = begin()
            for sub in range(2):
                chunk("OUT%d" % l, T, n=2 * i + sub, l=l, sub=sub)
            after_tile(T)
    s = stat(D, 1, False, "squares", 7, (6,))
    steps.append(dict(op="stat_bcast", **s))
    steps.append(dict(op="final", s=s["stat"]))
    return steps, st, tile_done, tmp_owner, redux_chunk, first


def build(nc, wt, adat, colst, matst, rmatst, xt, pos, wst, bst, poolt, decayt, rot, out):
    steps, totals, tile_done, tmp_owner, redux_chunk, head_tile = plan_steps()
    NT = totals["T"]
    cols_of = {T: HEAD_COLS if head_tile <= T < head_tile + MH // 2 else TILE for T in range(NT)}

    with ExitStack() as ctx:
        def sem(name):
            return ctx.enter_context(nc.semaphore(name))

        at = [(nc.sbuf_base + 31) // 32 * 32]

        def place(name, shape, dt, offset=None):
            n = 4 * int(np.prod(shape[1:]))
            n = (n + 31) // 32 * 32
            if offset is None:
                offset = at[0]
                at[0] += n
            return nc.alloc_sbuf_tensor_at(name, shape, dt, offset=offset)

        cols = place("cols", [P, NCOL], F32)
        mats = place("mats", [P, NMAT], F32)
        rmats = place("rmats", [P, 4, P], F32R)
        neg_tri, neg_ones, unseen, ident_r = (rmats[:, i, :] for i in range(4))
        mod = place("mod", [P, 8 * UNITS], F32)
        red = place("red", [P, 2, 8], F32)
        cond = place("cond", [P, 16], F32)
        h_scale = place("h_scale", [P, DEPTH, DC], F32)
        h_shift = place("h_shift", [P, DEPTH, DC], F32)
        gate = place("gate", [P, 2, DC], F32)
        q_gain = place("q_gain", [P, 2], F32)
        st_mean = place("st_mean", [P, NB], F32)
        st_sq = place("st_sq", [P, NB], F32)
        st_var = place("st_var", [P, NB], F32)
        st_sd = place("st_sd", [P, NB], F32)
        st_r = place("st_r", [P, NB], F32)
        st_mr = place("st_mr", [P, NB], F32)
        v_stats = place("v_stats", [P, 2, 6], F32)
        v_mv = place("v_mv", [P, 2, 2], F32)
        v_sd = place("v_sd", [P, 2], F32)
        v_rs = place("v_rs", [P, 2], F32)
        neg_max = place("neg_max", [P, NB], F32)
        esum = place("esum", [P, NB], F32)
        rsum = place("rsum", [P, NB], F32)
        w_at = [at[0] + 4 * TILE * i for i in range(6)]
        w_raw = [place(f"w_raw{i}", [P, TILE], F32) for i in range(2)]
        w_hi = [place(f"w_hi{i}", [P, TILE], F32R) for i in range(2)]
        w_lo = [place(f"w_lo{i}", [P, TILE], F32R) for i in range(2)]
        ada_raw = place("ada_raw", [P, 2, D], F32)
        acc = place("acc", [P, 2, D], F32)
        x = place("x", [P, DC, S], F32)
        h_at = at[0]
        h_hi = place("h_hi", [P, DC, S], F32R)
        h_lo = place("h_lo", [P, DC, S], F32R)
        tmp_at = at[0]
        tmp = place("tmp", [P, 4, S], F32)
        s_at = at[0]
        sum1 = place("sum1", [P, S], F32)
        sum2 = place("sum2", [P, S], F32)
        sqr = place("sqr", [P, S], F32)
        area = at[0]
        KB = 1024

        ada_first = place("ada_first", [P, 16, D], F32, area)
        vn = place("vn", [P, 2, NB, HD], F32, area)
        pooled = place("pooled", [P, 2, 2, S], F32, area)
        park = place("park", [P, DC, S], F32, area + 8 * KB)
        mixa_hi = place("mixa_hi", [P, DC, S], F32R, area + 24 * KB)
        mixa_lo = place("mixa_lo", [P, DC, S], F32R, area + 40 * KB)
        poolw = place("poolw", [P, 4, 2, HD], F32, area + 56 * KB)
        ws = place("ws", [P, GH, P], F32, area + 64 * KB)
        bs = place("bs", [P, GH, P], F32, area + 66 * KB)
        rb = place("rb", [P, DC, P], F32, area + 68 * KB)
        padded = place("padded", [P, 4, PAD + S], F32, area + 64 * KB)
        rmats_raw = place("rmats_raw", [P, 4 * P], F32, area + 64 * KB + 4 * 4 * (PAD + S))
        mixb_hi = place("mixb_hi", [P, DC, S], F32R, h_at)
        mixb_lo = place("mixb_lo", [P, DC, S], F32R, h_at + 16 * KB)
        sz = place("sz", [P, MH, S], F32, area)
        mixc_lo = place("mixc_lo", [P, MH, S], F32R, area)
        mixc_hi = place("mixc_hi", [P, MH, S], F32R, h_at)
        b = area + 32 * KB
        qc_hi = place("qc_hi", [P, 2, S], F32R, b)
        qc_lo = place("qc_lo", [P, 2, S], F32R, b + 4 * KB)
        kv_hi = place("kv_hi", [P, S], F32R, b + 8 * KB)
        kv_lo = place("kv_lo", [P, S], F32R, b + 10 * KB)
        kv_tok = place("kv_tok", [P, NB, P], F32, b + 12 * KB)
        kr_hi = place("kr_hi", [P, S], F32R, b + 14 * KB)
        kr_lo = place("kr_lo", [P, S], F32R, b + 16 * KB)
        cos1 = place("cos1", [P, S], F32, b + 18 * KB)
        sin1 = place("sin1", [P, S], F32, b + 20 * KB)
        qn_hi = place("qn_hi", [P, S], F32R, b + 22 * KB)
        qn_lo = place("qn_lo", [P, S], F32R, b + 24 * KB)
        ql_hi = place("ql_hi", [P, S], F32R, b + 26 * KB)
        ql_lo = place("ql_lo", [P, S], F32R, b + 28 * KB)
        qr_hi = place("qr_hi", [P, S], F32R, b + 30 * KB)
        qr_lo = place("qr_lo", [P, S], F32R, b + 32 * KB)
        tail = [w_at[i] + 4 * 3 * QUARTER for i in range(6)]
        p_even = [place(f"p_even{i}", [P, (i + 1) * P], F32, o)
                  for i, o in enumerate((tail[3], tail[3] + 4 * P, tail[4], tail[2]))]
        p_odd = [place(f"p_odd{i}", [P, (i + 1) * P], F32, tmp_at + 4 * P * i * (i + 1) // 2) for i in range(NB)]
        ol_hi = place("ol_hi", [P, S], F32R, tail[5])
        ol_lo = place("ol_lo", [P, S], F32R, tmp_at + 4 * P * 10)
        pT = place("pT", [P, NB, S], F32, b + 34 * KB)
        qkv = place("qkv", [P, 4, S], F32, b + 34 * KB)
        kv_f = place("kv_f", [P, S], F32, b + 26 * KB)
        kv_sq = place("kv_sq", [P, 2, S], F32, b + 28 * KB)
        ang = place("ang", [P, 3, S], F32, b + 22 * KB)
        posi = place("posi", [P, S], I32, b + 32 * KB)
        rope_t = place("rope_t", [P, S], F32, s_at)
        rope_y = place("rope_y", [P, S], F32, s_at + 2 * KB)
        qr_f = place("qr_f", [P, S], F32, s_at + 4 * KB)
        decay = place("decay", [P, RH, S], F32, area)
        rot_c = place("rot_c", [P, S], F32, area + 8 * KB)
        rot_s = place("rot_s", [P, S], F32, area + 10 * KB)
        b = area + 12 * KB
        aq_hi = place("aq_hi", [P, 2, S], F32R, b)
        aq_lo = place("aq_lo", [P, 2, S], F32R, b + 4 * KB)
        ak_hi = place("ak_hi", [P, S], F32R, b + 8 * KB)
        ak_lo = place("ak_lo", [P, S], F32R, b + 10 * KB)
        av_hi = place("av_hi", [P, NB, P], F32R, b + 12 * KB)
        av_lo = place("av_lo", [P, NB, P], F32R, b + 14 * KB)
        v_raw = place("v_raw", [P, S], F32, b + 16 * KB)
        ag = place("ag", [P, 2, S], F32, b + 18 * KB)
        mixf = place("mixf", [P, DC, S], F32, b + 22 * KB)
        sp_hi = place("sp_hi", [P, 5, S], F32R, b + 38 * KB)
        sp_lo = place("sp_lo", [P, 5, S], F32R, b + 48 * KB)
        sp_f = place("sp_f", [P, 5, S], F32, b + 48 * KB)
        rot_t = place("rot_t", [P, S], F32, b + 58 * KB)
        rot_y = place("rot_y", [P, S], F32, b + 60 * KB)
        ret_sq = place("ret_sq", [P, S], F32, s_at)
        outf = place("outf", [P, DC, S], F32, h_at)

        bank = ctx.enter_context(nc.psum_tensor("bank", [P, 8, S], F32))

        ident = mats[:, MAT["ident"]:MAT["ident"] + P]
        ones = mats[:, MAT["ones"]:MAT["ones"] + P]
        center = mats[:, MAT["center"]:MAT["center"] + P]
        strict = mats[:, MAT["strict"]:MAT["strict"] + P]

        def col(name, i=0, n=1):
            return cols[:, COL[name] + i:COL[name] + i + n]

        def f(t):
            return t.bitcast(F32)

        cols_in = sem("cols_in")
        const_in = sem("const_in")
        x_landed = [sem(f"x_landed{i}") for i in range(4)]
        rmats_in = sem("rmats_in")
        layer0_in = sem("layer0_in")
        pool_in = sem("pool_in")
        decay_in = sem("decay_in")
        w_landed = [sem(f"w_landed{i}") for i in range(2)]
        w_hi_done = sem("w_hi_done")
        w_lo_done = sem("w_lo_done")
        ada_landed = [sem(f"ada_landed{i}") for i in range(2)]
        ada_first_landed = [sem(f"ada_first_landed{i}") for i in range(16)]
        ada_done = sem("ada_done")
        cond_done = sem("cond_done")
        masks_done = sem("masks_done")
        chunk_full = sem("chunk_full")
        chunk_taken = sem("chunk_taken")
        post_done = sem("post_done")
        val_done = sem("val_done")
        cast_done = sem("cast_done")
        cols_done = sem("cols_done")
        h_t = sem("h_t")
        h_hi_done = sem("h_hi_done")
        h_v_done = sem("h_v_done")
        h_lo_done = sem("h_lo_done")
        x_new = sem("x_new")
        sums_done = sem("sums_done")
        last_sq = sem("last_sq")
        x_sq = sem("x_sq")
        x_sq_used = sem("x_sq_used")
        stc_done = sem("stc_done")
        stv_done = sem("stv_done")
        sts_done = sem("sts_done")
        str_done = sem("str_done")
        stb_done = sem("stb_done")
        v_var_done = sem("v_var_done")
        v_sd_done = sem("v_sd_done")
        rows_full = sem("rows_full")
        rb_done = sem("rb_done")
        ws_done = sem("ws_done")
        sv_full = sem("sv_full")
        sv_taken = sem("sv_taken")
        pad_done = sem("pad_done")
        mixb_hi_done = sem("mixb_hi_done")
        mixb_lo_done = sem("mixb_lo_done")
        ang_done = sem("ang_done")
        trig_done = sem("trig_done")
        sq_done = sem("sq_done")
        qk_val = sem("qk_val")
        qk_hi = sem("qk_hi")
        qk_lo = sem("qk_lo")
        kvt_full = sem("kvt_full")
        kvt_taken = sem("kvt_taken")
        fin_done = sem("fin_done")
        out_done = sem("out_done")
        sc_full = sem("sc_full")
        max_done = sem("max_done")
        exp_done = sem("exp_done")
        rsum_done = sem("rsum_done")
        p_done = sem("p_done")
        t_full = sem("t_full")
        t_taken = sem("t_taken")
        pv_full = sem("pv_full")
        ol_hi_done = sem("ol_hi_done")
        ol_lo_done = sem("ol_lo_done")
        o_full = sem("o_full")
        o_taken = sem("o_taken")
        mc_hi_done = sem("mc_hi_done")
        mc_lo_done = sem("mc_lo_done")
        qn_full = sem("qn_full")
        qn_hi_done = sem("qn_hi_done")
        qn_lo_done = sem("qn_lo_done")
        ql_full = sem("ql_full")
        ql_hi_done = sem("ql_hi_done")
        ql_lo_done = sem("ql_lo_done")
        qr_full = sem("qr_full")
        qr_taken = sem("qr_taken")
        qr_cos = sem("qr_cos")
        qr_turned = sem("qr_turned")
        qr_val = sem("qr_val")
        qr_hi_done = sem("qr_hi_done")
        qr_lo_done = sem("qr_lo_done")
        z_full = sem("z_full")
        z_abs = sem("z_abs")
        z_log = sem("z_log")
        sp_val = sem("sp_val")
        sp_hi_done = sem("sp_hi_done")
        sp_lo_done = sem("sp_lo_done")
        cum_full = sem("cum_full")
        a_exp = sem("a_exp")
        a_hi_done = sem("a_hi_done")
        a_lo_done = sem("a_lo_done")
        ao_full = sem("ao_full")
        mixf_done = sem("mixf_done")
        rs_full = sem("rs_full")
        rs_val = sem("rs_val")
        rs_hi_done = sem("rs_hi_done")
        rs_lo_done = sem("rs_lo_done")
        ro_full = sem("ro_full")
        rsq_done = sem("rsq_done")
        m_hi_done = sem("m_hi_done")
        m_lo_done = sem("m_lo_done")
        in_order = {e: sem(f"{e}_in_order") for e in ("act", "dve", "pool")}

        block = ctx.enter_context(nc.Block())

        def tri(J):
            a = [(0, 0), (1, 0), (2, 0), (3, 0)]
            b = [(4, 0), (3, 128), (2, 256), (1, 384)]
            return a[J], b[J]

        TURN_PLACE = [(4, 0), (4, P), (5, 0), (4, 0)]
        RET_PLACE = [(0, 0), (1, 0), (2, 0), (1, 384)]

        def chain(eng, name):
            count = [0]

            def link(ins):
                count[0] += 1
                ins.then_inc(in_order[name], 1)
                eng.wait_ge(in_order[name], count[0])
            return link

        def wait_unit_scores(eng, g):
            if g >= 0:
                l, u = g // 8, g % 8
                if u < SP_PAIRS:
                    eng.wait_ge(z_full, SP_PAIRS * l + u + 1)
                else:
                    eng.wait_ge(rs_full, RH * l + u - SP_PAIRS + 1)

        def wait_unit_out(eng, g):
            if g >= 0:
                l, u = g // 8, g % 8
                if u < SP_PAIRS:
                    eng.wait_ge(ao_full, SP_PAIRS * l + u + 1)
                else:
                    eng.wait_ge(ro_full, RH * l + u - SP_PAIRS + 1)

        def wait_tile_done(eng, T):
            if T < 0:
                return
            kind, n = tile_done[T]
            eng.wait_ge(chunk_full if kind == "chunk" else o_full, n)

        def p_of(t, i):
            return (p_odd if t % 2 else p_even)[i][:]

        def splits_in(t):
            if t % 2 == 0 and t + 2 < MH:
                return head_tile + t // 2 + 1
            return head_tile + MH // 2 if t == MH - 1 else None

        def uv_at(j):
            return D + 2 * P * (j // 2 % 2)

        MIX_ORDER = [4, 5, 6, 7, 0, 1, 2, 3]
        H_T_BASE = {("ln", 1): 0, ("ln", 2): DC, ("h", 2): 2 * DC, ("h", 3): 3 * DC}
        RET_UNIT = [8 * (r // RH) + SP_PAIRS + r % RH for r in range(2 * RH)]
        HEAD_CHUNK = tile_done[head_tile - 1][1]
        stats = [d for d in steps if d["op"] == "stat_cols"]
        RET_INDEX = {d["stat"]: i for i, d in enumerate(d for d in stats if d["lhs"] == "ret2")}
        RET_STAT = {i: s for s, i in RET_INDEX.items()}
        STAT_SUMS = {d["stat"]: i + 1 for i, d in enumerate(d for d in stats if d["lhs"] in ("sums", "squares"))}
        LAST_OUT = {}
        for d in steps:
            if d["op"] == "chunk" and d["kind"][:3] == "OUT":
                last_out = d["post"]
            if d["op"] == "stat_cols" and d["lhs"] in ("sums", "squares"):
                LAST_OUT[d["stat"]] = last_out
        H_BASE = {0: 0, 1: DC, 2: 2 * DC, 3: 3 * DC}
        kinds = [d for d in steps if d["op"] == "chunk"]
        Y_CHUNK = {d["g"]: d["C"] for d in kinds if d["kind"] == "Y" and d["e"] == 1}
        AG_CHUNK = {d["g"]: d["C"] for d in kinds if d["kind"] == "AG"}
        PAIRED = {d["C"] for d in kinds if (d["kind"], d.get("h", d.get("n", d.get("u"))), d.get("c", 0))
                  in (("V", 0, 0), ("QC", 0, 0), ("AQ", 0, 0))}
        OUT1_FIRST = next(d for d in kinds if d["kind"] == "OUT1")
        OUT1_EARLY = 6
        QC_CHUNK = min(d["C"] for d in kinds if d["kind"] == "QC")
        XB_LAST = max(d["C"] for d in kinds if d["kind"] == "XB")
        POST_VT_BEFORE = {}
        before = None
        post_of = {}
        for d in steps:
            if d["op"] == "chunk" and d["kind"] == "AV":
                POST_VT_BEFORE[d["C"]] = before
            if d["op"] == "chunk" and d["kind"] == "VT":
                before = d["post"]
            if d["op"] == "chunk":
                key = (d["kind"], d.get("l", 0), d.get("n", d.get("u", d.get("h"))), d.get("c", 0))
                post_of[key] = d["post"]

        @block.sync
        def _(sp):
            sp.dma_start(cols[:], colst).then_inc(cols_in, 16)
            for i in range(2 * SEC):
                sp.dma_start(ada_first[:, i, :], adat[i]).then_inc(ada_first_landed[i], 16)
                if i == 0:
                    sp.dma_start(mats[:], matst).then_inc(const_in, 16)
            for i in range(4):
                if i == 1:
                    sp.dma_start(w_raw[0][:], wt[0]).then_inc(w_landed[0], 16)
                sp.dma_start(x[:, 2 * i:2 * i + 2, :], xt[:, 2 * i:2 * i + 2, :]).then_inc(x_landed[i], 16)
            sp.dma_start(w_raw[1][:], wt[1]).then_inc(w_landed[1], 16)
            sp.dma_start(ws[:], wst).then_inc(layer0_in, 16)
            sp.dma_start(bs[:], bst).then_inc(layer0_in, 16)
            sp.dma_start(rmats_raw[:], rmatst).then_inc(rmats_in, 16)
            for T in range(NT):
                if T >= 2:
                    sp.wait_ge(w_lo_done, T - 1)
                n = cols_of[T]
                if T >= 2:
                    sp.dma_start(w_raw[T % 2][:, 0:n], wt[T, :, 0:n]).then_inc(w_landed[T % 2], 16)
                q = T + 2 * SEC
                if q < SEC * UNITS:
                    if T >= 2:
                        sp.wait_ge(ada_done, q - 1)
                    sp.dma_start(ada_raw[:, T % 2, :], adat[q]).then_inc(ada_landed[T % 2], 16)
                if T == 4:
                    sp.wait_ge(ada_done, 2 * SEC)
                    sp.dma_start(poolw[:], poolt).then_inc(pool_in, 16)
                if T == 29:
                    sp.wait_ge(h_lo_done, 2 * DC)
                    sp.dma_start(posi[:], pos.partition_broadcast(P)).then_inc(layer0_in, 16)
                if T == head_tile + MH // 2 + DC + 1:
                    wait_tile_done(sp, T - 2)
                    sp.dma_start(decay[:], decayt).then_inc(decay_in, 16)
                    sp.dma_start(rot_c[:], rot[0]).then_inc(decay_in, 16)
                    sp.dma_start(rot_s[:], rot[1]).then_inc(decay_in, 16)
            for n in range(DC):
                sp.wait_ge(fin_done, n + 1)
                sp.dma_start(out[:, n, :], outf[:, n, :]).then_inc(out_done, 16)
            sp.wait_ge(out_done, 16 * DC)

        @block.tensor
        def _(pe):
            def mm3(dst, ah, al, bh, bl, start, stop):
                pe.matmul(dst, ah, bl, start=start, stop=False, skip_group_check=True)
                pe.matmul(dst, al, bh, start=False, stop=False, skip_group_check=True)
                return pe.matmul(dst, ah, bh, start=False, stop=stop, skip_group_check=True)

            h_seen = [0]

            def wait_h(l, k):
                if 8 * l + k + 1 > h_seen[0]:
                    h_seen[0] = 8 * l + k + 1
                    pe.wait_ge(h_lo_done, h_seen[0])

            layer = [0]

            def chunk_pair(d):
                kind, T, C = d["kind"], d["T"], d["C"]
                pe.wait_ge(chunk_taken, C)
                for k in range(DC):
                    wait_h(layer[0], k)
                    for c in range(2):
                        dst = bank[:, (C + c) % 2, :]
                        if kind == "V":
                            for i in range(2):
                                blk = slice((2 * c + i) * P, (2 * c + i + 1) * P)
                                w = slice(k * HD, (k + 1) * HD)
                                ins = mm3(dst[:, i * HD:(i + 1) * HD], h_hi[:, k, blk], h_lo[:, k, blk],
                                          w_hi[T % 2][:, w], w_lo[T % 2][:, w], i == 0 and k == 0, k == DC - 1)
                        else:
                            a = k * HD + c * P
                            ins = mm3(dst, w_hi[T % 2][:, a:a + P], w_lo[T % 2][:, a:a + P],
                                      h_hi[:, k, :], h_lo[:, k, :], k == 0, k == DC - 1)
                        if k == DC - 1:
                            ins.then_inc(chunk_full, 1)

            def out_chunk(d, ks):
                kind, T = d["kind"], d["T"]
                for k in ks:
                    w = slice(k * P, (k + 1) * P)
                    if kind == "OUT0":
                        if d["n"] == 0 and k == 0:
                            pe.wait_ge(post_done, post_of["Z", 0, DC - 1, 0])
                        if d["n"] == 0 and k >= DC:
                            pe.wait_ge(mixb_lo_done, k - DC + 1)
                        rh, rl = (mixa_hi, mixa_lo) if k < DC else (mixb_hi, mixb_lo)
                        rh, rl = rh[:, k % DC, :], rl[:, k % DC, :]
                    else:
                        if d["n"] == 0:
                            pe.wait_ge(mc_lo_done, k + 1)
                        rh, rl = mixc_hi[:, k, :], mixc_lo[:, k, :]
                    ins = mm3(bank[:, d["C"] % 2, :], w_hi[T % 2][:, w], w_lo[T % 2][:, w], rh, rl,
                              k == 0, k == 2 * DC - 1)
                return ins

            def out_part(d):
                T, C = d["T"], d["C"]
                for i in d["part"]:
                    k = MIX_ORDER[i]
                    if i == 0:
                        pe.wait_ge(w_lo_done, T + 1)
                        pe.wait_ge(chunk_taken, C)
                    pe.wait_ge(m_lo_done, DC * (d["l"] - 2) + i + 1)
                    for c in range(2):
                        a = k * HD + c * P
                        ins = mm3(bank[:, (C + c) % 2, :], w_hi[T % 2][:, a:a + P], w_lo[T % 2][:, a:a + P],
                                  h_hi[:, k, :], h_lo[:, k, :], i == 0, i == DC - 1)
                        if i == DC - 1:
                            ins.then_inc(chunk_full, 1)

            def chunk(d):
                kind, T, C = d["kind"], d["T"], d["C"]
                if C in PAIRED:
                    return chunk_pair(d)
                if C - 1 in PAIRED or kind in ("OUT2", "OUT3") and d["n"] < 2:
                    return
                if C >= 2:
                    pe.wait_ge(chunk_taken, C - 1)
                dst = bank[:, C % 2, :]
                if kind == "redux":
                    u = d["u"]
                    pe.wait_ge(ada_done, SEC * (u + 1))
                    if u == 0:
                        pe.wait_ge(const_in, 16)
                    for j in range(DC):
                        ins = pe.matmul(dst[:, j:j + 1], acc[:, u % 2, j * P:(j + 1) * P], ones[:, 0:1],
                                        start=True, stop=True)
                elif kind == "V":
                    for i in range(2):
                        blk = 2 * d["c"] + i
                        for k in range(DC):
                            wait_h(0, k)
                            w = slice(k * HD, (k + 1) * HD)
                            ins = mm3(dst[:, i * HD:(i + 1) * HD],
                                      h_hi[:, k, blk * P:(blk + 1) * P], h_lo[:, k, blk * P:(blk + 1) * P],
                                      w_hi[T % 2][:, w], w_lo[T % 2][:, w], i == 0 and k == 0, k == DC - 1)
                elif kind == "Y":
                    g, e = d["g"], d["e"]
                    if g == 0 and e == 0:
                        pe.wait_ge(pool_in, 16)
                    pe.wait_ge(post_done, post_of["XB", 0, 2 * g + 1, 0])
                    for k in range(2):
                        ins = pe.matmul(dst, poolw[:, g, k, e * P:(e + 1) * P], pooled[:, g % 2, k, :],
                                        start=k == 0, stop=k == 1)
                elif kind in ("OUT0", "OUT1"):
                    first = OUT1_EARLY if kind == "OUT1" and d["n"] == 0 else 0
                    ins = out_chunk(d, range(first, 2 * DC))
                elif kind == "VT":
                    pe.wait_ge(chunk_taken, C - 1)
                    for b in range(NB):
                        o, v = dst[:, b * P:(b + 1) * P], v_raw[:, b * P:(b + 1) * P]
                        if d["u"] < SP_PAIRS:
                            ins = pe.transpose(o, v, ident)
                        else:
                            ins = pe.matmul(o, v, center, start=True, stop=True)
                else:
                    order = MIX_ORDER if kind in ("OUT2", "OUT3") else range(DC)
                    for i, k in enumerate(order):
                        if kind not in ("OUT2", "OUT3"):
                            wait_h(layer[0], k)
                        a = k * HD + d["sub"] * P
                        ins = mm3(dst, w_hi[T % 2][:, a:a + P], w_lo[T % 2][:, a:a + P],
                                  h_hi[:, k, :], h_lo[:, k, :], i == 0, i == DC - 1)
                ins.then_inc(chunk_full, 1)

            def head_qr(t):
                T = head_tile + t // 2
                pe.wait_ge(w_lo_done, T + 1)
                if t == 0:
                    pe.wait_ge(qk_lo, 4)
                else:
                    pe.wait_ge(ql_lo_done, t)
                for k in range(2):
                    w = slice(k * 384 + 2 * P, k * 384 + 3 * P)
                    ins = mm3(bank[:, 7, :], w_hi[T % 2][:, w], w_lo[T % 2][:, w],
                              qc_hi[:, k, :], qc_lo[:, k, :], k == 0, k == 1)
                ins.then_inc(qr_full, 1)

            def head_q(t):
                j, e = t // 2, t % 2
                T = head_tile + j
                if e == 0:
                    pe.wait_ge(qr_taken, j + 1)
                else:
                    pe.wait_ge(ql_lo_done, t)
                for k in range(2):
                    w = slice(k * 384 + e * P, k * 384 + (e + 1) * P)
                    ins = mm3(bank[:, 7, :], w_hi[T % 2][:, w], w_lo[T % 2][:, w],
                              qc_hi[:, k, :], qc_lo[:, k, :], k == 0, k == 1)
                ins.then_inc(qn_full, 1)

            def head_ql(t):
                T, e = head_tile + t // 2, t % 2
                pe.wait_ge(qn_lo_done, t + 1)
                w = slice(768 + e * P, 768 + (e + 1) * P)
                mm3(bank[:, 7, :], w_hi[T % 2][:, w], w_lo[T % 2][:, w], qn_hi[:], qn_lo[:],
                    True, True).then_inc(ql_full, 1)

            def head_scores(t, i):
                e = t % 2
                r = slice(64 * e, 64 * e + 64)
                if i == 0:
                    pe.wait_ge(ql_lo_done, t + 1)
                    pe.wait_ge(qr_lo_done, t // 2 + 1)
                if t >= 1:
                    pe.wait_ge(exp_done, NB * (t - 1) + i + 1)
                n = (i + 1) * P
                q = slice(i * P, (i + 1) * P)
                mm3(bank[:, i, 0:n], ql_hi[:, q], ql_lo[:, q], kv_hi[:, 0:n], kv_lo[:, 0:n], True, False)
                mm3(bank[:, i, 0:n], qr_hi[r, q], qr_lo[r, q], kr_hi[r, 0:n], kr_lo[r, 0:n],
                    False, True).then_inc(sc_full, 1)

            def head_turn(t):
                for i in range(NB):
                    pe.wait_ge(p_done, NB * t + i + 1)
                    if i == 0 and t >= 1:
                        pe.wait_ge(t_taken, NB * t)
                    if i == NB - 1:
                        pe.wait_ge(t_taken, NB * t + 2)
                    bk, c0 = TURN_PLACE[i]
                    for kb in range(i + 1):
                        ins = pe.transpose(bank[:, bk, c0 + kb * P:c0 + (kb + 1) * P],
                                           p_of(t, i)[:, kb * P:(kb + 1) * P], ident)
                    ins.then_inc(t_full, 1)

            def head_pv(t):
                if t >= 1:
                    pe.wait_ge(o_taken, t)
                last = (NB - 1) * P
                pe.wait_ge(t_taken, NB * t + NB - 1)
                for kb in range(NB - 1):
                    pe.matmul(bank[:, 6, kb * P:last], kv_tok[:, kb, :], pT[:, kb, kb * P:last],
                              start=kb == 0, stop=False, skip_group_check=True)
                pe.wait_ge(t_taken, NB * (t + 1))
                for kb in range(NB):
                    ins = pe.matmul(bank[:, 6, last:S], kv_tok[:, kb, :], pT[:, kb, last:S],
                                    start=False, stop=kb == NB - 1, skip_group_check=True)
                ins.then_inc(pv_full, 1)

            def head_o(t):
                j, e = t // 2, t % 2
                T = head_tile + j
                pe.wait_ge(ol_lo_done, t + 1)
                w = slice(uv_at(j) + e * P, uv_at(j) + (e + 1) * P)
                mm3(bank[:, 6, :], w_hi[T % 2][:, w], w_lo[T % 2][:, w], ol_hi[:], ol_lo[:],
                    True, True).then_inc(o_full, 1)

            for d in steps:
                op = d["op"]
                if op == "tile":
                    pe.wait_ge(w_lo_done, d["T"] + 1)
                elif op == "chunk":
                    chunk(d)
                elif op == "h":
                    layer[0] = d["l"]
                elif op == "ln":
                    layer[0] = 1
                elif op == "spatial_rows":
                    pe.wait_ge(ws_done, 1)
                    pe.matmul(bank[:, 4, :], ones, ws[:].rearrange("p h t -> p (h t)"), start=True,
                              stop=True).then_inc(rows_full, 1)
                elif op == "spatial":
                    h = d["h"]
                    if h == 0:
                        pe.wait_ge(rb_done, DC)
                    pe.wait_ge(post_done, post_of["V", 0, h, 1])
                    for j in range(2):
                        if h >= 1:
                            pe.wait_ge(sv_taken, 2 * (h - 1) + j + 1)
                        for b in range(NB):
                            ins = pe.matmul(bank[:, 4 + j, b * P:(b + 1) * P], vn[:, h % 2, b, j * P:(j + 1) * P],
                                            ws[:, h, :], start=True, stop=True)
                        ins.then_inc(sv_full, 1)
                elif op == "out_part":
                    out_part(d)
                elif op == "stat_cols":
                    lhs, si = d["lhs"], d["stat"]
                    column = ones[:, 0:1]
                    blocks = [slice(b * P, (b + 1) * P) for b in range(NB)]
                    if lhs == "stream":
                        for k in range(DC):
                            pe.wait_ge(x_sq, k + 1)
                            for b in range(NB):
                                ins = pe.matmul(bank[:, 7, b:b + 1], (sum2, sqr)[k % 2][:, blocks[b]], column,
                                                start=k == b == 0, stop=k == DC - 1, skip_group_check=True)
                            if k < DC - 1:
                                ins.then_inc(x_sq_used, 1)
                    elif lhs in ("sums", "squares"):
                        pe.wait_ge(sums_done, STAT_SUMS[si])
                        for b in range(NB):
                            pe.matmul(bank[:, 7, b:b + 1], sum2[:, blocks[b]], column, start=b == 0, stop=False,
                                      skip_group_check=True)
                            if d["mean"]:
                                pe.matmul(bank[:, 7, NB + b:NB + b + 1], sum1[:, blocks[b]], column, start=False,
                                          stop=False, skip_group_check=True)
                        if d["mean"]:
                            pe.wait_ge(post_done, LAST_OUT[si])
                            for b in range(NB):
                                pe.matmul(bank[:, 7, NB + b:NB + b + 1], x[:, DC - 1, blocks[b]], column,
                                          start=False, stop=True, skip_group_check=True)
                        pe.wait_ge(last_sq, STAT_SUMS[si])
                        for b in range(NB):
                            ins = pe.matmul(bank[:, 7, b:b + 1], sqr[:, blocks[b]], column, start=False, stop=True,
                                            skip_group_check=True)
                    else:
                        if lhs in ("q2", "kv2"):
                            pe.wait_ge(sq_done, 1 if lhs == "q2" else 2)
                        else:
                            r = RET_INDEX[si]
                            pe.wait_ge(rsq_done, r + 1)
                            if r >= 1:
                                pe.wait_ge(mixf_done, RET_UNIT[r - 1] + 1)
                        src = {"q2": kv_sq[:, 0, :], "kv2": kv_sq[:, 1, :], "ret2": ret_sq[:]}[lhs]
                        for b in range(NB):
                            ins = pe.matmul(bank[:, 7, b:b + 1], src[:, blocks[b]], column, start=True, stop=True)
                    ins.then_inc(stc_done, 1)
                elif op == "stat_bcast":
                    pe.wait_ge(str_done, d["stat"] + 1)
                    for src, bk in zip((st_r, st_mr), d["banks"]):
                        for b in range(NB):
                            ins = pe.matmul(bank[:, bk, b * P:(b + 1) * P],
                                            src[:, b:b + 1].broadcast_to([P, P]), ident, start=True, stop=True)
                    ins.then_inc(stb_done, 1)
                elif op == "kv_transpose":
                    pe.wait_ge(qk_val, 3)
                    for b in range(NB):
                        ins = pe.transpose(bank[:, 4, b * P:(b + 1) * P], kv_f[:, b * P:(b + 1) * P], ident)
                    ins.then_inc(kvt_full, 1)
                elif op == "head":
                    t = d["h"]
                    if t == 0:
                        pe.wait_ge(kvt_taken, 1)
                        pe.wait_ge(chunk_taken, HEAD_CHUNK)
                    here, ahead = 0 <= t < MH, t + 1 < MH
                    if here:
                        head_scores(t, 0)
                    if ahead and t % 2 == 1 or t == -1:
                        head_qr(t + 1)
                    if here:
                        head_scores(t, 1)
                    if 0 <= t - 2 < MH:
                        head_o(t - 2)
                    if ahead:
                        head_q(t + 1)
                    if here:
                        head_scores(t, 2)
                        head_scores(t, 3)
                    if ahead:
                        head_ql(t + 1)
                    if 0 <= t - 1 < MH:
                        head_turn(t - 1)
                        if t == MH:
                            pe.wait_ge(w_lo_done, OUT1_FIRST["T"] + 1)
                            pe.wait_ge(exp_done, NB * MH)
                            out_chunk(OUT1_FIRST, range(2))
                        head_pv(t - 1)
                        if t == MH:
                            out_chunk(OUT1_FIRST, range(2, OUT1_EARLY))
                elif op == "att_scores":
                    g, u, l = d["g"], d["u"], d["l"]
                    if u == SP_PAIRS:
                        pe.wait_ge(mixf_done, g)
                    if u < SP_PAIRS:
                        s = SP_PAIRS * (l - 2) + u
                        pe.wait_ge(post_done, post_of["AK", l, u, 0])
                        started = set()
                        pe.wait_ge(masks_done, 1)
                        for e, J in sorted(((e, J) for e in range(2) for J in range(NB)),
                                           key=lambda p: tri(p[1])[p[0]][0] < 2):
                            bk, c0 = tri(J)[e]
                            if bk < 2 and u >= 1:
                                pe.wait_ge(mixf_done, g)
                            ins = mm3(bank[:, 2 + bk, c0:c0 + (NB - J) * P], ak_hi[:, J * P:(J + 1) * P],
                                      ak_lo[:, J * P:(J + 1) * P], aq_hi[:, e, J * P:S],
                                      aq_lo[:, e, J * P:S], bk not in started, False)
                            started.add(bk)
                            ins = pe.matmul(bank[:, 2 + bk, c0:c0 + P], ident_r, unseen,
                                            start=False, stop=False, skip_group_check=True)
                        ins.then_inc(z_full, 1)
                    else:
                        r = RH * (l - 2) + u - SP_PAIRS
                        pe.wait_ge(post_done, post_of["AK", l, u, 0])
                        for J in range(NB):
                            bk, c0 = RET_PLACE[J]
                            ins = mm3(bank[:, 2 + bk, c0:c0 + (NB - J) * P], ak_hi[:, J * P:(J + 1) * P],
                                      ak_lo[:, J * P:(J + 1) * P], aq_hi[:, 0, J * P:S], aq_lo[:, 0, J * P:S],
                                      J < 3, True)
                        ins.then_inc(rs_full, 1)
                elif op == "att_mid":
                    u, l = d["u"], d["l"]
                    if u < SP_PAIRS:
                        s = SP_PAIRS * (l - 2) + u
                        pe.wait_ge(sp_lo_done, 5 * (s + 1))
                        for e in range(2):
                            for J in range(NB):
                                bk, c0 = tri(J)[e]
                                for j in range(J, NB):
                                    bj, cj = tri(j)[e]
                                    lhs = neg_tri if j == J else neg_ones
                                    o = bank[:, 2 + bk, c0 + (j - J) * P:c0 + (NB - J) * P]
                                    for part in (sp_lo, sp_hi):
                                        ins = pe.matmul(o, lhs, part[:, bj, cj:cj + (NB - j) * P],
                                                        start=False, stop=False, skip_group_check=True)
                        ins.then_inc(cum_full, 1)
                    else:
                        r = RH * (l - 2) + u - SP_PAIRS
                        pe.wait_ge(rs_lo_done, 3 * (r + 1))
                        pe.wait_ge(post_done, post_of["VT", l, u, 0])
                        if r >= 2:
                            pe.wait_ge(mixf_done, RET_UNIT[r - 2] + 1)
                        for J in range(NB):
                            bk, c0 = RET_PLACE[J]
                            w = slice(c0, c0 + (NB - J) * P)
                            ins = mm3(bank[:, 5 + r % 2, J * P:S], av_hi[:, J, :], av_lo[:, J, :], sp_hi[:, bk, w],
                                      sp_lo[:, bk, w], J == 0, J == NB - 1)
                        ins.then_inc(ro_full, 1)
                elif op == "att_out":
                    u, l = d["u"], d["l"]
                    if u < SP_PAIRS:
                        s = SP_PAIRS * (l - 2) + u
                        pe.wait_ge(a_lo_done, 5 * (s + 1))
                        pe.wait_ge(post_done, post_of["VT", l, u, 0])
                        for e in range(2):
                            for J in range(NB):
                                bk, c0 = tri(J)[e]
                                w = slice(c0, c0 + (NB - J) * P)
                                ins = mm3(bank[:, 2 + e, J * P:S], av_hi[:, J, :], av_lo[:, J, :],
                                          sp_hi[:, bk, w], sp_lo[:, bk, w], J == 0, J == NB - 1)
                        ins.then_inc(ao_full, 1)

        @block.scalar
        def _(act):
            link = chain(act, "act")

            def split_tile(T):
                n = cols_of[T]
                act.wait_ge(w_landed[T % 2], 16 * (T // 2 + 1))
                j = T - head_tile
                if 2 <= j < MH // 2:
                    act.wait_ge(ql_full, 2 * (j - 1))
                    if j >= 4:
                        act.wait_ge(o_full, 2 * (j - 3))
                else:
                    wait_tile_done(act, T - 2)
                if n == TILE:
                    act.activation(w_hi[T % 2][:, 0:n], w_raw[T % 2][:, 0:n], ACT.Copy).then_inc(w_hi_done, 1)
                else:
                    u = uv_at(T - head_tile)
                    act.activation(w_hi[T % 2][:, u:u + 2 * P], w_raw[T % 2][:, D:D + 2 * P], ACT.Copy)
                    act.activation(w_hi[T % 2][:, 0:D], w_raw[T % 2][:, 0:D], ACT.Copy).then_inc(w_hi_done, 1)

            def chunk(d):
                kind, C, l = d["kind"], d["C"], d.get("l", 0)
                act.wait_ge(chunk_full, C + 1)
                if "m" in d:
                    if d["m"] >= 4:
                        act.wait_ge(post_done, tmp_owner[d["m"] - 4])
                    dst = tmp[:, d["m"] % 4, :]
                src = bank[:, C % 2, :]
                func, scale, bias = ACT.Copy, 1.0, 0.0
                if kind == "redux":
                    u = d["u"]
                    if u >= 2:
                        act.wait_ge(post_done, post_of["redux", 0, u - 2, 0])
                    dst, src = red[:, u % 2, :], src[:, 0:8]
                elif kind == "Z":
                    func = ACT.Silu
                elif kind == "ZB":
                    act.wait_ge(post_done, post_of["Z", 0, d["n"], 0])
                    func, dst = ACT.Silu, park[:, d["n"], :]
                elif kind == "XB":
                    if d["n"] >= 2:
                        act.wait_ge(post_done, post_of["XB", 0, d["n"] - 2, 0])
                    else:
                        act.wait_ge(pad_done, 4)
                    dst = padded[:, d["n"] % 2, PAD:PAD + S]
                elif kind == "Y":
                    func, bias = ACT.Identity, col("pool_b", d["n"])
                elif kind in ("OUT0", "OUT1"):
                    scale = gate[:, l, d["n"]:d["n"] + 1]
                elif kind in ("OUT2", "OUT3"):
                    scale = mod[:, 8 * (3 * l + 2) + d["n"]:8 * (3 * l + 2) + d["n"] + 1]
                elif kind == "QC":
                    dst = qkv[:, d["n"], :]
                elif kind == "SZ":
                    func, dst = ACT.Silu, sz[:, d["n"], :]
                elif kind == "AQ" and d["u"] < SP_PAIRS:
                    scale = 0.125
                elif kind == "AV":
                    if d["g"] >= 1:
                        act.wait_ge(post_done, POST_VT_BEFORE[d["C"]])
                    dst = v_raw[:]
                elif kind == "AG":
                    g = d["g"]
                    if g >= 2:
                        act.wait_ge(mixf_done, g - 1)
                    func, dst = ACT.Silu, ag[:, g % 2, :]
                if kind[:3] == "OUT" and d["n"] == 0:
                    act.wait_ge(post_done, post_of["redux", 0, 3 * l + 2, 0])
                act.activation(dst, src, func, scale=scale, bias=bias).then_inc(chunk_taken, 1)
                if kind in ("AQ", "AK", "VT") and d["u"] < SP_PAIRS:
                    act.wait_ge(chunk_taken, C + 1)
                    if kind == "VT":
                        wait_unit_out(act, d["g"] - 1)
                        ins = act.activation(av_hi[:].rearrange("p b r -> p (b r)"), dst, ACT.Copy)
                    elif kind == "AK":
                        wait_unit_scores(act, d["g"] - 1)
                        ins = act.activation(ak_hi[:], dst, ACT.Copy)
                    else:
                        wait_unit_scores(act, d["g"] - 1)
                        for e in range(2):
                            ins = act.activation(aq_hi[:, e, :], dst, ACT.Copy, scale=col("half", e))
                    ins.then_inc(cast_done, 1)

            act.wait_ge(cols_in, 16)
            act.activation(cond[:], col("c", 0, 16), ACT.Silu).then_inc(cond_done, 1)
            v_count = 0
            for d in steps:
                op = d["op"]
                if op == "tile":
                    T = d["T"] + 1
                    if T < NT:
                        split_tile(T)
                elif op == "chunk":
                    chunk(d)
                    if d["kind"] == "redux" and d["u"] == 0:
                        split_tile(0)
                    if d["kind"] == "V":
                        v_count += 1
                        act.wait_ge(v_var_done, v_count)
                        act.activation(v_sd[:], v_mv[:, :, 1], ACT.Sqrt, bias=col("eps", 0)).then_inc(v_sd_done, 1)
                elif op == "stat_cols":
                    if d["lhs"] in ("sums", "squares"):
                        act.wait_ge(post_done, LAST_OUT[d["stat"]])
                        act.wait_ge(sums_done, STAT_SUMS[d["stat"]])
                        act.activation(sqr[:], x[:, DC - 1, :], ACT.Square).then_inc(last_sq, 1)
                    act.wait_ge(stv_done, d["stat"] + 1)
                    act.activation(st_sd[:], st_var[:], ACT.Sqrt,
                                   bias=col("eps", d["eps"])).then_inc(sts_done, 1)
                elif op == "h" and d["l"] == 0:
                    act.wait_ge(cols_done, 1)
                    for k in range(DC):
                        act.wait_ge(x_landed[k // 2], 16)
                        act.activation(h_hi[:, k, :], x[:, k, :], ACT.Identity, scale=h_scale[:, 0, k:k + 1],
                                       bias=h_shift[:, 0, k:k + 1]).then_inc(h_hi_done, 1)
                    act.wait_ge(rmats_in, 16)
                    act.activation(rmats[:].rearrange("p a b -> p (a b)"), rmats_raw[:],
                                   ACT.Copy).then_inc(masks_done, 1)
                elif op == "ln" or op == "h":
                    l = d["l"]
                    first = H_T_BASE[op, l]
                    if op == "h" or l == 1:
                        act.wait_ge(cols_done, l + 1)
                    for k in range(DC):
                        act.wait_ge(h_t, first + k + 1)
                        t = x[:, k, :] if op == "ln" else tmp[:, k % 2, :]
                        if op == "h" or l == 1:
                            act.activation(h_hi[:, k, :], t, ACT.Identity, scale=h_scale[:, l, k:k + 1],
                                           bias=h_shift[:, l, k:k + 1]).then_inc(h_hi_done, 1)
                        if op == "ln":
                            g = DC * (l - 1) + k
                            if l == 1:
                                act.wait_ge(h_v_done, DC + k + 1)
                                act.wait_ge(h_hi_done, DC + k + 1)
                            act.activation(x[:, k, :], x[:, k, :], ACT.Identity, scale=col("ln_g", g),
                                           bias=col("ln_b", g)).then_inc(x_new, 1)
                            if l == 2:
                                act.wait_ge(x_new, g + 1)
                                if k >= 2:
                                    act.wait_ge(x_sq_used, k - 1)
                                act.activation((sum2, sqr)[k % 2][:], x[:, k, :], ACT.Square).then_inc(x_sq, 1)
                elif op == "trig":
                    act.wait_ge(ang_done, 1)
                    act.activation(sin1[:], ang[:, 1, :], ACT.Sin, scale=col("inv", 1)).then_inc(trig_done, 1)
                    act.wait_ge(ang_done, 2)
                    act.activation(cos1[:], ang[:, 2, :], ACT.Sin).then_inc(trig_done, 1)
                elif op == "kv_transpose":
                    act.wait_ge(kvt_full, 1)
                    act.activation(kv_tok[:].rearrange("p b r -> p (b r)"), bank[:, 4, :],
                                   ACT.Copy).then_inc(kvt_taken, 1)
                elif op == "head":
                    t = d["h"]
                    here, ahead = 0 <= t < MH, t + 1 < MH

                    def exp(i):
                        g = NB * t + i
                        act.wait_ge(max_done, g + 1)
                        if t >= 1:
                            act.wait_ge(rsum_done, g - 3)
                        if t >= 2:
                            act.wait_ge(t_full, NB * (t - 2) + i + 1)
                        act.activation(p_of(t, i), bank[:, i, 0:(i + 1) * P], ACT.Exp, bias=neg_max[:, i:i + 1],
                                       accum_out=esum[:, i:i + 1]).then_inc(exp_done, 1)

                    def copy_turned(i):
                        g = NB * (t - 1) + i
                        bk, c0 = TURN_PLACE[i]
                        act.wait_ge(t_full, max(g + 1, NB * (t - 1) + 2))
                        if i == 0 and t >= 2:
                            act.wait_ge(pv_full, t - 1)
                        act.activation(pT[:, 0:i + 1, i * P:(i + 1) * P],
                                       bank[:, bk, c0:c0 + (i + 1) * P].rearrange("p (a b) -> p a b", b=P),
                                       ACT.Copy).then_inc(t_taken, 1)

                    if here:
                        exp(0)
                    if ahead and t % 2 == 1 or t == -1:
                        j = (t + 1) // 2
                        act.wait_ge(qr_full, j + 1)
                        if j >= 1:
                            act.wait_ge(qr_turned, 4 * j)
                            act.wait_ge(qr_cos, j)
                        act.activation(qr_f[:], bank[:, 7, :], ACT.Copy).then_inc(qr_taken, 1)
                    if here:
                        exp(1)
                    if ahead:
                        act.wait_ge(qn_full, t + 2)
                        if t >= 0:
                            act.wait_ge(ql_full, t + 1)
                        act.activation(qn_hi[:], bank[:, 7, :], ACT.Copy).then_inc(qn_hi_done, 1)
                    if t < MH - 1 and splits_in(t) is not None:
                        split_tile(splits_in(t))
                    if here:
                        exp(2)
                    if ahead:
                        act.wait_ge(ql_full, t + 2)
                        if t >= 0:
                            act.wait_ge(sc_full, NB * (t + 1))
                        act.activation(ql_hi[:], bank[:, 7, :], ACT.Copy).then_inc(ql_hi_done, 1)
                    if 0 <= t - 1 < MH:
                        copy_turned(0)
                        copy_turned(1)
                    if here:
                        exp(3)
                    if 0 <= t - 1 < MH:
                        copy_turned(2)
                        copy_turned(3)
                    if ahead and t % 2 == 1 or t == -1:
                        act.wait_ge(qr_val, (t + 1) // 2 + 1)
                        act.activation(qr_hi[:], rope_y[:], ACT.Copy).then_inc(qr_hi_done, 1)
                    if 0 <= t - 1 < MH:
                        act.wait_ge(pv_full, t)
                        if t >= 2:
                            act.wait_ge(o_full, t - 1)
                        act.activation(ol_hi[:], bank[:, 6, :], ACT.Copy).then_inc(ol_hi_done, 1)
                    if t == MH - 1:
                        split_tile(splits_in(t))
                elif op in ("att_scores", "att_scores2") and d["u"] < SP_PAIRS:
                    s = SP_PAIRS * (d["l"] - 2) + d["u"]
                    if op == "att_scores":
                        nc.scalar.preload_act_table_set("natural_log_exp_and_others")
                    for i in range(3) if op == "att_scores" else range(3, 6):
                        if i < 5:
                            if i in (1, 3):
                                act.wait_ge(z_abs, 2 * s + i // 2 + 1)
                            else:
                                act.wait_ge(z_full, s + 1)
                                link(act.activation(sp_f[:, i, :], bank[:, 2 + i, :], ACT.Abs))
                            link(act.activation(sp_f[:, i, :], sp_f[:, i, :], ACT.Exp, scale=-1.0))
                            act.activation(sp_f[:, i, :], sp_f[:, i, :], ACT.Ln,
                                           bias=1.0).then_inc(z_log, 1)
                        if i >= 1:
                            act.wait_ge(sp_val, 5 * s + i)
                            act.activation(sp_hi[:, i - 1, :], sp_f[:, i - 1, :],
                                           ACT.Copy).then_inc(sp_hi_done, 1)
                elif op == "att_scores":
                    r = RH * (d["l"] - 2) + d["u"] - SP_PAIRS
                    for i in range(3):
                        n = (S, S, 2 * P)[i]
                        act.wait_ge(rs_val, 3 * r + i + 1)
                        act.activation(sp_hi[:, i, 0:n], sp_f[:, i, 0:n], ACT.Copy).then_inc(rs_hi_done, 1)
                elif op == "mix_split":
                    l = d["l"]
                    act.wait_ge(chunk_full, AG_CHUNK[8 * (l - 2) + 7] + 1)
                    for i in d["part"]:
                        k = MIX_ORDER[i]
                        act.wait_ge(mixf_done, 8 * (l - 2) + i + 1)
                        act.activation(h_hi[:, k, :], mixf[:, k, :], ACT.Copy).then_inc(m_hi_done, 1)
                elif op == "att_mid":
                    u, l = d["u"], d["l"]
                    if u < SP_PAIRS:
                        s = SP_PAIRS * (l - 2) + u
                        act.wait_ge(cum_full, s + 1)
                        for i in range(5):
                            act.activation(sp_f[:, i, :], bank[:, 2 + i, :], ACT.Exp).then_inc(a_exp, 1)
                            act.activation(sp_hi[:, i, :], bank[:, 2 + i, :], ACT.Exp).then_inc(a_hi_done, 1)
                    else:
                        r = RH * (l - 2) + u - SP_PAIRS
                        act.wait_ge(ro_full, r + 1)
                        if r >= 1:
                            act.wait_ge(stc_done, RET_STAT[r - 1] + 1)
                        act.activation(ret_sq[:], bank[:, 5 + r % 2, :], ACT.Square).then_inc(rsq_done, 1)

        @block.vector
        def _(dve):
            link = chain(dve, "dve")

            def split_tile(T):
                n = cols_of[T]
                dve.wait_ge(w_hi_done, T + 1)
                if n == TILE:
                    dve.tensor_tensor(w_lo[T % 2][:, 0:n], w_raw[T % 2][:, 0:n], f(w_hi[T % 2][:, 0:n]),
                                      ALU.subtract).then_inc(w_lo_done, 1)
                else:
                    u = uv_at(T - head_tile)
                    dve.tensor_tensor(w_lo[T % 2][:, u:u + 2 * P], w_raw[T % 2][:, D:D + 2 * P],
                                      f(w_hi[T % 2][:, u:u + 2 * P]), ALU.subtract)
                    dve.tensor_tensor(w_lo[T % 2][:, 0:D], w_raw[T % 2][:, 0:D], f(w_hi[T % 2][:, 0:D]),
                                      ALU.subtract).then_inc(w_lo_done, 1)

            def ada_piece(q):
                u, k = q // SEC, q % SEC
                if q >= SEC * UNITS:
                    return
                if q < 2 * SEC:
                    dve.wait_ge(ada_first_landed[q], 16)
                    src = ada_first[:, q, :]
                else:
                    i = q - 2 * SEC
                    dve.wait_ge(ada_landed[i % 2], 16 * (i // 2 + 1))
                    src = ada_raw[:, i % 2, :]
                c = cond[:, 8 * (u // 6) + k:8 * (u // 6) + k + 1]
                if k == 0:
                    if u >= 2:
                        dve.wait_ge(chunk_full, redux_chunk[u - 2] + 1)
                    dve.tensor_scalar(acc[:, u % 2, :], src, c, None, ALU.mult).then_inc(ada_done, 1)
                else:
                    dve.wait_ge(ada_done, q)
                    dve.scalar_tensor_tensor(acc[:, u % 2, :], src, c, acc[:, u % 2, :], ALU.mult,
                                             ALU.add).then_inc(ada_done, 1)

            def rope(src, ct, sn, turned, res, half, signal):
                for a in range(0, P, 2 * half):
                    x1, x2 = slice(a, a + half), slice(a + half, a + 2 * half)
                    dve.tensor_tensor(turned[x1, :], src[x2, :], sn[x2, :], ALU.mult)
                    ins = dve.tensor_tensor(turned[x2, :], src[x1, :], sn[x1, :], ALU.mult)
                link(ins)
                link(dve.tensor_tensor(res, src, ct, ALU.mult))
                dve.tensor_tensor(res, res, turned, ALU.add).then_inc(signal, 1)

            def chunk(d):
                kind, C, l, n = d["kind"], d["C"], d.get("l", 0), d.get("n")
                if d["post"] is None:
                    return
                dve.wait_ge(chunk_taken, C + 1)
                if d["post"] >= 2:
                    dve.wait_ge(post_done, d["post"] - 1)
                t = tmp[:, d["m"] % 4, :] if "m" in d else None
                if kind == "redux":
                    u = d["u"]
                    m = mod[:, 8 * u:8 * u + 8]
                    ins = dve.tensor_tensor(m, red[:, u % 2, :], col("ada_b", 8 * u, 8), ALU.add)
                    if u % 3 == 2 and u < 6:
                        link(ins)
                        ins = dve.tensor_scalar(gate[:, u // 3, :], m, 1.0, None, ALU.add)
                elif kind == "V":
                    h, c = d["h"], d["c"]
                    for i in range(2):
                        ins = dve.bn_stats(v_stats[:, i, :], t[:, i * HD:(i + 1) * HD])
                    link(ins)
                    for i in range(2):
                        ins = dve.bn_aggr(v_mv[:, i, :], v_stats[:, i, :])
                    ins.then_inc(v_var_done, 1)
                    count = 2 * h + c + 1
                    dve.wait_ge(v_sd_done, count)
                    link(dve.reciprocal(v_rs[:], v_sd[:]))
                    if h >= 2:
                        dve.wait_ge(sv_full, 2 * (h - 1))
                    for i in range(2):
                        ins = dve.tensor_scalar(vn[:, h % 2, 2 * c + i, :], t[:, i * HD:(i + 1) * HD],
                                                v_mv[:, i, 0:1], v_rs[:, i:i + 1], ALU.subtract, ALU.mult)
                elif kind == "U":
                    dve.wait_ge(sv_taken, n + 1)
                    ins = dve.tensor_tensor(park[:, n, :], park[:, n, :], t, ALU.mult)
                elif kind == "Z":
                    dve.wait_ge(post_done, post_of["U", 0, n, 0])
                    dve.tensor_tensor(park[:, n, :], park[:, n, :], t, ALU.mult).then_inc(val_done, 1)
                    dve.wait_ge(cast_done, d["cast"] + 1)
                    ins = dve.tensor_tensor(mixa_lo[:, n, :], park[:, n, :], f(mixa_hi[:, n, :]), ALU.subtract)
                elif kind == "XB":
                    g = d["g"]
                    win = WINDOWS[g]
                    src = padded[:, n % 2, :]
                    cur, step = src, 1
                    for i in range(g + 1):
                        nxt = padded[:, 2 + i % 2, :]
                        link(dve.tensor_tensor(nxt[:, PAD:], cur[:, PAD:], cur[:, PAD - step:PAD + S - step],
                                               ALU.add))
                        cur, step = nxt, 2 * step
                    edge = mats[:, MAT["edge"] + g * PAD:MAT["edge"] + g * PAD + win]
                    link(dve.tensor_tensor(cur[:, PAD:PAD + win], cur[:, PAD:PAD + win], edge, ALU.mult))
                    if g == 0:
                        dve.wait_ge(sv_full, 2 * GH)
                    if g >= 2:
                        dve.wait_ge(chunk_full, Y_CHUNK[g - 2] + 1)
                    ins = dve.scalar_tensor_tensor(pooled[:, g % 2, n % 2, :], cur[:, PAD:], 1.0 / win,
                                                   src[:, PAD:], ALU.mult, ALU.subtract)
                elif kind == "Y":
                    ins = dve.scalar_tensor_tensor(park[:, n, :], t, col("pool_scale", n), park[:, n, :],
                                                   ALU.mult, ALU.mult)
                elif kind in ("OUT0", "OUT1"):
                    if n == 0 and l == 1:
                        dve.wait_ge(x_new, DC)
                    ins = dve.scalar_tensor_tensor(x[:, n, :], x[:, n, :], ALPHA, t, ALU.mult, ALU.add)
                elif kind in ("OUT2", "OUT3"):
                    if n == 0:
                        dve.wait_ge(x_new, 2 * DC)
                    ins = dve.tensor_tensor(x[:, n, :], x[:, n, :], t, ALU.add)
                elif kind in ("AQ", "AK"):
                    u, g = d["u"], d["g"]
                    if u >= SP_PAIRS:
                        if u == SP_PAIRS:
                            dve.wait_ge(decay_in, 48)
                        rope(t, rot_c[:], rot_s[:], rot_t[:], rot_y[:], 64, val_done)
                        src = rot_y[:]
                    else:
                        src = t
                    dve.wait_ge(cast_done, d["cast"] + 1)
                    if kind == "AK":
                        ins = dve.tensor_tensor(ak_lo[:], src, f(ak_hi[:]), ALU.subtract)
                    elif u >= SP_PAIRS:
                        ins = dve.tensor_tensor(aq_lo[:, 0, :], src, f(aq_hi[:, 0, :]), ALU.subtract)
                    else:
                        for e in range(2):
                            ins = dve.scalar_tensor_tensor(aq_lo[:, e, :], src, col("half", e), f(aq_hi[:, e, :]),
                                                           ALU.mult, ALU.subtract)
                elif kind == "VT":
                    dve.wait_ge(cast_done, d["cast"] + 1)
                    ins = dve.tensor_tensor(av_lo[:].rearrange("p b r -> p (b r)"), t,
                                            f(av_hi[:].rearrange("p b r -> p (b r)")), ALU.subtract)
                ins.then_inc(post_done, 1)

            def h_low(l, k):
                dve.wait_ge(h_hi_done, H_BASE[l] + k + 1)
                dve.wait_ge(h_v_done, H_BASE[l] + k + 1)
                dve.tensor_tensor(h_lo[:, k, :], tmp[:, 2 + k % 2, :], f(h_hi[:, k, :]),
                                  ALU.subtract).then_inc(h_lo_done, 1)

            def h_columns(l):
                shift, scale = mod[:, 24 * l:24 * l + 8], mod[:, 24 * l + 8:24 * l + 16]
                if l == 0:
                    dve.wait_ge(post_done, post_of["redux", 0, 1, 0])
                    dve.tensor_scalar(h_scale[:, 0, :], scale, 1.0, None, ALU.add)
                    dve.tensor_copy(h_shift[:, 0, :], shift).then_inc(cols_done, 1)
                    return
                dve.wait_ge(post_done, post_of["redux", 0, 3 * l + 1, 0])
                gain = col("ln_g", 0, 8) if l == 1 else col("norm_g", 8 * (l - 2), 8)
                link(dve.tensor_scalar(h_scale[:, l, :], scale, 1.0, None, ALU.add))
                if l == 1:
                    link(dve.tensor_tensor(h_shift[:, 1, :], h_scale[:, 1, :], col("ln_b", 0, 8), ALU.mult))
                    link(dve.tensor_tensor(h_shift[:, 1, :], h_shift[:, 1, :], shift, ALU.add))
                else:
                    link(dve.tensor_copy(h_shift[:, l, :], shift))
                dve.tensor_tensor(h_scale[:, l, :], h_scale[:, l, :], gain, ALU.mult).then_inc(cols_done, 1)

            def statistics(d):
                si, w = d["stat"], 1.0 / d["width"]
                dve.wait_ge(stc_done, si + 1)
                if d["mean"]:
                    dve.tensor_scalar(st_sq[:], bank[:, 7, 0:NB], w, None, ALU.mult)
                    link(dve.tensor_scalar(st_mean[:], bank[:, 7, NB:2 * NB], w, None, ALU.mult))
                    link(dve.tensor_tensor(st_var[:], st_mean[:], st_mean[:], ALU.mult))
                    link(dve.tensor_tensor(st_var[:], st_sq[:], st_var[:], ALU.subtract))
                    dve.tensor_scalar(st_var[:], st_var[:], 0.0, None, ALU.max).then_inc(stv_done, 1)
                else:
                    dve.tensor_scalar(st_var[:], bank[:, 7, 0:NB], w, None, ALU.mult).then_inc(stv_done, 1)
                dve.wait_ge(sts_done, si + 1)
                ins = dve.reciprocal(st_r[:], st_sd[:])
                if d["mean"]:
                    link(ins)
                    ins = dve.tensor_tensor(st_mr[:], st_mean[:], st_r[:], ALU.mult)
                ins.then_inc(str_done, 1)

            def angles():
                dve.wait_ge(layer0_in, 48)
                dve.wait_ge(x_new, DC)
                a0, a1, a2 = (ang[:, i, :] for i in range(3))
                link(dve.tensor_copy(a0, posi[:]))
                link(dve.tensor_scalar(a0, a0, col("inv", 0), None, ALU.mult))
                for dst, turn, more in ((a1, 0.0, 0.0), (a2, 0.25, HALF_PI)):
                    link(dve.tensor_scalar(rope_t[:], a0, INV_2PI, turn, ALU.mult, ALU.add))
                    link(dve.tensor_scalar(rope_t[:], rope_t[:], ROUND, None, ALU.add))
                    link(dve.tensor_scalar(rope_t[:], rope_t[:], ROUND, None, ALU.subtract))
                    link(dve.scalar_tensor_tensor(dst, rope_t[:], -TWO_PI_PARTS[0], a0, ALU.mult, ALU.add))
                    link(dve.scalar_tensor_tensor(dst, rope_t[:], -TWO_PI_PARTS[1], dst, ALU.mult, ALU.add))
                    link(dve.scalar_tensor_tensor(dst, rope_t[:], -TWO_PI_PARTS[2], dst, ALU.mult, ALU.add))
                    if more:
                        link(dve.tensor_scalar(dst, dst, more, None, ALU.add))
                    dve.tensor_scalar(dst, dst, PI_DOWN, -PI_DOWN, ALU.min, ALU.max).then_inc(ang_done, 1)

            def head_max(t, i):
                g = NB * t + i
                dve.wait_ge(sc_full, g + 1)
                link(dve.memset(bank[0:64, i, i * P + 64:(i + 1) * P], MASKED))
                if t >= 1:
                    dve.wait_ge(exp_done, g - 3)
                dve.tensor_reduce(neg_max[:, i:i + 1], bank[:, i, 0:(i + 1) * P], AX.X, ALU.max,
                                  negate=True).then_inc(max_done, 1)

            def head(t):
                here, ahead = 0 <= t < MH, t + 1 < MH
                pair = ahead and t % 2 == 1 or t == -1
                j = (t + 1) // 2
                if here:
                    head_max(t, 0)
                    head_max(t, 1)
                if 0 <= t - 2 < MH:
                    dve.wait_ge(o_full, t - 1)
                    dve.wait_ge(chunk_taken, HEAD_CHUNK)
                    dve.tensor_tensor(sz[:, t - 2, :], bank[:, 6, :], sz[:, t - 2, :],
                                      ALU.mult).then_inc(o_taken, 1)
                if ahead:
                    dve.wait_ge(qn_hi_done, t + 2)
                    dve.tensor_tensor(qn_lo[:], bank[:, 7, :], f(qn_hi[:]), ALU.subtract).then_inc(qn_lo_done, 1)
                if pair:
                    dve.wait_ge(qr_taken, j + 1)
                    dve.tensor_tensor(rope_y[:], qr_f[:], cos1[:], ALU.mult).then_inc(qr_cos, 1)
                if here:
                    head_max(t, 2)
                    head_max(t, 3)
                if ahead:
                    dve.wait_ge(ql_hi_done, t + 2)
                    dve.tensor_tensor(ql_lo[:], bank[:, 7, :], f(ql_hi[:]), ALU.subtract).then_inc(ql_lo_done, 1)
                if here:
                    for i in range(NB):
                        g = NB * t + i
                        dve.wait_ge(exp_done, g + 1)
                        if t >= 1:
                            dve.wait_ge(p_done, g - 3)
                        dve.reciprocal(rsum[:, i:i + 1], esum[:, i:i + 1]).then_inc(rsum_done, 1)
                    for i in range(NB):
                        dve.wait_ge(rsum_done, NB * t + i + 1)
                        dve.tensor_scalar(p_of(t, i), p_of(t, i), rsum[:, i:i + 1], None,
                                          ALU.mult).then_inc(p_done, 1)
                T = splits_in(t)
                if T is not None and t < MH - 1:
                    split_tile(T)
                if pair:
                    dve.wait_ge(qr_cos, j + 1)
                    dve.wait_ge(qr_turned, 4 * (j + 1))
                    dve.tensor_tensor(rope_y[:], rope_y[:], rope_t[:], ALU.add).then_inc(qr_val, 1)
                if pair:
                    dve.wait_ge(qr_hi_done, j + 1)
                    dve.tensor_tensor(qr_lo[:], rope_y[:], f(qr_hi[:]), ALU.subtract).then_inc(qr_lo_done, 1)
                if 0 <= t - 2 < MH:
                    dve.wait_ge(mc_hi_done, t - 1)
                    dve.tensor_tensor(mixc_lo[:, t - 2, :], sz[:, t - 2, :], f(mixc_hi[:, t - 2, :]),
                                      ALU.subtract).then_inc(mc_lo_done, 1)
                if T is not None and t < MH - 1:
                    ada_piece(T - 1 + 2 * SEC)
                if 0 <= t - 1 < MH:
                    dve.wait_ge(ol_hi_done, t)
                    dve.tensor_tensor(ol_lo[:], bank[:, 6, :], f(ol_hi[:]), ALU.subtract).then_inc(ol_lo_done, 1)
                if t == MH - 1:
                    split_tile(T)
                    ada_piece(T - 1 + 2 * SEC)

            dve.wait_ge(cond_done, 1)
            for q in range(2 * SEC):
                ada_piece(q)
            for d in steps:
                op = d["op"]
                if op == "tile":
                    T = d["T"]
                    if T + 1 < NT:
                        split_tile(T + 1)
                    if not d["late_ada"]:
                        ada_piece(T + 2 * SEC)
                elif op == "chunk":
                    if d["kind"] == "XB" and d["n"] == 0:
                        dve.wait_ge(sv_full, 2 * GH)
                        dve.wait_ge(sv_taken, 2 * GH)
                        for i in range(4):
                            dve.memset(padded[:, i, 0:PAD], 0.0).then_inc(pad_done, 1)
                        dve.wait_ge(pad_done, 4)
                    chunk(d)
                    if d["kind"] == "redux" and d["u"] == 0:
                        split_tile(0)
                elif op == "spatial_rows":
                    dve.wait_ge(rows_full, 1)
                    for i in range(DC):
                        hh, j = i // 2, i % 2
                        dve.scalar_tensor_tensor(rb[:, i, :], bank[:, 4, hh * P:(hh + 1) * P],
                                                 col("gmlp_b", j), bs[:, hh, :], ALU.mult,
                                                 ALU.add).then_inc(rb_done, 1)
                elif op == "spatial":
                    h = d["h"]
                    if h == 0:
                        dve.wait_ge(rb_done, DC)
                    for j in range(2):
                        n = 2 * h + j
                        dve.wait_ge(sv_full, n + 1)
                        dve.scalar_tensor_tensor(park[:, n, :].rearrange("p (b t) -> p b t", b=NB),
                                                 bank[:, 4 + j, :].rearrange("p (b t) -> p b t", b=NB),
                                                 col("gmlp_g", j),
                                                 rb[:, n:n + 1, :].broadcast_to([P, NB, P]),
                                                 ALU.mult, ALU.add).then_inc(sv_taken, 1)
                elif op == "mixb_split":
                    for n in range(DC):
                        dve.wait_ge(mixb_hi_done, n + 1)
                        dve.tensor_tensor(mixb_lo[:, n, :], park[:, n, :], f(mixb_hi[:, n, :]),
                                          ALU.subtract).then_inc(mixb_lo_done, 1)
                elif op == "h" and d["l"] == 0:
                    h_columns(0)
                    for k in range(DC):
                        h_low(0, k)
                    dve.wait_ge(layer0_in, 32)
                    dve.memset(ws[64:P, :, 0:64], 0.0).then_inc(ws_done, 1)
                elif op == "h":
                    l = d["l"]
                    h_columns(l)
                    dve.wait_ge(stb_done, d["s"] + 1)
                    for k in range(DC + 1):
                        if k < DC:
                            dve.tensor_tensor(tmp[:, k % 2, :], x[:, k, :], bank[:, 6, :],
                                              ALU.mult).then_inc(h_t, 1)
                        if k >= 1:
                            h_low(l, k - 1)
                elif op == "ln":
                    l = d["l"]
                    if l == 1:
                        h_columns(1)
                    dve.wait_ge(stb_done, d["s"] + 1)
                    for k in range(DC + 1):
                        if k < DC:
                            link(dve.tensor_tensor(x[:, k, :], x[:, k, :], bank[:, 6, :], ALU.mult))
                            dve.tensor_tensor(x[:, k, :], x[:, k, :], bank[:, 5, :], ALU.subtract).then_inc(h_t, 1)
                        if k >= 1 and l == 1:
                            h_low(1, k - 1)
                elif op == "stat_cols":
                    statistics(d)
                elif op == "trig":
                    angles()
                elif op == "qkv_squares":
                    dve.wait_ge(chunk_taken, QC_CHUNK + 4)
                    dve.tensor_tensor(kv_sq[:, 0, :], qkv[:, 0, :], qkv[:, 0, :], ALU.mult)
                    link(dve.tensor_tensor(kv_sq[:, 1, :], qkv[:, 1, :], qkv[:, 1, :], ALU.mult))
                    dve.tensor_tensor(kv_sq[:, 0, :], kv_sq[:, 0, :], kv_sq[:, 1, :], ALU.add).then_inc(sq_done, 1)
                    dve.wait_ge(sq_done, 1)
                    dve.tensor_tensor(kv_sq[:, 1, :], qkv[:, 2, :], qkv[:, 2, :], ALU.mult).then_inc(sq_done, 1)
                    link(dve.tensor_scalar(q_gain[:], col("q_g", 0, 2), MLA_SCALE, None, ALU.mult))
                elif op == "q_norm":
                    dve.wait_ge(stb_done, d["s"] + 1)
                    for c in range(2):
                        dve.scalar_tensor_tensor(qkv[:, c, :], qkv[:, c, :], q_gain[:, c:c + 1], bank[:, 6, :],
                                                 ALU.mult, ALU.mult).then_inc(qk_val, 1)
                    for c in range(2):
                        dve.wait_ge(qk_hi, c + 1)
                        dve.tensor_tensor(qc_lo[:, c, :], qkv[:, c, :], f(qc_hi[:, c, :]),
                                          ALU.subtract).then_inc(qk_lo, 1)
                elif op == "kv_norm":
                    dve.wait_ge(stb_done, d["s"] + 1)
                    dve.wait_ge(trig_done, 2)
                    dve.scalar_tensor_tensor(kv_f[:], qkv[:, 2, :], col("kv_g"), bank[:, 6, :], ALU.mult,
                                             ALU.mult).then_inc(qk_val, 1)
                    dve.wait_ge(qk_hi, 3)
                    dve.tensor_tensor(kv_lo[:], kv_f[:], f(kv_hi[:]), ALU.subtract).then_inc(qk_lo, 1)
                elif op == "k_rope":
                    rope(qkv[:, 3, :], cos1[:], sin1[:], rope_t[:], rope_y[:], 32, qk_val)
                    dve.wait_ge(qk_hi, 4)
                    dve.tensor_tensor(kr_lo[:], rope_y[:], f(kr_hi[:]), ALU.subtract).then_inc(qk_lo, 1)
                elif op == "head":
                    head(d["h"])
                elif op in ("att_scores", "att_scores2") and d["u"] < SP_PAIRS:
                    s = SP_PAIRS * (d["l"] - 2) + d["u"]
                    dve.wait_ge(z_full, s + 1)
                    for i in range(4) if op == "att_scores" else range(4, 7):
                        if i + 1 in (1, 3):
                            link(dve.tensor_scalar(sp_f[:, i + 1, :], bank[:, 3 + i, :], -1.0, None, ALU.mult))
                            dve.tensor_tensor(sp_f[:, i + 1, :], bank[:, 3 + i, :], sp_f[:, i + 1, :],
                                              ALU.max).then_inc(z_abs, 1)
                        if 1 <= i < 6:
                            dve.wait_ge(z_log, 5 * s + i)
                            dve.scalar_tensor_tensor(sp_f[:, i - 1, :], bank[:, 1 + i, :], 0.0,
                                                     sp_f[:, i - 1, :], ALU.max, ALU.add).then_inc(sp_val, 1)
                        if 2 <= i < 7:
                            dve.wait_ge(sp_hi_done, 5 * s + i - 1)
                            dve.tensor_tensor(sp_lo[:, i - 2, :], sp_f[:, i - 2, :],
                                              f(sp_hi[:, i - 2, :]), ALU.subtract).then_inc(sp_lo_done, 1)
                elif op == "att_scores":
                    r = RH * (d["l"] - 2) + d["u"] - SP_PAIRS
                    h = d["u"] - SP_PAIRS
                    dve.wait_ge(rs_full, r + 1)
                    wait_unit_out(dve, d["g"] - 1)
                    for i in range(3):
                        for J in range(NB):
                            bk, c0 = RET_PLACE[J]
                            if bk == i:
                                w = slice(c0, c0 + (NB - J) * P)
                                ins = dve.tensor_tensor(sp_f[:, i, w], bank[:, 2 + i, w],
                                                        decay[:, h, 0:(NB - J) * P], ALU.mult)
                        ins.then_inc(rs_val, 1)
                    for i in range(3):
                        n = (S, S, 2 * P)[i]
                        dve.wait_ge(rs_hi_done, 3 * r + i + 1)
                        dve.tensor_tensor(sp_lo[:, i, 0:n], sp_f[:, i, 0:n], f(sp_hi[:, i, 0:n]),
                                          ALU.subtract).then_inc(rs_lo_done, 1)
                elif op == "att_mid" and d["u"] < SP_PAIRS:
                    s = SP_PAIRS * (d["l"] - 2) + d["u"]
                    for i in range(5):
                        dve.wait_ge(a_hi_done, 5 * s + i + 1)
                        dve.tensor_tensor(sp_lo[:, i, :], sp_f[:, i, :], f(sp_hi[:, i, :]),
                                          ALU.subtract).then_inc(a_lo_done, 1)
                elif op == "att_out" and d["u"] < SP_PAIRS:
                    s = SP_PAIRS * (d["l"] - 2) + d["u"]
                    k = RH + d["u"]
                    dve.wait_ge(ao_full, s + 1)
                    dve.wait_ge(chunk_taken, AG_CHUNK[d["g"]] + 1)
                    dve.tensor_tensor(mixf[0:64, k, :], bank[0:64, 2, :], ag[0:64, d["g"] % 2, :], ALU.mult)
                    dve.tensor_tensor(mixf[64:P, k, :], bank[64:P, 3, :], ag[64:P, d["g"] % 2, :],
                                      ALU.mult).then_inc(mixf_done, 1)
                elif op == "ret_norm":
                    k = d["u"] - SP_PAIRS
                    g = 8 * (d["l"] - 2) + d["u"]
                    dve.wait_ge(stb_done, d["s"] + 1)
                    dve.wait_ge(chunk_taken, AG_CHUNK[g] + 1)
                    link(dve.tensor_tensor(mixf[:, k, :], bank[:, 5 + k % 2, :], ag[:, g % 2, :], ALU.mult))
                    dve.tensor_tensor(mixf[:, k, :], mixf[:, k, :], bank[:, 7, :], ALU.mult).then_inc(mixf_done, 1)
                elif op == "mix_split":
                    l = d["l"]
                    for i in d["part"]:
                        k = MIX_ORDER[i]
                        dve.wait_ge(m_hi_done, DC * (l - 2) + i + 1)
                        dve.tensor_tensor(h_lo[:, k, :], mixf[:, k, :], f(h_hi[:, k, :]),
                                          ALU.subtract).then_inc(m_lo_done, 1)
                    if d["part"] == (7,):
                        ada_piece(T + 2 * SEC)
                elif op == "final":
                    dve.wait_ge(stb_done, d["s"] + 1)
                    for n in range(DC):
                        dve.scalar_tensor_tensor(outf[:, n, :], x[:, n, :], col("final_g", n), bank[:, 6, :],
                                                 ALU.mult, ALU.mult).then_inc(fin_done, 1)

        @block.gpsimd
        def _(pool):
            link = chain(pool, "pool")

            def cast(dst, src):
                return pool.tensor_scalar(dst, src, 1.0, None, ALU.mult)

            def sums(n, mean):
                if mean:
                    if n == 0:
                        link(pool.tensor_scalar(sum1[:], x[:, 0, :], 1.0, None, ALU.mult))
                    else:
                        link(pool.tensor_tensor(sum1[:], sum1[:], x[:, n, :], ALU.add))
                if n == 0:
                    link(pool.tensor_tensor(sum2[:], x[:, 0, :], x[:, 0, :], ALU.mult))
                else:
                    link(pool.tensor_tensor(sqr[:], x[:, n, :], x[:, n, :], ALU.mult))
                    ins = pool.tensor_tensor(sum2[:], sum2[:], sqr[:], ALU.add)
                    if n == DC - 2:
                        ins.then_inc(sums_done, 1)
                    else:
                        link(ins)

            for d in steps:
                op = d["op"]
                if op == "chunk":
                    kind, C, l = d["kind"], d["C"], d.get("l", 0)
                    if "cast" in d and d.get("u", SP_PAIRS) >= SP_PAIRS:
                        if "val" in d:
                            pool.wait_ge(val_done, d["val"] + 1)
                        else:
                            pool.wait_ge(chunk_taken, C + 1)
                        t = tmp[:, d["m"] % 4, :]
                        if kind == "Z":
                            ins = cast(mixa_hi[:, d["n"], :], park[:, d["n"], :])
                        elif kind in ("AQ", "AK"):
                            wait_unit_scores(pool, d["g"] - 1)
                            ins = cast(ak_hi[:] if kind == "AK" else aq_hi[:, 0, :], rot_y[:])
                        elif kind == "VT":
                            wait_unit_out(pool, d["g"] - 1)
                            ins = cast(av_hi[:].rearrange("p b r -> p (b r)"), t)
                        ins.then_inc(cast_done, 1)
                    if kind[:3] == "OUT" and d["n"] < DC - 1:
                        pool.wait_ge(post_done, d["post"])
                        sums(d["n"], l < 2)
                elif op == "mixb_split":
                    pool.wait_ge(chunk_full, XB_LAST + 1)
                    for n in range(DC):
                        pool.wait_ge(post_done, post_of["Y", 0, n, 0])
                        cast(mixb_hi[:, n, :], park[:, n, :]).then_inc(mixb_hi_done, 1)
                elif op == "h" and d["l"] == 0:
                    pool.wait_ge(cols_done, 1)
                    for k in range(DC):
                        pool.wait_ge(x_landed[k // 2], 16)
                        if k >= 2:
                            pool.wait_ge(h_lo_done, k - 1)
                        pool.tensor_scalar(tmp[:, 2 + k % 2, :], x[:, k, :], h_scale[:, 0, k:k + 1],
                                           h_shift[:, 0, k:k + 1], ALU.mult, ALU.add).then_inc(h_v_done, 1)
                elif op == "h" or op == "ln":
                    l = d["l"]
                    if op == "ln" and l == 2:
                        continue
                    pool.wait_ge(cols_done, l + 1)
                    for k in range(DC):
                        pool.wait_ge(h_t, H_T_BASE[op, l] + k + 1)
                        if k >= 2:
                            pool.wait_ge(h_lo_done, H_BASE[l] + k - 1)
                        t = x[:, k, :] if op == "ln" else tmp[:, k % 2, :]
                        pool.tensor_scalar(tmp[:, 2 + k % 2, :], t, h_scale[:, l, k:k + 1],
                                           h_shift[:, l, k:k + 1], ALU.mult, ALU.add).then_inc(h_v_done, 1)
                elif op == "q_norm":
                    for c in range(2):
                        pool.wait_ge(qk_val, c + 1)
                        cast(qc_hi[:, c, :], qkv[:, c, :]).then_inc(qk_hi, 1)
                elif op == "kv_norm":
                    pool.wait_ge(qk_val, 3)
                    cast(kv_hi[:], kv_f[:]).then_inc(qk_hi, 1)
                elif op == "k_rope":
                    pool.wait_ge(qk_val, 4)
                    cast(kr_hi[:], rope_y[:]).then_inc(qk_hi, 1)
                elif op == "head":
                    t = d["h"]
                    if t % 2 == 1 and t + 1 < MH or t == -1:
                        j = (t + 1) // 2
                        pool.wait_ge(qr_taken, j + 1)
                        for i in range(4):
                            to, of = slice(32 * i, 32 * i + 32), slice(32 * (i ^ 1), 32 * (i ^ 1) + 32)
                            pool.tensor_tensor(rope_t[to, :], qr_f[of, :], sin1[of, :], ALU.mult).then_inc(qr_turned, 1)
                            pool.wait_ge(qr_turned, 4 * j + i + 1)
                    if 0 <= t - 2 < MH:
                        pool.wait_ge(o_taken, t - 1)
                        cast(mixc_hi[:, t - 2, :], sz[:, t - 2, :]).then_inc(mc_hi_done, 1)


def kernel(x, c, positions, ada_w, ada_b, ln_g, ln_b, e_w_in, gmlp_norm_g, gmlp_norm_b, gmlp_ws, gmlp_bs,
           pool_w, pool_b, pool_scale, e_w_out, o_w_in, mla_q_norm_g, mla_kv_norm_g, mla_w_uq, mla_w_uk,
           mla_w_uv, o_w_out, c_2, norm_g_2, w_ada_2, b_ada_2, w_in_2, w_out_2, final_g_2):
    import concourse.bacc as bacc
    from concourse.bass_utils import run_bass_kernel_spmd as run

    A = np.asarray
    f32 = np.float32

    def rows(w):
        return A(w).reshape(-1, P, w.shape[-1]).transpose(1, 0, 2)

    tiles = []

    def add(t):
        t = t.reshape(P, -1)
        if t.shape[1] < TILE:
            t = np.concatenate([t, np.zeros((P, TILE - t.shape[1]), f32)], axis=1)
        tiles.append(t)

    w = rows(A(e_w_in)[0])
    for base in (D, 0, 2 * D, 4 * D, 3 * D):
        for i in range(4):
            add(w[:, :, base + i * HD:base + (i + 1) * HD])
    w = rows(A(e_w_out)[0])
    for n in range(DC):
        add(w[:, :, n * P:(n + 1) * P])
    w = rows(A(o_w_in)[0])
    add(w[:, :, 0:256])
    kr = w[:, :, 384:448]
    add(np.concatenate([w[:, :, 256:384], kr, kr], axis=2))
    for i in range(8):
        add(w[:, :, 448 + i * 256:448 + (i + 1) * 256])
    uq = rows(A(mla_w_uq)[0].reshape(256, MH * 192)).reshape(P, 2, MH, 192)
    uk = A(mla_w_uk)[0].transpose(2, 1, 0)
    uv = A(mla_w_uv)[0]
    for j in range(MH // 2):
        a, b = 2 * j, 2 * j + 1
        q = np.concatenate([uq[:, :, a, 0:P], uq[:, :, b, 0:P], uq[:, :, a, P:], uq[:, :, b, P:]], axis=2)
        add(np.concatenate([q.reshape(P, 768), uk[:, a], uk[:, b], uv[:, a], uv[:, b]], axis=1))
    w = rows(A(o_w_out)[0])
    for n in range(DC):
        add(w[:, :, n * P:(n + 1) * P])
    for l in range(2):
        w = rows(A(w_in_2)[l])
        for u in range(8):
            first, i = (4 * 512, u) if u < SP_PAIRS else (0, u - SP_PAIRS)
            q, k, v, g = (w[:, :, first + 512 * s + i * P:first + 512 * s + (i + 1) * P] for s in range(4))
            add(np.concatenate([q, k], axis=2))
            add(np.concatenate([v, g], axis=2))
        w = rows(A(w_out_2)[l])
        for n in range(4):
            add(w[:, :, n * 256:(n + 1) * 256])
    wt = np.stack(tiles)

    ada = np.concatenate([A(ada_w), A(w_ada_2)]).reshape(DEPTH, DC, P, 3, D).transpose(0, 3, 1, 2, 4)
    ada = np.ascontiguousarray(ada.reshape(DEPTH * 3 * DC, P, D))

    def col(v):
        return A(v).reshape(-1, P).T

    inv1 = (1.0 / (f32(10000.0) ** (np.arange(0, MLA_ROPE, 2, dtype=f32) / f32(MLA_ROPE)))).astype(f32)
    sign = np.tile(np.repeat(np.array([1.0, -1.0], f32), 32), 2)
    colst = np.concatenate([
        col(ada_b), col(b_ada_2), col(c), col(c_2), col(ln_g), col(ln_b), col(gmlp_norm_g), col(gmlp_norm_b),
        col(pool_b), col(pool_scale), col(mla_q_norm_g), col(mla_kv_norm_g), col(norm_g_2), col(final_g_2),
        np.tile(inv1, 4)[:, None], sign[:, None], np.full((P, 1), 1e-5, f32), np.full((P, 1), 1e-6, f32),
        np.repeat(np.eye(2, dtype=f32), 64, axis=0),
    ], axis=1)

    i = np.arange(P)
    edge = np.ones((P, 4, PAD), f32)
    for g, win in enumerate(WINDOWS):
        edge[:, g, 0:win] = (win / np.arange(1, win + 1)).astype(f32)
    matst = np.concatenate([
        np.eye(P), np.ones((P, P)), np.eye(P) - 1.0 / P, i[:, None] < i[None, :],
        edge.reshape(P, 4 * PAD)], axis=1).astype(f32)
    rmatst = np.concatenate([-1.0 * (i[:, None] >= i[None, :]), -np.ones((P, P)),
                             MASKED * (i[:, None] >= i[None, :]), np.eye(P)], axis=1).astype(f32)

    m, n = np.arange(P)[:, None], np.arange(S)[None, :]
    same = (m // 64) == (n // 64)
    power = np.where(same, np.abs(n - m), n - m)
    seen = (m // 64) <= (n // 64)
    logs = np.log1p(-(2.0 ** (-5.0 - np.arange(RH))))
    decayt = np.stack([np.where(seen, np.exp(np.where(seen, power, 0) * g), 0.0) * P ** -0.5 for g in logs],
                      axis=1).astype(f32)
    inv2 = (f32(10000.0) ** (-np.arange(64, dtype=f32) / f32(64))).astype(f32)
    angle = (inv2[:, None] * np.arange(S, dtype=f32)[None, :]).astype(np.float64)
    sn = np.sin(angle)
    rot = np.stack([np.concatenate([np.cos(angle)] * 2), np.concatenate([sn, -sn])]).astype(f32)

    arrays = {
        "wt": wt, "adat": ada, "colst": colst, "matst": matst, "rmatst": rmatst,
        "xt": A(x)[0].T.reshape(DC, P, S).transpose(1, 0, 2),
        "pos": A(positions)[0],
        "wst": A(gmlp_ws)[0].transpose(2, 0, 1),
        "bst": np.broadcast_to(A(gmlp_bs)[0][None], (P, GH, P)),
        "poolt": A(pool_w)[0].reshape(4, 2, P, HD).transpose(2, 0, 1, 3),
        "decayt": decayt, "rot": rot,
    }
    arrays = {k: np.ascontiguousarray(v) for k, v in arrays.items()}
    nc = bacc.Bacc("TRN2", target_bir_lowering=False, num_devices=1)
    args = [nc.dram_tensor(k, v.shape, mybir.dt.from_np(v.dtype), kind="ExternalInput").ap()
            for k, v in arrays.items()]
    out = nc.dram_tensor("out", (P, DC, S), F32, kind="ExternalOutput").ap()
    build(nc, *args, out)
    r = run(nc, [arrays], core_ids=[0])
    return r.results[0]["out"].transpose(1, 0, 2).reshape(D, S).T[None]
```
